# Optimizing a Trainium2 kernel written in Bass

```python
import numpy as np
import jax
import jax.numpy as jnp
from jax import lax

D_MODEL = 2048
BATCH = 1
SEQ = 256
DEPTH = 2

CHUNK = 64
RET_WIDTH = D_MODEL // 2
RET_HEADS = 4
RET_HEAD_DIM = RET_WIDTH // RET_HEADS
ROPE_BASE = 10000.0
RET_GN_EPS = 1e-5
RWKV_WIDTH = D_MODEL - RET_WIDTH
RWKV_HEAD_DIM = 64
RWKV_HEADS = RWKV_WIDTH // RWKV_HEAD_DIM
RWKV_LN_EPS = 64e-5

def _rwkv_lora_rank(mult, power):
    return max(32, int(round(mult * RWKV_WIDTH ** power / 32)) * 32)

DECAY_RANK = _rwkv_lora_rank(1.8, 0.5)
ICLR_RANK = _rwkv_lora_rank(1.8, 0.5)
VRES_RANK = _rwkv_lora_rank(1.3, 0.5)
GATE_RANK = _rwkv_lora_rank(0.6, 0.8)
RET_IN = 4 * RET_WIDTH
RWKV_IN = 3 * RWKV_WIDTH + DECAY_RANK + ICLR_RANK + GATE_RANK
EVEN_IN = RET_IN + RWKV_IN
LRU_WIDTH = D_MODEL
LRU_BLOCK = 256
LRU_BLOCKS = LRU_WIDTH // LRU_BLOCK
CONV_WIDTH = 4
LRU_C = 8.0
D_FF = 4 * D_MODEL
NORM_EPS = 1e-6
N_EVEN = (DEPTH + 1) // 2
N_ODD = DEPTH // 2

kernel_name = 'hybrid_retention_rwkv7_rglru_trunk'

def _rmsnorm(x, g):
    x32 = x.astype(jnp.float32)
    y = x32 * lax.rsqrt(jnp.mean(x32 * x32, axis=-1, keepdims=True) + NORM_EPS)
    return (y * g.astype(jnp.float32)).astype(x.dtype)

def _head_norm(y, eps):
    mu = jnp.mean(y, axis=-1, keepdims=True)
    var = jnp.mean(jnp.square(y - mu), axis=-1, keepdims=True)
    return (y - mu) * lax.rsqrt(var + eps)

def _split(z, sizes):
    return jnp.split(z, np.cumsum(sizes)[:-1].tolist(), axis=-1)

def _time_shift(z):
    return jnp.pad(z, ((0, 0), (1, 0), (0, 0)))[:, :-1]

def _rotary(t):
    T, d = t.shape[1], t.shape[-1]
    inv = 1.0 / (ROPE_BASE ** (jnp.arange(0, d, 2, dtype=jnp.float32) / d))
    ang = jnp.arange(T, dtype=jnp.float32)[:, None] * inv[None, :]
    cos = jnp.cos(ang)[None, :, None, :]
    sin = jnp.sin(ang)[None, :, None, :]
    t1, t2 = jnp.split(t, 2, axis=-1)
    return jnp.concatenate([t1 * cos - t2 * sin, t2 * cos + t1 * sin], axis=-1)

def _to_chunks(t):
    B, T, H, d = t.shape
    return t.reshape(B, T // CHUNK, CHUNK, H, d).transpose(1, 0, 3, 2, 4)

def _from_chunks(t):
    Nc, B, H, C, d = t.shape
    return t.transpose(1, 0, 3, 2, 4).reshape(B, Nc * C, H, d)

def _retention(q, k, v):
    B, _, H, dk = q.shape
    dv = v.shape[-1]
    log_g = jnp.log1p(-jnp.exp2(-5.0 - jnp.arange(H, dtype=jnp.float32)))
    pos = jnp.arange(CHUNK, dtype=jnp.float32)
    intra_decay = jnp.exp(log_g[:, None, None] * jnp.abs(pos[:, None] - pos[None, :]))
    q_decay = jnp.exp(log_g[:, None] * (pos + 1.0))[:, :, None]
    k_decay = jnp.exp(log_g[:, None] * (CHUNK - 1.0 - pos))[:, :, None]
    chunk_decay = jnp.exp(log_g * CHUNK)[:, None, None]

    def step(state, qkv):
        qc, kc, vc = qkv
        scores = jnp.einsum('bhnd,bhmd->bhnm', qc, kc) * intra_decay
        out = (jnp.einsum('bhnm,bhme->bhne', scores, vc)
               + jnp.einsum('bhnd,bhde->bhne', qc * q_decay, state))
        state = state * chunk_decay + jnp.einsum('bhmd,bhme->bhde', kc * k_decay, vc)
        return state, out

    s0 = jnp.zeros((B, H, dk, dv), jnp.float32)
    _, out = lax.scan(step, s0, (_to_chunks(q), _to_chunks(k), _to_chunks(v)))
    return _from_chunks(out)

def _rwkv7_scan(r, w, k, v, kk, a):
    B, T, H, N = r.shape

    def step(S, inp):
        r_t, w_t, k_t, v_t, kk_t, a_t = inp
        sa = jnp.einsum('bhvk,bhk->bhv', S, kk_t)
        S = (S * w_t[:, :, None, :]
             - jnp.einsum('bhv,bhk->bhvk', sa, kk_t * a_t)
             + jnp.einsum('bhv,bhk->bhvk', v_t, k_t))
        return S, jnp.einsum('bhvk,bhk->bhv', S, r_t)

    tm = lambda t: jnp.moveaxis(t, 1, 0)
    s0 = jnp.zeros((B, H, N, N), jnp.float32)
    _, y = lax.scan(step, s0, (tm(r), tm(w), tm(k), tm(v), tm(kk), tm(a)))
    return jnp.moveaxis(y, 0, 1)

def _even_mixer(h, w_in, w_out, mu, w0, w2, a0, a2, g2, k_k, k_a, r_k, lnx_w, lnx_b,
                v_first, v_res):
    B, T, _ = h.shape
    heads = lambda t, n: t.reshape(B, T, n, -1)
    z = (h @ w_in).astype(jnp.float32)
    z_ret, z_rw = z[..., :RET_IN], z[..., RET_IN:]

    q, k, v, g = _split(z_ret, [RET_WIDTH] * 4)
    q = _rotary(heads(q, RET_HEADS))
    k = _rotary(heads(k, RET_HEADS)) * (RET_HEAD_DIM ** -0.5)
    y_ret = _head_norm(_retention(q, k, heads(v, RET_HEADS)), RET_GN_EPS)
    out_ret = jax.nn.silu(g) * y_ret.reshape(B, T, RET_WIDTH)

    zs = z_rw + mu * (_time_shift(z_rw) - z_rw)
    r, kr, vr, wl, al, gl = _split(zs, [RWKV_WIDTH] * 3 + [DECAY_RANK, ICLR_RANK, GATE_RANK])
    decay = jnp.exp(-jnp.exp(-jax.nn.softplus(-(w0 + jnp.tanh(wl) @ w2)) - 0.5))
    iclr = jax.nn.sigmoid(a0 + al @ a2)
    gate = jax.nn.sigmoid(gl) @ g2
    if v_res is None:
        v_first = vr
    else:
        v0, v1, v2 = v_res
        vr = vr + (v_first - vr) * jax.nn.sigmoid(v0 + (vr @ v1) @ v2)
    kk = heads(kr * k_k, RWKV_HEADS)
    kk = kk / jnp.maximum(jnp.linalg.norm(kk, axis=-1, keepdims=True), 1e-12)
    kr = kr * (1.0 + (iclr - 1.0) * k_a)
    rh, kh, vh, wh, ah = [heads(t, RWKV_HEADS) for t in (r, kr, vr, decay, iclr)]
    y_rw = _rwkv7_scan(rh, wh, kh, vh, kk, ah)
    y_rw = _head_norm(y_rw, RWKV_LN_EPS).reshape(B, T, RWKV_WIDTH) * lnx_w + lnx_b
    bonus = (jnp.sum(rh * kh * r_k, axis=-1, keepdims=True) * vh).reshape(B, T, RWKV_WIDTH)
    out_rw = (y_rw + bonus) * gate

    mixed = jnp.concatenate([out_ret, out_rw], axis=-1).astype(h.dtype) @ w_out
    return mixed, v_first

def _linear_combine(left, right):
    a_l, b_l = left
    a_r, b_r = right
    return a_l * a_r, a_r * b_l + b_r

def _odd_mixer(h, w_in, conv_w, conv_b, gx_w, gx_b, ga_w, ga_b, lam, w_out):
    B, T, _ = h.shape
    z = (h @ w_in).astype(jnp.float32)
    y_br, x_br = jnp.split(z, 2, axis=-1)
    y_br = jax.nn.gelu(y_br, approximate=True)
    x_br = lax.conv_general_dilated(
        x_br, conv_w.astype(jnp.float32)[:, None, :], window_strides=(1,),
        padding=[(CONV_WIDTH - 1, 0)], dimension_numbers=('NWC', 'WIO', 'NWC'),
        feature_group_count=LRU_WIDTH) + conv_b
    xb = x_br.reshape(B, T, LRU_BLOCKS, LRU_BLOCK)
    gate_x = jax.nn.sigmoid(jnp.einsum('btni,nij->btnj', xb, gx_w).reshape(B, T, LRU_WIDTH) + gx_b)
    gate_a = jax.nn.sigmoid(jnp.einsum('btni,nij->btnj', xb, ga_w).reshape(B, T, LRU_WIDTH) + ga_b)
    log_a = -LRU_C * gate_a * jax.nn.softplus(-lam)
    a = jnp.exp(log_a)
    b = x_br * gate_x * jnp.sqrt(-jnp.expm1(2.0 * log_a))
    _, hs = lax.associative_scan(_linear_combine, (a, b), axis=1)
    return (y_br * hs).astype(h.dtype) @ w_out

def _sq_relu_mlp(h, w1, w2):
    return jnp.square(jax.nn.relu(h @ w1)) @ w2

def setup_inputs(seed: int = 0) -> dict:
    key = jax.random.key(seed)
    ks = iter(jax.random.split(key, 48))
    f32 = jnp.float32

    def normal(shape, scale):
        return jax.random.normal(next(ks), shape, f32) * scale

    def uniform(shape, lo, hi):
        return jax.random.uniform(next(ks), shape, f32, lo, hi)

    def gain(shape):
        return 1.0 + normal(shape, 0.02)

    NE1 = N_EVEN - 1
    ramp = jnp.linspace(0.0, 1.0, RWKV_WIDTH, dtype=f32)
    s = uniform((N_ODD, LRU_WIDTH), 0.9, 0.999) ** (1.0 / LRU_C)
    return {
        'x': normal((BATCH, SEQ, D_MODEL), 1.0),
        'ev_norm': gain((N_EVEN, D_MODEL)),
        'ev_w_in': normal((N_EVEN, D_MODEL, EVEN_IN), D_MODEL ** -0.5),
        'ev_w_out': normal((N_EVEN, RET_WIDTH + RWKV_WIDTH, D_MODEL), (RET_WIDTH + RWKV_WIDTH) ** -0.5),
        'rw_mu': uniform((N_EVEN, RWKV_IN), 0.2, 0.8),
        'rw_w0': -6.5 + 5.0 * ramp ** 0.85 + normal((N_EVEN, RWKV_WIDTH), 0.1),
        'rw_w2': normal((N_EVEN, DECAY_RANK, RWKV_WIDTH), 0.5 * DECAY_RANK ** -0.5),
        'rw_a0': normal((N_EVEN, RWKV_WIDTH), 0.1),
        'rw_a2': normal((N_EVEN, ICLR_RANK, RWKV_WIDTH), 0.5 * ICLR_RANK ** -0.5),
        'rw_g2': normal((N_EVEN, GATE_RANK, RWKV_WIDTH), GATE_RANK ** -0.5),
        'rw_k_k': 0.85 + normal((N_EVEN, RWKV_WIDTH), 0.02),
        'rw_k_a': 1.0 + normal((N_EVEN, RWKV_WIDTH), 0.02),
        'rw_r_k': -0.04 + normal((N_EVEN, RWKV_HEADS, RWKV_HEAD_DIM), 0.1),
        'rw_lnx_w': gain((N_EVEN, RWKV_WIDTH)),
        'rw_lnx_b': normal((N_EVEN, RWKV_WIDTH), 0.02),
        'rw_v0': 1.0 + normal((NE1, RWKV_WIDTH), 0.1),
        'rw_v1': normal((NE1, RWKV_WIDTH, VRES_RANK), RWKV_WIDTH ** -0.5),
        'rw_v2': normal((NE1, VRES_RANK, RWKV_WIDTH), 0.5 * VRES_RANK ** -0.5),
        'od_norm': gain((N_ODD, D_MODEL)),
        'od_w_in': normal((N_ODD, D_MODEL, 2 * LRU_WIDTH), D_MODEL ** -0.5),
        'od_conv_w': normal((N_ODD, CONV_WIDTH, LRU_WIDTH), CONV_WIDTH ** -0.5),
        'od_conv_b': normal((N_ODD, LRU_WIDTH), 0.02),
        'od_gx_w': normal((N_ODD, LRU_BLOCKS, LRU_BLOCK, LRU_BLOCK), LRU_BLOCK ** -0.5),
        'od_gx_b': normal((N_ODD, LRU_WIDTH), 0.02),
        'od_ga_w': normal((N_ODD, LRU_BLOCKS, LRU_BLOCK, LRU_BLOCK), LRU_BLOCK ** -0.5),
        'od_ga_b': normal((N_ODD, LRU_WIDTH), 0.02),
        'od_lam': jnp.log(s) - jnp.log1p(-s),
        'od_w_out': normal((N_ODD, LRU_WIDTH, D_MODEL), LRU_WIDTH ** -0.5),
        'ff_norm': gain((DEPTH, D_MODEL)),
        'ff_w1': normal((DEPTH, D_MODEL, D_FF), D_MODEL ** -0.5),
        'ff_w2': normal((DEPTH, D_FF, D_MODEL), D_FF ** -0.5),
        'final_norm': gain((D_MODEL,)),
    }

def reference(x, ev_norm, ev_w_in, ev_w_out, rw_mu, rw_w0, rw_w2, rw_a0, rw_a2, rw_g2,
              rw_k_k, rw_k_a, rw_r_k, rw_lnx_w, rw_lnx_b, rw_v0, rw_v1, rw_v2,
              od_norm, od_w_in, od_conv_w, od_conv_b, od_gx_w, od_gx_b, od_ga_w, od_ga_b,
              od_lam, od_w_out, ff_norm, ff_w1, ff_w2, final_norm):
    h = x
    v_first = None
    for layer in range(DEPTH):
        if layer % 2 == 0:
            e = layer // 2
            v_res = None if e == 0 else (rw_v0[e - 1], rw_v1[e - 1], rw_v2[e - 1])
            mix, v_first = _even_mixer(
                _rmsnorm(h, ev_norm[e]), ev_w_in[e], ev_w_out[e], rw_mu[e], rw_w0[e], rw_w2[e],
                rw_a0[e], rw_a2[e], rw_g2[e], rw_k_k[e], rw_k_a[e], rw_r_k[e],
                rw_lnx_w[e], rw_lnx_b[e], v_first, v_res)
        else:
            o = layer // 2
            mix = _odd_mixer(
                _rmsnorm(h, od_norm[o]), od_w_in[o], od_conv_w[o], od_conv_b[o],
                od_gx_w[o], od_gx_b[o], od_ga_w[o], od_ga_b[o], od_lam[o], od_w_out[o])
        h = h + mix
        h = h + _sq_relu_mlp(_rmsnorm(h, ff_norm[layer]), ff_w1[layer], ff_w2[layer])
    return _rmsnorm(h, final_norm)


_drawn_inputs = setup_inputs


def setup_inputs(seed=0):
    import zlib

    import numpy as np

    out = dict(_drawn_inputs(seed))
    spreads = {}
    factors = {'rw_w2': 4.131,
     'rw_a0': 3.375,
     'rw_k_k': 94.583,
     'rw_k_a': 6.277,
     'rw_lnx_w': 7.459,
     'rw_lnx_b': 5.472,
     'od_norm': 12.846,
     'od_gx_b': 25.037,
     'od_ga_b': 27.104,
     'final_norm': 23.826,
     'od_conv_b': 3.489,
     'ff_norm': 4.307}
    for name, (base, spread) in spreads.items():
        noise = np.random.default_rng([zlib.crc32(name.encode()), seed]).standard_normal(out[name].shape)
        drawn = base * np.exp(spread * noise) if base else spread * noise
        out[name] = jnp.asarray(drawn.astype(out[name].dtype))
    for name, factor in factors.items():
        out[name] = (out[name] * factor).astype(out[name].dtype)
    return out
```

```python
from contextlib import ExitStack

import concourse.bass as bass
from concourse import mybir

ALU = mybir.AluOpType
ACT = mybir.ActivationFunctionType
AX_X = mybir.AxisListType.X
F32 = mybir.dt.float32
F32R = mybir.dt.float32r

P = 128
T = 256
HALVES = T // P
D = 2048
KT = D // P
WIDE = 512
UNITS = 8
KU = KT // UNITS
RING = 4
CHUNK = 64
NCHUNK = T // CHUNK
RET_W = 1024
RET_HEADS = 4
RW_BLOCKS = 8
LEVELS = 6
CONV = 4
SLAB = 212832
LORA_W = 288
FF = 8192
QUARTERS = FF // D
NORM_EPS = 1e-6
RET_EPS = 1e-5
RW_EPS = 64e-5
DECAY_C = 0.6065306597126334
LRU_C = 8.0
LRU_BLOCKS = 8

COLS = {}
for _name, _n in (("mu", 27), ("w0", 8), ("a0", 8), ("k_k", 8), ("k_a", 8), ("r_k", 8), ("lnx_w", 8), ("lnx_b", 8),
                  ("ev_norm", 16), ("ff_norm0", 16), ("od_norm", 16), ("ff_norm1", 16), ("conv_w", 64),
                  ("conv_b", 16), ("gx_b", 16), ("ga_b", 16), ("lam", 16)):
    COLS[_name] = (sum(n for _, n in COLS.values()), _n)
NPAR = sum(n for _, n in COLS.values())
CIDENT, CONES, CLEVEL, CSTRICT, CINCL, CSEG = 0, 128, 256, 256 + 128 * LEVELS, 384 + 128 * LEVELS, 448 + 128 * LEVELS
NCONST = CSEG + 256


def trunk(nc, x_in, params, consts, cossin, rdecay, ev_w_in, ev_w_out, rw_w2, rw_a2, rw_g2, od_w_in, gx_w, ga_w,
          od_w_out, ff_w1, ff_w2, final_norm, out):
    ctx = ExitStack()
    with ctx:
        def sb(name, shape, dt=F32, scope=ctx):
            return scope.enter_context(nc.sbuf_tensor(name, shape, dt))

        sems = {}

        def sem(name):
            if name not in sems:
                sems[name] = ctx.enter_context(nc.semaphore(name))
            return sems[name]

        def nbytes(shape):
            n = 4
            for v in shape[1:]:
                n *= v
            return -(-n // 32) * 32

        slab_start = -(-nc.sbuf_base // 32) * 32
        slab = sb("slab", [P, SLAB // 4])

        class Region:
            def __init__(self, at):
                self.at = at

            def __call__(self, name, shape, dt=F32):
                t = nc.alloc_sbuf_tensor_at(name, shape, dt, offset=slab_start + self.at)
                self.at += nbytes(shape)
                assert self.at <= SLAB, (name, self.at)
                return t

        lasting = Region(0)
        x = lasting("x", [P, HALVES, D])
        xT_hi = lasting("xT_hi", [P, KT, T], F32R)
        xT_lo = lasting("xT_lo", [P, KT, T], F32R)
        raw = lasting("raw", [P, RING, KU, WIDE])
        w_hi = lasting("w_hi", [P, RING, KU, WIDE], F32R)
        w_lo = lasting("w_lo", [P, RING, KU, WIDE], F32R)
        par = lasting("par", [P, NPAR])
        con = lasting("con", [P, NCONST])
        ssq = lasting("ssq", [P, 4, HALVES])
        rstd = lasting("rstd", [P, HALVES])
        lam = lasting("lam", [P, 6, KT])
        stg = lasting("stg", [P, 2, HALVES, WIDE])
        junk = lasting("junk", [P, WIDE])
        ident = con[:, CIDENT:CIDENT + P]
        HALF = KT // 2 * T * 4

        low = lasting.at
        at_a = Region(low)
        hidA_hi, hidA_lo = (at_a(n, [P, KT // 2, T], F32R) for n in ("hidA_hi", "hidA_lo"))
        at_b = Region(low + 4 * HALF)
        hidB_hi, hidB_lo = (at_b(n, [P, KT // 2, T], F32R) for n in ("hidB_hi", "hidB_lo"))
        early = Region(low)
        ret_tok = early("ret_tok", [P, 8, HALVES, WIDE])
        z = early("z", [P, 3 * RW_BLOCKS, T])
        rw = Region(early.at)
        lora_in = rw("lora_in", [P, 4, T])
        lora_w = rw("lora_w", [P, 3, P])
        half_bias = rw("half_bias", [P, 2, RW_BLOCKS])

        def diagonal(name):
            return rw(name, [P, NCHUNK, P])

        v_bd, beta_bd, key_bd, kappa_bd = (diagonal(n) for n in ("v_bd", "beta_bd", "key_bd", "kappa_bd"))
        v_tok, key_tok, beta_tok = (diagonal(n) for n in ("v_tok", "key_tok", "beta_tok"))
        level_a, inv_t, seen_v = (diagonal(n) for n in ("level_a", "inv_t", "seen_v"))
        seen_y = rw("seen_y", [P, 2, NCHUNK, CHUNK])
        state = rw("state", [P, 2, P])
        scaled, rhs_u, u_bd = (rw(n, [P, P]) for n in ("scaled", "rhs_u", "u_bd"))
        decay = rw("decay", [P, NCHUNK, CHUNK + 1])
        extra = rw("extra", [P, 4, T])
        rt = Region(early.at)
        qT, kT = rt("qT", [P, 8, T]), rt("kT", [P, 8, T])
        table_d = rt("table_d", [P, 2, HALVES, T])
        table_cs = rt("table_cs", [P, HALVES, 2, P])
        rot_q, rot_k = (rt(n, [P, 4, HALVES, P]) for n in ("rot_q", "rot_k"))
        scores, y_ret = (rt(n, [P, 2, HALVES, T]) for n in ("scores", "y_ret"))
        rstat, rmean, rdev = rt("rstat", [P, HALVES, 6]), rt("rmean", [P, HALVES, 2]), rt("rdev", [P, HALVES])
        od_a = Region(low)
        gate_a = od_a("gate_a", [P, KT, T])
        od_b = Region(low + 4 * HALF)
        gate_x = od_b("gate_x", [P, KT, T])
        x_rest = Region(low + 2 * HALF)
        conv = x_rest("conv", [P, KT, T])
        x_raw = od_b("x_raw", [P, KT, T + CONV - 1])
        gate_w = od_b("gate_w", [P, 2, 2, 2, T])
        gate_t = od_b("gate_t", [P, KT, T])

        acc = [ctx.enter_context(nc.psum_tensor(f"acc{i}", [P, WIDE], F32)) for i in range(4)]
        tp = [ctx.enter_context(nc.psum_tensor(f"tp{i}", [P, WIDE], F32)) for i in range(4)]

        def pcol(name, k):
            return par[:, COLS[name][0] + k:COLS[name][0] + k + 1]

        def xT(kt):
            return xT_hi[:, kt, :], xT_lo[:, kt, :]

        def hid(kt):
            a, b = (hidA_hi, hidA_lo) if kt < KT // 2 else (hidB_hi, hidB_lo)
            return a[:, kt % (KT // 2), :], b[:, kt % (KT // 2), :]

        raw_landed = [sem(f"raw_landed{i}") for i in range(RING)]
        hi_ready, lo_ready, unit_used = sem("hi_ready"), sem("lo_ready"), sem("unit_used")
        t_done = [sem("t_done0"), sem("t_done1")]
        x_landed, x_updated, ssq_done = sem("x_landed"), sem("x_updated"), sem("ssq_done")
        stg_written, squared, t_hi, lhs_ready, z_ready = (sem("stg_written"), sem("squared"), sem("t_hi"),
                                                         sem("lhs_ready"), sem("z_ready"))
        var_ready, std_ready, rstd_ready = sem("var_ready"), sem("std_ready"), sem("rstd_ready")

        def wait_count(eng, s, value):
            if not isinstance(value, int) or value > 0:
                eng.wait_ge(s, value)

        def load_unit(sp, n, j, w, row0, col0, wide=WIDE):
            wait_count(sp, lo_ready, 8 * n + j - RING + 1)
            src = w[bass.ds(row0 + j * KU * P, KU * P), bass.ds(col0, wide)].rearrange("(k p) n -> p k n", p=P)
            sp.dma_start(raw[:, j % RING, :, 0:wide], src).then_inc(raw_landed[j % RING], 16)

        def split_hi(act, n, j, wide=WIDE):
            act.wait_ge(raw_landed[j % RING], 16 * (2 * n + j // RING + 1))
            wait_count(act, unit_used, 8 * n + j - RING + 1)
            act.activation(w_hi[:, j % RING, :, 0:wide], raw[:, j % RING, :, 0:wide], ACT.Copy).then_inc(hi_ready, 1)

        def split_lo(dve, n, j, wide=WIDE):
            dve.wait_ge(hi_ready, 8 * n + j + 1)
            dve.tensor_tensor(w_lo[:, j % RING, :, 0:wide], raw[:, j % RING, :, 0:wide],
                              w_hi[:, j % RING, :, 0:wide], ALU.subtract).then_inc(lo_ready, 1)

        def multiply_part(pe, n, part, lhs, bank, wide=WIDE):
            j, kt, h = part // 4, part // 2, part % 2
            if part % 4 == 0:
                pe.wait_ge(lo_ready, 8 * n + j + 1)
            hi, lo = lhs(kt)
            o, tok = acc[2 * bank + h][:, 0:wide], slice(h * P, (h + 1) * P)
            wh, wl = w_hi[:, j % RING, kt % KU, 0:wide], w_lo[:, j % RING, kt % KU, 0:wide]
            nc.tensor.matmul(o, hi[:, tok], wh, start=(kt == 0), stop=False)
            nc.tensor.matmul(o, hi[:, tok], wl, start=False, stop=False)
            last = nc.tensor.matmul(o, lo[:, tok], wh, start=False, stop=(kt == KT - 1))
            if part % 4 == 3:
                last.then_inc(unit_used, 1)

        def multiply_unit(pe, n, j, lhs, bank, wide=WIDE):
            for part in range(4 * j, 4 * j + 4):
                multiply_part(pe, n, part, lhs, bank, wide)

        def sp_group(sp, g, w, row0, col0):
            for j in range(UNITS):
                load_unit(sp, g["n"], j, w, row0, col0, g["wide"])

        def pe_group(pe, g, lhs, prev=None):
            if g["free"]:
                pe.wait_ge(*g["free"])
            for j in range(UNITS):
                if j == 2 and prev:
                    pe_post(pe, prev)
                if callable(g["need"]):
                    g["need"](pe, j)
                elif g["need"] is not None and j in (0, 6):
                    pe.wait_ge(lhs_ready, g["need"][j // 6])
                multiply_unit(pe, g["n"], j, lhs, g["bank"], g["wide"])

        def act_group(act, g, prev=None):
            for j in range(UNITS):
                split_hi(act, g["n"], j, g["wide"])
                if j == 2 and prev:
                    act_evacuate(act, prev)
                if j == 5 and prev:
                    act_after_transpose(act, prev)

        def dve_group(dve, g, prev=None):
            for j in range(UNITS):
                split_lo(dve, g["n"], j, g["wide"])
                if j == 2 and prev:
                    dve_evacuate(dve, prev)
                if j == 5 and prev:
                    dve_after_transpose(dve, prev)
                if j == 7 and prev:
                    dve_finish_norm(dve, prev)

        def act_evacuate(act, g):
            if g["post"] in ("square", "z"):
                act.wait_ge(unit_used, 8 * (g["n"] + 1))
                act.wait_ge(rstd_ready, g["norm"])
                wait_count(act, t_done[g["bank"]], g["tused"])
                for h in range(HALVES):
                    last = act.activation(stg[:, g["bank"], h, 0:g["wide"]], acc[2 * g["bank"] + h][:, 0:g["wide"]],
                                          g.get("func", ACT.Relu if g["post"] == "square" else ACT.Copy),
                                          scale=rstd[:, h:h + 1])
                    last.then_inc(stg_written, 1)

        def pool_square(pool, g):
            pool.wait_ge(stg_written, 2 * g["stg"] + 2)
            s = stg[:, g["bank"], :, :]
            pool.tensor_tensor(s, s, s, ALU.mult).then_inc(squared, 1)

        def pe_post(pe, g):
            b = g["bank"]
            if g["post"] == "x":
                if not g["transposed"]:
                    return
                if g.get("loaded"):
                    pe.wait_ge(x_landed, 32)
                else:
                    pe.wait_ge(x_updated, g["xu"] + 1)
                src = lambda h, c: x[:, h, g["col"] + c * P:g["col"] + (c + 1) * P]
            else:
                if g["post"] == "square":
                    pe.wait_ge(squared, g["hid"] + 1)
                else:
                    pe.wait_ge(stg_written, 2 * g["stg"] + 2)
                src = lambda h, c: stg[:, b, h, c * P:min((c + 1) * P, g["wide"])]
            if g["tp"]:
                pe.wait_ge(*g["tp"])
            for c in range(-(-g["wide"] // P)):
                for h in range(HALVES):
                    s = src(h, c)
                    last = nc.tensor.transpose(tp[2 * b + c // 2][0:s.shape[1], (c % 2) * T + h * P:(c % 2) * T + (h + 1) * P],
                                               s, ident)
            last.then_inc(t_done[b], 1)

        def act_after_transpose(act, g):
            b = g["bank"]
            if g["post"] == "x" and g.get("summed", True):
                for h in range(HALVES):
                    if g.get("loaded"):
                        act.wait_ge(x_landed, 32)
                    else:
                        act.wait_ge(x_updated, g["xu"] + 1)
                    wait_count(act, ssq_done, HALVES * g["xs"] + h)
                    act.activation(junk[:, :], x[:, h, g["col"]:g["col"] + WIDE], ACT.Square,
                                   accum_out=ssq[:, g["col"] // WIDE, h:h + 1]).then_inc(ssq_done, 1)
                if g["transposed"]:
                    act.wait_ge(t_done[b], g["tused"] + 1)
                    for c in range(4):
                        kt = g["col"] // P + c
                        act.activation(xT_hi[:, kt, :], tp[2 * b + c // 2][:, (c % 2) * T:(c % 2 + 1) * T], ACT.Copy,
                                       scale=pcol(g["gain"], kt)).then_inc(t_hi, 1)
                if g["col"] == 3 * WIDE and g.get("summed", True):
                    act.wait_ge(var_ready, 2 * g["norm"])
                    act.activation(rstd[:, :], rstd[:, :], ACT.Sqrt).then_inc(std_ready, 1)
            if g["post"] == "square":
                act.wait_ge(t_done[b], g["tused"] + 1)
                for c in range(2):
                    t = (hidA_hi if g["g"] < 2 else hidB_hi)[:, (4 * g["g"] + 2 * c) % 8:(4 * g["g"] + 2 * c) % 8 + 2, :]
                    act.activation(t, tp[2 * b + c][:, :].rearrange("p (c t) -> p c t", c=2), ACT.Copy).then_inc(t_hi, 1)

        def dve_evacuate(dve, g):
            if g["post"] == "x" and not g.get("loaded"):
                dve.wait_ge(unit_used, 8 * (g["n"] + 1))
                for h in range(HALVES):
                    xs = x[:, h, g["col"]:g["col"] + WIDE]
                    last = dve.tensor_tensor(xs, acc[2 * g["bank"] + h][:, :], xs, ALU.add)
                last.then_inc(x_updated, 1)

        def dve_after_transpose(dve, g):
            b = g["bank"]
            if g["post"] == "x":
                if g["transposed"]:
                    for c in range(4):
                        kt = g["col"] // P + c
                        dve.wait_ge(t_hi, g["thi"] + 2 * (c // 2) + 2)
                        last = dve.scalar_tensor_tensor(xT_lo[:, kt, :], tp[2 * b + c // 2][:, (c % 2) * T:(c % 2 + 1) * T],
                                                        pcol(g["gain"], kt), xT_hi[:, kt, :], ALU.mult, ALU.subtract)
                        last.then_inc(lhs_ready, 1)
                if g["col"] == 3 * WIDE and g.get("summed", True):
                    dve.wait_ge(ssq_done, HALVES * (g["xs"] + 1))
                    dve.tensor_reduce(rstd[:, :], ssq[:, :, :].rearrange("p g h -> p h g"), AX_X, ALU.add).then_inc(var_ready, 1)
                    dve.wait_ge(var_ready, 2 * g["norm"] - 1)
                    dve.tensor_scalar(rstd[:, :], rstd[:, :], 1.0 / D, NORM_EPS, ALU.mult, ALU.add).then_inc(var_ready, 1)
            if g["post"] == "square":
                for c in range(2):
                    k = (4 * g["g"] + 2 * c) % 8
                    a, l = (hidA_hi, hidA_lo) if g["g"] < 2 else (hidB_hi, hidB_lo)
                    dve.wait_ge(t_hi, g["thi"] + c + 1)
                    dve.tensor_tensor(l[:, k:k + 2, :], tp[2 * b + c][:, :].rearrange("p (c t) -> p c t", c=2),
                                      a[:, k:k + 2, :], ALU.subtract).then_inc(lhs_ready, 1)
            if g["post"] == "z":
                for c in range(-(-g["wide"] // (2 * P))):
                    dve.wait_ge(t_done[b], g["tused"] + 1)
                    g["move"](dve, c, tp[2 * b + c]).then_inc(z_ready, 1)

        def dve_finish_norm(dve, g):
            if g["post"] == "x" and g["col"] == 3 * WIDE and g.get("summed", True):
                dve.wait_ge(std_ready, g["norm"])
                dve.reciprocal(rstd[:, :], rstd[:, :]).then_inc(rstd_ready, 1)

        def step(role, eng, g, w, row0, col0, lhs, prev):
            if role == "sp":
                sp_group(eng, g, w, row0, col0)
            elif role == "pe":
                pe_group(eng, g, lhs, prev)
            elif role == "act":
                act_group(eng, g, prev)
            elif role == "dve":
                dve_group(eng, g, prev)
            elif prev and prev["post"] == "square":
                pool_square(eng, prev)

        def finish(role, eng, prev):
            if role == "pe":
                pe_post(eng, prev)
            elif role == "act":
                act_evacuate(eng, prev)
                act_after_transpose(eng, prev)
            elif role == "dve":
                dve_evacuate(eng, prev)
                dve_after_transpose(eng, prev)
                dve_finish_norm(eng, prev)
            elif role == "pool" and prev["post"] == "square":
                pool_square(eng, prev)

        def load_posts(gain):
            return [dict(post="x", loaded=True, transposed=True, gain=gain, col=k * WIDE, bank=k % 2, wide=WIDE,
                         tused=k // 2, tp=(lhs_ready, 4 * (k - 1)) if k > 1 else None, xu=0, xs=k, thi=4 * k,
                         lhs=4 * k, norm=1) for k in range(4)]

        def residual(c, k, gain, q=0, last=True):
            return dict(n=c["n"] + k, bank=k % 2, post="x", col=k * WIDE, transposed=last and gain is not None, gain=gain,
                        summed=last, wide=WIDE, tused=c["tused"][k % 2] + k // 2, xu=c["xu"] + k, xs=c["xs"] + k,
                        thi=c["thi"] + 4 * k, lhs=c["lhs"] + 4 * k, tp=(lhs_ready, c["lhs"] + 4 * max(k - 1, 0)),
                        norm=c["norm"] + 1)

        def mlp_group(c, q, g, gain):
            n, lhs0 = c["n"] + 8 * q, c["lhs"] + 8 * q
            if g < 4:
                free = (x_updated, c["xu"] + 4 * (q - 1) + g + 3) if g < 2 else (stg_written, 2 * (c["stg"] + 4 * q + g - 1))
                return dict(n=n + g, bank=g % 2, post="square", g=g, wide=WIDE, free=free, need=(c["lhs"] - 4, c["lhs"]),
                            tused=c["tused"][g % 2] + 2 * q + g // 2, stg=c["stg"] + 4 * q + g, hid=c["hid"] + 4 * q + g,
                            thi=c["thi"] + 8 * q + 2 * g, lhs=lhs0 + 2 * g, tp=(lhs_ready, lhs0 + 2 * max(g - 1, 0)),
                            norm=c["norm"])
            k, last = g - 4, isinstance(q, int) and q == QUARTERS - 1
            at = dict(n=n + 4, tused=[t + 2 * q + 2 for t in c["tused"]], xu=c["xu"] + 4 * q, xs=c["xs"], thi=c["thi"] + 8 * q + 8,
                      lhs=lhs0 + 8, norm=c["norm"])
            r = residual(at, k, gain, last=last)
            r["free"] = (stg_written, 2 * (c["stg"] + 4 * q + g - 1)) if k < 2 else (x_updated, at["xu"] + k - 1)
            r["need"] = (lhs0 + 6, lhs0 + 8)
            return r

        def mlp(role, eng, layer, c, prev, gain):
            w1, w2 = ff_w1[layer], ff_w2[layer]

            def part(q, g, prev):
                if g < 4:
                    step(role, eng, mlp_group(c, q, g, gain), w1, 0, q * D + g * WIDE, xT, prev)
                else:
                    step(role, eng, mlp_group(c, q, g, gain), w2, q * D, (g - 4) * WIDE, hid, prev)

            part(0, 0, prev)
            with eng.Fori(0, QUARTERS - 1) as q:
                for g in range(1, 8):
                    part(q, g, mlp_group(c, q, g - 1, gain))
                part(q + 1, 0, mlp_group(c, q, 7, gain))
            for g in range(1, 8):
                part(QUARTERS - 1, g, mlp_group(c, QUARTERS - 1, g - 1, gain))
            return mlp_group(c, QUARTERS - 1, 7, gain)

        def after_mlp(c, gain):
            t = 4 if gain else 0
            return dict(n=c["n"] + 32, tused=[v + 8 + t // 2 for v in c["tused"]], stg=c["stg"] + 16, hid=c["hid"] + 16,
                        xu=c["xu"] + 16, xs=c["xs"] + 4, thi=c["thi"] + 32 + 4 * t, lhs=c["lhs"] + 32 + 4 * t,
                        norm=c["norm"] + 1)

        z_lora = extra

        def tile(t, i):
            return t[:, i // 4, (i // 2) % 2, (i % 2) * T:(i % 2 + 1) * T]

        k_t, r_t, v_t, kk_t, b_t, km_t, sq_t, nrm_t = (tile(stg, i) for i in range(8))
        rho_t, em_t = junk[:, 0:T], junk[:, T:2 * T]
        thw_t, sum_t, iclr_t, outg_t = (extra[:, i, :] for i in range(4))

        def lora_move(dve, c, bank):
            if c == 0:
                return dve.tensor_copy(z_lora[:, 0:2, :], bank[:, :].rearrange("p (c t) -> p c t", c=2))
            return dve.tensor_copy(z_lora[0:32, 2, :], bank[0:32, 0:T])

        LORA = dict(n=0, bank=0, post="z", wide=LORA_W, free=None, need=(12, 16), tused=2, stg=0, norm=1,
                    tp=(lhs_ready, 16), move=lora_move)

        def rkv(i, odd):
            v = 2 * i + odd

            def move(dve, c, bank):
                return dve.tensor_copy(z[:, bass.ds(4 * v + 2 * c, 2), :], bank[:, :].rearrange("p (c t) -> p c t", c=2))

            return dict(n=1 + v, bank=1 - odd, post="z", wide=WIDE, need=None, stg=1 + v, norm=1, move=move,
                        free=None if isinstance(v, int) and v == 0 else (stg_written, 2 * v), tused=2 + odd + i,
                        tp=(z_ready, 2 * v + 2))

        RET_IN = 4 * RET_W

        def even_in(role, eng, prev):
            step(role, eng, LORA, ev_w_in, 0, RET_IN + 3 * RET_W, xT, prev)
            step(role, eng, rkv(0, 0), ev_w_in, 0, RET_IN, xT, LORA)
            with eng.Fori(0, 2) as i:
                step(role, eng, rkv(i, 1), ev_w_in, 0, RET_IN + (2 * i + 1) * WIDE, xT, rkv(i, 0))
                step(role, eng, rkv(i + 1, 0), ev_w_in, 0, RET_IN + (2 * i + 2) * WIDE, xT, rkv(i, 1))
            step(role, eng, rkv(2, 1), ev_w_in, 0, RET_IN + 5 * WIDE, xT, rkv(2, 0))
            finish(role, eng, rkv(2, 1))

        RET_N, RET_STG = 7, 7

        def once(eng, name, count):
            eng.wait_ge(sem(name), count)

        class Own:

            def __init__(self, eng, name, it=0, per=0):
                self.eng, self.sem, self.base, self.per, self.k = eng, sem(name), it * per, per, 0

            def __call__(self, ins):
                self.k += 1
                ins.then_inc(self.sem, 1)
                self.eng.wait_ge(self.sem, self.base + self.k)

            def end(self):
                assert not self.per or self.k == self.per, self.k

        HEADS = ((slice(0, 64), slice(0, 64)), (slice(64, 128), slice(64, 128)))

        def chunks(t):
            return t.rearrange("p (c t) -> p c t", c=NCHUNK)

        def over_chunks(col, wide=P):
            return con[:, col:col + wide].rearrange("p (o n) -> p o n", o=1).broadcast_to((P, NCHUNK, wide))

        def pcol_at(name, p):
            return par[:, bass.ds(p + COLS[name][0], 1)]

        def mix_difference(dve, own, dst, src, rows=P):
            dve.tensor_tensor(dst[0:rows, 1:T], src[0:rows, 0:T - 1], src[0:rows, 1:T], ALU.subtract).then_inc(own, 1)
            dve.tensor_scalar(dst[0:rows, 0:1], src[0:rows, 0:1], -1.0, None, ALU.mult).then_inc(own, 1)

        def rwkv_zero(dve):
            for t in (v_bd, beta_bd, key_bd, kappa_bd):
                dve.memset(t[:, :, :], 0.0).then_inc(sem("rw_zeroed"), 1)
            for t in (lora_in[64:128, 0, :], lora_in[0:64, 1, :], lora_in[32:64, 3, :], lora_in[64:128, 3, :],
                      lora_w[32:64, 2, :], lora_w[64:128, 2, :]):
                dve.memset(t, 0.0).then_inc(sem("rw_zeroed"), 1)
            dve.memset(decay[:, :, 0:1], 1.0).then_inc(sem("rw_zeroed"), 1)

        def load_lora(pool, p):
            landed = sem("lora_landed")
            cols = bass.ds(p * P, P)
            pool.dma_start(lora_w[0:64, 0, :], rw_w2[:, cols]).then_inc(landed, 16)
            pool.dma_start(lora_w[64:128, 0, :], rw_a2[:, cols]).then_inc(landed, 16)
            pool.dma_start(lora_w[:, 1, :], rw_g2[0:P, cols]).then_inc(landed, 16)
            pool.dma_start(lora_w[0:32, 2, :], rw_g2[P:P + 32, cols]).then_inc(landed, 16)

        def rwkv_prepare_dve(dve):
            for i, name in enumerate(("w0", "a0")):
                c0 = COLS[name][0]
                dve.tensor_scalar(half_bias[:, i, :], par[:, c0:c0 + RW_BLOCKS], 0.5, None, ALU.mult)\
                   .then_inc(sem("half_bias_ready"), 1)
            once(dve, "z_ready", 14)
            rows = (P, P, 32)
            for i, (dst, n) in enumerate(zip((kk_t, b_t, km_t), rows)):
                mix_difference(dve, sem("lora_difference"), dst, z_lora[:, i, :], n)
            for i, (dst, dif, n) in enumerate(zip((k_t, r_t, v_t), (kk_t, b_t, km_t), rows)):
                once(dve, "lora_difference", 2 * i + 2)
                mu = par[0:n, COLS["mu"][0] + 24 + i:COLS["mu"][0] + 25 + i]
                dve.scalar_tensor_tensor(dst[0:n], dif[0:n], mu, z_lora[0:n, i, :], ALU.mult, ALU.add)\
                   .then_inc(sem("lora_mixed"), 1)
            once(dve, "lora_inputs", 4)

        def rwkv_prepare_act(act):
            once(act, "rw_zeroed", 11)
            once(act, "lora_mixed", 3)
            done = sem("lora_inputs")
            act.activation(lora_in[0:64, 0, :], k_t[0:64], ACT.Tanh).then_inc(done, 1)
            act.activation(lora_in[64:128, 1, :], k_t[64:128], ACT.Copy).then_inc(done, 1)
            act.activation(lora_in[:, 2, :], r_t, ACT.Sigmoid).then_inc(done, 1)
            act.activation(lora_in[0:32, 3, :], v_t[0:32], ACT.Sigmoid).then_inc(done, 1)
            once(act, "half_bias_ready", 2)

        def rwkv_pool(pool, p, load):
            if load:
                pool.wait_ge(sem("lora_done"), p + 1)
                load_lora(pool, p + 1)
            for l in range(1, LEVELS):
                if l == 1:
                    pool.wait_ge(sem("inv_start"), p + 1)
                else:
                    pool.wait_ge(sem("y_done"), 5 * p + l - 1)
                pool.tensor_tensor(level_a[:, :, :], v_bd[:, :, :], over_chunks(CLEVEL + l * P), ALU.mult)\
                    .then_inc(sem("level_ready"), 1)

        def rwkv_dve(dve, p):
            n = RET_N + p
            own = Own(dve, "dve_own", p, 13)
            split_lo(dve, n, 0)
            dif = sem("difference")
            for i, (dst, blk) in enumerate(((kk_t, 8), (b_t, 0), (km_t, 16))):
                mix_difference(dve, dif, dst, z[:, bass.ds(p + blk, 1), :].rearrange("p o t -> p (o t)"))
            for i, (dst, d, blk) in enumerate(((k_t, kk_t, 8), (r_t, b_t, 0), (v_t, km_t, 16))):
                dve.wait_ge(dif, 6 * p + 2 * i + 2)
                dve.scalar_tensor_tensor(dst, d, pcol_at("mu", p + blk), z[:, bass.ds(p + blk, 1), :]
                                         .rearrange("p o t -> p (o t)"), ALU.mult, ALU.add).then_inc(sem("mixed"), 1)
            split_lo(dve, n, 1)
            dve.wait_ge(sem("kk_sum_done"), p + 1)
            dve.tensor_scalar(nrm_t, tp[0][:, 0:T], 1e-24, None, ALU.max).then_inc(sem("kk_sum_read"), 1)
            dve.wait_ge(sem("tanh_ready"), 2 * p + 1)
            own(dve.tensor_scalar(thw_t, thw_t, 1.0, None, ALU.add))
            dve.tensor_tensor_scan(sum_t, con[:, CSEG:CSEG + T], thw_t, 0.0, ALU.mult, ALU.add)\
               .then_inc(sem("log_decay_ready"), 1)
            dve.wait_ge(sem("tanh_ready"), 2 * p + 2)
            own(dve.tensor_scalar(iclr_t, iclr_t, 0.5, 0.5, ALU.mult, ALU.add))
            own(dve.tensor_scalar(km_t, iclr_t, -1.0, pcol_at("k_a", p), ALU.add, ALU.mult))
            own(dve.scalar_tensor_tensor(km_t, km_t, 1.0, k_t, ALU.add, ALU.mult))
            dve.wait_ge(sem("kk_root_ready"), p + 1)
            own(dve.reciprocal(nrm_t, nrm_t))
            own(dve.scalar_tensor_tensor(kk_t, k_t, pcol_at("k_k", p), nrm_t, ALU.mult, ALU.mult))
            own(dve.tensor_tensor(b_t, kk_t, iclr_t, ALU.mult))
            split_lo(dve, n, 2)
            dve.wait_ge(sem("decay_ready"), 2 * p + 2)
            for a, b in HEADS:
                dve.tensor_tensor(kappa_bd[a, :, b], chunks(kk_t[a]), decay[a, :, 0:CHUNK], ALU.mult).then_inc(sem("kappa_ready"), 1)
            dve.tensor_tensor(chunks(rho_t), chunks(r_t), decay[:, :, 1:CHUNK + 1], ALU.mult).then_inc(sem("kappa_ready"), 1)
            for a, b in HEADS:
                dve.tensor_tensor(beta_bd[a, :, b], chunks(b_t[a]), chunks(em_t[a]), ALU.mult).then_inc(sem("kappa_ready"), 1)
            for a, b in HEADS:
                dve.tensor_tensor(key_bd[a, :, b], chunks(km_t[a]), chunks(em_t[a]), ALU.mult).then_inc(sem("kappa_ready"), 1)
            dve.scalar_tensor_tensor(sq_t, r_t, pcol_at("r_k", p), km_t, ALU.mult, ALU.mult).then_inc(sem("bonus_in"), 1)
            split_lo(dve, n, 3)
            dve.wait_ge(sem("products_done"), p + 1)
            dve.tensor_tensor(seen_v[:, :, :], tp[2][:, :].rearrange("p (c n) -> p c n", c=NCHUNK), over_chunks(CSTRICT),
                              ALU.mult).then_inc(sem("seen_ready"), 1)
            dve.scalar_tensor_tensor(seen_y[:, 0, :, :], chunks(tp[3][:, 0:T]), -1.0, over_chunks(CINCL, CHUNK),
                                     ALU.mult, ALU.mult).then_inc(sem("seen_ready"), 1)
            dve.tensor_tensor(seen_y[:, 1, :, :], chunks(tp[3][:, T:2 * T]), over_chunks(CINCL, CHUNK),
                              ALU.mult).then_inc(sem("seen_ready"), 1)
            dve.wait_ge(sem("a_copied"), p + 1)
            own(dve.tensor_tensor(level_a[:, :, :], v_bd[:, :, :], over_chunks(CLEVEL), ALU.mult))
            dve.wait_ge(sem("tokens_done"), 3 * p + 2)
            own(dve.tensor_tensor(key_bd[:, :, :], over_chunks(CIDENT), level_a[:, :, :], ALU.subtract))
            dve.sem_inc(sem("inv_start"), 1)
            split_lo(dve, n, 4)
            for l in range(1, LEVELS):
                dve.wait_ge(sem("y_done"), 5 * p + l)
                if l == 1:
                    dve.wait_ge(sem("tokens_done"), 3 * p + 3)
                dve.tensor_tensor(beta_bd[:, :, :], over_chunks(CIDENT), tp[2][:, :].rearrange("p (c n) -> p c n", c=NCHUNK),
                                  ALU.subtract).then_inc(sem("w_ready"), 1)
                if l < LEVELS - 1:
                    dve.wait_ge(sem("inv_done"), 4 * p + l)
                    dve.tensor_copy(key_bd[:, :, :], tp[0][:, :].rearrange("p (c n) -> p c n", c=NCHUNK))\
                       .then_inc(sem("inv_ready"), 1)
                if l == 2:
                    split_lo(dve, n, 5)
            split_lo(dve, n, 6)
            for c in range(NCHUNK - 1):
                dve.wait_ge(sem("state_done"), 3 * p + c + 1)
                new, end = state[:, (c + 1) % 2, :], decay[:, c, CHUNK:CHUNK + 1]
                if c == 0:
                    dve.tensor_scalar(new, tp[0][:, 0:P], end, None, ALU.mult).then_inc(sem("state_ready"), 1)
                else:
                    dve.scalar_tensor_tensor(new, tp[0][:, 0:P], end, scaled[:, :], ALU.mult, ALU.add)\
                       .then_inc(sem("state_ready"), 1)
                if c < NCHUNK - 2:
                    dve.wait_ge(sem("state_ready"), 3 * p + c + 1)
                    own(dve.tensor_scalar(scaled[:, :], new, decay[:, c + 1, CHUNK:CHUNK + 1], None, ALU.mult))
                if c == 1:
                    split_lo(dve, n, 7)
            dve.wait_ge(sem("mean_done"), p + 1)
            dve.scalar_tensor_tensor(b_t, tp[2][:, 0:T], -1.0 / CHUNK, kk_t, ALU.mult, ALU.add).then_inc(sem("centred"), 1)
            dve.wait_ge(sem("bonus_done"), p + 1)
            dve.tensor_tensor(km_t, tp[0][:, 0:T], v_t, ALU.mult).then_inc(sem("bonus_ready"), 1)
            dve.wait_ge(sem("variance_done"), p + 1)
            dve.tensor_scalar(nrm_t, tp[3][:, 0:T], 1.0 / CHUNK, RW_EPS, ALU.mult, ALU.add).then_inc(sem("variance_ready"), 1)
            dve.wait_ge(sem("deviation_ready"), p + 1)
            own(dve.reciprocal(nrm_t, nrm_t))
            own(dve.tensor_tensor(b_t, b_t, nrm_t, ALU.mult))
            dve.tensor_scalar(b_t, b_t, pcol_at("lnx_w", p), pcol_at("lnx_b", p), ALU.mult, ALU.add).then_inc(sem("normed"), 1)
            dve.wait_ge(sem("normed"), 2 * p + 1)
            dve.wait_ge(sem("bonus_ready"), p + 1)
            dve.tensor_tensor(b_t, b_t, km_t, ALU.add).then_inc(sem("normed"), 1)
            dve.wait_ge(sem("normed"), 2 * p + 2)
            dve.tensor_tensor(b_t, b_t, outg_t, ALU.mult).then_inc(sem("gated"), 1)
            dve.wait_ge(sem("rw_hi"), p + 1)
            dve.tensor_tensor(hidB_lo[:, bass.ds(p, 1), :].rearrange("p o t -> p (o t)"), b_t,
                              hidB_hi[:, bass.ds(p, 1), :].rearrange("p o t -> p (o t)"), ALU.subtract)\
               .then_inc(sem("rw_split"), 1)
            dve.wait_ge(sem("rw_split"), p + 1)
            own.end()

        def rwkv_act(act, p):
            n = RET_N + p
            split_hi(act, n, 0)
            split_hi(act, n, 1)
            act.wait_ge(sem("mixed"), 3 * p + 1)
            act.activation(sq_t, k_t, ACT.Square, scale=pcol_at("k_k", p)).then_inc(sem("kk_square"), 1)
            act.wait_ge(sem("mixed"), 3 * p + 3)
            for a, b in HEADS:
                act.activation(v_bd[a, :, b], chunks(v_t[a]), ACT.Copy).then_inc(sem("v_ready"), 1)
            act.wait_ge(sem("kk_sum_read"), p + 1)
            act.activation(nrm_t, nrm_t, ACT.Sqrt).then_inc(sem("kk_root_ready"), 1)
            act.wait_ge(sem("lora_done"), p + 1)
            act.activation(thw_t, tp[1][:, 0:T], ACT.Tanh, scale=0.5,
                           bias=half_bias[:, 0, bass.ds(p, 1)]).then_inc(sem("tanh_ready"), 1)
            act.activation(iclr_t, tp[2][:, 0:T], ACT.Tanh, scale=0.5,
                           bias=half_bias[:, 1, bass.ds(p, 1)]).then_inc(sem("tanh_ready"), 1)
            act.activation(outg_t, tp[3][:, 0:T], ACT.Copy).then_inc(sem("gate_ready"), 1)
            split_hi(act, n, 2)
            act.wait_ge(sem("tokens_done"), 3 * p + 1)
            act.activation(v_tok[:, :, :], tp[0][:, :].rearrange("p (c n) -> p c n", c=NCHUNK), ACT.Copy)\
               .then_inc(sem("tokens_ready"), 1)
            act.wait_ge(sem("log_decay_ready"), p + 1)
            act.activation(decay[:, :, 1:CHUNK + 1], chunks(sum_t), ACT.Exp, scale=-DECAY_C / 2).then_inc(sem("decay_ready"), 1)
            act.activation(em_t, sum_t, ACT.Exp, scale=DECAY_C / 2).then_inc(sem("decay_ready"), 1)
            split_hi(act, n, 3)
            act.wait_ge(sem("products_done"), p + 1)
            act.activation(v_bd[:, :, :], tp[1][:, :].rearrange("p (c n) -> p c n", c=NCHUNK), ACT.Copy)\
               .then_inc(sem("a_copied"), 1)
            act.wait_ge(sem("tokens_done"), 3 * p + 2)
            act.activation(key_tok[:, :, :], tp[0][:, :].rearrange("p (c n) -> p c n", c=NCHUNK), ACT.Copy)\
               .then_inc(sem("tokens_ready"), 1)
            act.wait_ge(sem("tokens_done"), 3 * p + 3)
            act.activation(beta_tok[:, :, :], tp[3][:, :].rearrange("p (c n) -> p c n", c=NCHUNK), ACT.Copy, scale=-1.0)\
               .then_inc(sem("tokens_ready"), 1)
            split_hi(act, n, 4)
            for l in range(LEVELS):
                act.wait_ge(sem("inv_t_done"), LEVELS * p + l + 1)
                act.activation(inv_t[:, :, :], tp[1][:, :].rearrange("p (c n) -> p c n", c=NCHUNK), ACT.Copy)\
                   .then_inc(sem("inv_t_ready"), 1)
                if l == 2:
                    split_hi(act, n, 5)
            split_hi(act, n, 6)
            for c in range(NCHUNK):
                act.wait_ge(sem("rhs_done"), NCHUNK * p + c + 1)
                act.activation(rhs_u[:, :], tp[2][:, 0:P], ACT.Copy).then_inc(sem("rhs_ready"), 1)
                act.wait_ge(sem("u_done"), NCHUNK * p + c + 1)
                act.activation(u_bd[:, :], tp[3][:, 0:P], ACT.Copy).then_inc(sem("u_ready"), 1)
                if c == 1:
                    split_hi(act, n, 7)
            act.wait_ge(sem("out_done"), p + 1)
            act.activation(kk_t, tp[1][:, 0:T], ACT.Copy).then_inc(sem("out_copied"), 1)
            act.wait_ge(sem("centred"), p + 1)
            act.activation(em_t, b_t, ACT.Square).then_inc(sem("centred_square"), 1)
            act.wait_ge(sem("variance_ready"), p + 1)
            act.activation(nrm_t, nrm_t, ACT.Sqrt).then_inc(sem("deviation_ready"), 1)
            act.wait_ge(sem("gated"), p + 1)
            act.activation(hidB_hi[:, bass.ds(p, 1), :].rearrange("p o t -> p (o t)"), b_t, ACT.Copy).then_inc(sem("rw_hi"), 1)
            act.wait_ge(unit_used, 8 * (n + 1))
            for h in range(HALVES):
                act.activation(ret_tok[:, bass.ds(p, 1), h, :].rearrange("p o n -> p (o n)"), acc[2 + h][:, :], ACT.Copy,
                               scale=rstd[:, h:h + 1]).then_inc(stg_written, 1)

        def rwkv_pe(pe, p):
            n = RET_N + p
            done_parts = [0]

            def more(m):
                for part in range(done_parts[0], done_parts[0] + m):
                    multiply_part(pe, n, part, xT, 1)
                done_parts[0] += m

            def mm(out, lhsT, rhs, first=True, last=True):
                return nc.tensor.matmul(out, lhsT, rhs, start=first, stop=last)

            ones = con[:, CONES:CONES + P]
            pe.wait_ge(stg_written, 2 * (RET_STG + p))
            more(2)
            pe.wait_ge(sem("kk_square"), p + 1)
            mm(tp[0][:, 0:T], ones, sq_t).then_inc(sem("kk_sum_done"), 1)
            pe.wait_ge(sem("lora_landed"), 64 * (p + 1))
            mm(tp[1][:, 0:T], lora_w[:, 0, :], lora_in[:, 0, :])
            mm(tp[2][:, 0:T], lora_w[:, 0, :], lora_in[:, 1, :])
            mm(tp[3][:, 0:T], lora_w[:, 1, :], lora_in[:, 2, :], last=False)
            mm(tp[3][:, 0:T], lora_w[:, 2, :], lora_in[:, 3, :], first=False).then_inc(sem("lora_done"), 1)
            more(2)
            pe.wait_ge(sem("v_ready"), 2 * p + 2)
            pe.wait_ge(sem("kk_sum_read"), p + 1)
            for c in range(NCHUNK):
                last = nc.tensor.transpose(tp[0][:, c * P:(c + 1) * P], v_bd[:, c, :], ident)
            last.then_inc(sem("tokens_done"), 1)
            more(3)
            pe.wait_ge(sem("kappa_ready"), 7 * p + 7)
            pe.wait_ge(sem("gate_ready"), p + 1)
            for c in range(NCHUNK):
                rho = chunks(rho_t)[:, c, :]
                mm(tp[1][:, c * P:(c + 1) * P], kappa_bd[:, c, :], beta_bd[:, c, :])
                mm(tp[2][:, c * P:(c + 1) * P], key_bd[:, c, :], kappa_bd[:, c, :])
                mm(tp[3][:, c * CHUNK:(c + 1) * CHUNK], beta_bd[:, c, :], rho)
                last = mm(tp[3][:, T + c * CHUNK:T + (c + 1) * CHUNK], key_bd[:, c, :], rho)
            last.then_inc(sem("products_done"), 1)
            pe.wait_ge(sem("tokens_ready"), 3 * p + 1)
            for c in range(NCHUNK):
                last = nc.tensor.transpose(tp[0][:, c * P:(c + 1) * P], key_bd[:, c, :], ident)
            last.then_inc(sem("tokens_done"), 1)
            more(2)
            pe.wait_ge(sem("seen_ready"), 3 * p + 3)
            for c in range(NCHUNK):
                last = nc.tensor.transpose(tp[3][:, c * P:(c + 1) * P], beta_bd[:, c, :], ident)
            last.then_inc(sem("tokens_done"), 1)
            more(1)
            pe.wait_ge(sem("inv_start"), p + 1)
            for c in range(NCHUNK):
                last = nc.tensor.transpose(tp[1][:, c * P:(c + 1) * P], key_bd[:, c, :], ident)
            last.then_inc(sem("inv_t_done"), 1)
            pe.wait_ge(sem("tokens_ready"), 3 * p + 2)
            for l in range(1, LEVELS):
                more(1)
                pe.wait_ge(sem("level_ready"), 5 * p + l)
                pe.wait_ge(sem("inv_t_ready"), LEVELS * p + l)
                for c in range(NCHUNK):
                    last = mm(tp[2][:, c * P:(c + 1) * P], level_a[:, c, :], inv_t[:, c, :])
                last.then_inc(sem("y_done"), 1)
                more(1)
                pe.wait_ge(sem("w_ready"), 5 * p + l)
                if l > 1:
                    pe.wait_ge(sem("inv_ready"), 4 * p + l - 1)
                for c in range(NCHUNK):
                    last = mm(tp[1][:, c * P:(c + 1) * P], key_bd[:, c, :], beta_bd[:, c, :])
                last.then_inc(sem("inv_t_done"), 1)
                if l < LEVELS - 1:
                    for c in range(NCHUNK):
                        last = mm(tp[0][:, c * P:(c + 1) * P], beta_bd[:, c, :], key_bd[:, c, :])
                    last.then_inc(sem("inv_done"), 1)
            pe.wait_ge(sem("tokens_ready"), 3 * p + 3)
            pe.wait_ge(sem("inv_t_ready"), LEVELS * (p + 1))
            for c in range(NCHUNK):
                s, v = state[:, c % 2, :], v_tok[:, c, :]
                if c:
                    pe.wait_ge(sem("state_ready"), 3 * p + c)
                    mm(tp[2][:, 0:P], kappa_bd[:, c, :], s, last=False)
                mm(tp[2][:, 0:P], seen_v[:, c, :], v, first=(c == 0)).then_inc(sem("rhs_done"), 1)
                more(1)
                pe.wait_ge(sem("rhs_ready"), NCHUNK * p + c + 1)
                mm(tp[3][:, 0:P], inv_t[:, c, :], rhs_u[:, :]).then_inc(sem("u_done"), 1)
                more(1)
                pe.wait_ge(sem("u_ready"), NCHUNK * p + c + 1)
                if c < NCHUNK - 1:
                    mm(tp[0][:, 0:P], key_tok[:, c, :], v, last=False)
                    mm(tp[0][:, 0:P], beta_tok[:, c, :], u_bd[:, :], first=False).then_inc(sem("state_done"), 1)
                y = tp[1][:, c * CHUNK:(c + 1) * CHUNK]
                if c:
                    mm(y, s, chunks(rho_t)[:, c, :], last=False)
                mm(y, v, seen_y[:, 1, c, :], first=(c == 0), last=False)
                last = mm(y, u_bd[:, :], seen_y[:, 0, c, :], first=False)
            last.then_inc(sem("out_done"), 1)
            mm(tp[0][:, 0:T], ones, sq_t).then_inc(sem("bonus_done"), 1)
            more(2)
            pe.wait_ge(sem("out_copied"), p + 1)
            mm(tp[2][:, 0:T], ones, kk_t).then_inc(sem("mean_done"), 1)
            more(32 - done_parts[0])
            pe.wait_ge(sem("centred_square"), p + 1)
            mm(tp[3][:, 0:T], ones, em_t).then_inc(sem("variance_done"), 1)

        def rwkv(role, eng):
            if role == "sp":
                with eng.Fori(0, RW_BLOCKS) as p:
                    for j in range(UNITS):
                        load_unit(eng, RET_N + p, j, ev_w_in, 0, p * WIDE)
            elif role == "pool":
                once(eng, "rw_zeroed", 11)
                load_lora(eng, 0)
                with eng.Fori(0, RW_BLOCKS - 1) as p:
                    rwkv_pool(eng, p, True)
                rwkv_pool(eng, RW_BLOCKS - 1, False)
            elif role == "dve":
                rwkv_prepare_dve(eng)
                with eng.Fori(0, RW_BLOCKS) as p:
                    rwkv_dve(eng, p)
            elif role == "act":
                rwkv_prepare_act(eng)
                with eng.Fori(0, RW_BLOCKS) as p:
                    rwkv_act(eng, p)
            elif role == "pe":
                eng.wait_ge(sem("lora_inputs"), 4)
                with eng.Fori(0, RW_BLOCKS) as p:
                    rwkv_pe(eng, p)

        def ret_view(kind, h, half=None, part=None):
            group, c0 = 2 * kind + h // 2, (h % 2) * 2 * P + (part or 0) * P
            c1 = c0 + (2 * P if part is None else P)
            return ret_tok[:, group, :, c0:c1] if half is None else ret_tok[:, group, half, c0:c1]

        def rotate(eng, kind, rot, name):
            cos, sin = table_cs[:, :, 0, :], table_cs[:, :, 1, :]
            products, done = sem(name + "_products"), sem(name + "_rotated")
            for h in range(RET_HEADS):
                t1, t2 = ret_view(kind, h, part=0), ret_view(kind, h, part=1)
                if h:
                    eng.wait_ge(done, 2 * h)
                for i, (a, b) in enumerate(((t1, cos), (t2, sin), (t2, cos), (t1, sin))):
                    eng.tensor_tensor(rot[:, i, :, :], a, b, ALU.mult).then_inc(products, 1)
                eng.wait_ge(products, 4 * h + 4)
                eng.tensor_tensor(t1, rot[:, 0, :, :], rot[:, 1, :, :], ALU.subtract).then_inc(done, 1)
                eng.tensor_tensor(t2, rot[:, 2, :, :], rot[:, 3, :, :], ALU.add).then_inc(done, 1)

        RET_DONE = 2 * (RET_STG + 8)

        def retention(role, eng):
            if role == "sp":
                once(eng, "rw_split", RW_BLOCKS)
                eng.dma_start(table_cs[:, :, :, :], cossin.rearrange("(h p) a c -> p h a c", p=P)).then_inc(sem("cs_landed"), 16)
                for h in range(RET_HEADS):
                    if h >= 2:
                        once(eng, "scores_ready", h - 1)
                    eng.dma_start(table_d[:, h % 2, :, :], rdecay[h].rearrange("(m p) n -> p m n", p=P))\
                       .then_inc(sem(f"decay_landed{h % 2}"), 16)
            elif role == "pool":
                once(eng, "cs_landed", 16)
                once(eng, "stg_written", RET_DONE)
                rotate(eng, 1, rot_k, "k")
            elif role == "dve":
                once(eng, "cs_landed", 16)
                once(eng, "stg_written", RET_DONE)
                rotate(eng, 0, rot_q, "q")
                for s in range(RET_HEADS + 2):
                    if s < RET_HEADS:
                        if s >= 2:
                            once(eng, "ret_out_done", s - 1)
                        once(eng, "scores_done", s + 1)
                        once(eng, f"decay_landed{s % 2}", 16 * (s // 2 + 1))
                        eng.tensor_tensor(scores[:, s % 2, :, :], acc[s % 2][:, :].rearrange("p (m n) -> p m n", m=HALVES),
                                          table_d[:, s % 2, :, :], ALU.mult).then_inc(sem("scores_ready"), 1)
                    h = s - 1
                    if 0 <= h < RET_HEADS:
                        once(eng, "ret_out_done", h + 1)
                        own = Own(eng, "ret_own", h, 8)
                        for i in range(HALVES):
                            own(eng.bn_stats(rstat[:, i, :], acc[2 + h % 2][:, i * T:(i + 1) * T]))
                        for i in range(HALVES):
                            own(eng.bn_aggr(rmean[:, i, :], rstat[:, i, :]))
                        eng.tensor_scalar(rdev[:, :], rmean[:, :, 1], RET_EPS, None, ALU.add).then_inc(sem("ret_variance"), 1)
                        once(eng, "ret_deviation", h + 1)
                        own(eng.reciprocal(rdev[:, :], rdev[:, :]))
                        for i in range(HALVES):
                            own(eng.tensor_scalar(y_ret[:, h % 2, i, :], acc[2 + h % 2][:, i * T:(i + 1) * T],
                                                  rmean[:, i, 0:1], rdev[:, i:i + 1], ALU.subtract, ALU.mult))
                        once(eng, "ret_gate", 2)
                        own(eng.tensor_tensor(y_ret[:, h % 2, :, :], y_ret[:, h % 2, :, :], ret_view(3, h), ALU.mult))
                        own.end()
                    h = s - 2
                    if h >= 0:
                        once(eng, "ret_hi", h + 1)
                        eng.tensor_tensor(hidA_lo[:, 2 * h:2 * h + 2, :],
                                          tp[2 * (h % 2)][:, :].rearrange("p (c t) -> p c t", c=2),
                                          hidA_hi[:, 2 * h:2 * h + 2, :], ALU.subtract).then_inc(sem("ret_split"), 1)
            elif role == "act":
                once(eng, "stg_written", RET_DONE)
                for i in range(2):
                    g = ret_tok[:, 6 + i, :, :]
                    eng.activation(g, g, ACT.Silu).then_inc(sem("ret_gate"), 1)
                for h in range(RET_HEADS):
                    for i, (t, name) in enumerate(((qT, "q_turned"), (kT, "k_turned"))):
                        once(eng, name, h + 1)
                        eng.activation(t[:, 2 * h:2 * h + 2, :],
                                       tp[2 * (h % 2) + i][:, :].rearrange("p (c t) -> p c t", c=2), ACT.Copy)\
                           .then_inc(sem("qk_ready"), 1)
                for s in range(1, RET_HEADS + 2):
                    if s - 1 < RET_HEADS:
                        once(eng, "ret_variance", s)
                        eng.activation(rdev[:, :], rdev[:, :], ACT.Sqrt).then_inc(sem("ret_deviation"), 1)
                    h = s - 2
                    if h >= 0:
                        once(eng, "y_turned", h + 1)
                        eng.activation(hidA_hi[:, 2 * h:2 * h + 2, :],
                                       tp[2 * (h % 2)][:, :].rearrange("p (c t) -> p c t", c=2), ACT.Copy)\
                           .then_inc(sem("ret_hi"), 1)
            elif role == "pe":
                def turn(bank, view, name):
                    for part in range(2):
                        for half in range(HALVES):
                            last = nc.tensor.transpose(tp[bank][:, part * T + half * P:part * T + (half + 1) * P],
                                                       view(half, part), ident)
                    last.then_inc(sem(name), 1)

                once(eng, "bonus_ready", RW_BLOCKS)
                once(eng, "variance_ready", RW_BLOCKS)
                once(eng, "out_copied", RW_BLOCKS)
                once(eng, "centred", RW_BLOCKS)
                for h in range(RET_HEADS):
                    if h >= 2:
                        once(eng, "qk_ready", 2 * (h - 1))
                    once(eng, "q_rotated", 2 * h + 2)
                    turn(2 * (h % 2), lambda half, part: ret_view(0, h, half, part), "q_turned")
                    once(eng, "k_rotated", 2 * h + 2)
                    turn(2 * (h % 2) + 1, lambda half, part: ret_view(1, h, half, part), "k_turned")
                for s in range(RET_HEADS + 2):
                    if s < RET_HEADS:
                        if s >= 2:
                            once(eng, "scores_ready", s - 1)
                        once(eng, "qk_ready", 2 * s + 2)
                        for m in range(HALVES):
                            for d in range(2):
                                last = nc.tensor.matmul(acc[s % 2][:, m * T:(m + 1) * T],
                                                        kT[:, 2 * s + d, m * P:(m + 1) * P], qT[:, 2 * s + d, :],
                                                        start=(d == 0), stop=(d == 1))
                        last.then_inc(sem("scores_done"), 1)
                    h = s - 1
                    if 0 <= h < RET_HEADS:
                        once(eng, "scores_ready", h + 1)
                        for i in range(HALVES):
                            for m in range(i + 1):
                                last = nc.tensor.matmul(acc[2 + h % 2][:, i * T:(i + 1) * T],
                                                        scores[:, h % 2, m, i * P:(i + 1) * P], ret_view(2, h, m),
                                                        start=(m == 0), stop=(m == i))
                        last.then_inc(sem("ret_out_done"), 1)
                    h = s - 2
                    if h >= 0:
                        if h >= 2:
                            once(eng, "ret_split", h - 1)
                        once(eng, "ret_own", 8 * h + 8)
                        turn(2 * (h % 2), lambda half, part: y_ret[:, h % 2, half, part * P:(part + 1) * P], "y_turned")

        C_EVEN_OUT = dict(n=15, tused=(6, 5), xu=0, xs=4, thi=16, lhs=16, norm=1)

        def out_projection(role, eng, c, w, gain, free, tp_first, need, prev=None):
            def g(k):
                r = residual(c, k, gain)
                r["free"] = free(k) if k < 2 else (x_updated, c["xu"] + k - 1)
                r["need"] = need if k == 0 else None
                if k < 2 and tp_first:
                    r["tp"] = tp_first
                return r

            for k in range(4):
                step(role, eng, g(k), w, 0, k * WIDE, hid, prev)
                prev = g(k)
            return prev

        def even_mixed(pe, j):
            once(pe, "ret_split", min(j + 1, RET_HEADS))
            once(pe, "rw_split", RW_BLOCKS)

        C_MLP0 = dict(n=19, tused=(8, 7), stg=15, hid=0, xu=4, xs=8, thi=32, lhs=32, norm=2)

        C_ODD = after_mlp(C_MLP0, "od_norm")
        ODD_STG, ODD_Z = C_ODD["stg"], 14

        def branch(v):
            k = v % 4

            def move(dve, c, bank):
                return dve.tensor_copy(x_raw[:, 4 * k + 2 * c:4 * k + 2 * c + 2, CONV - 1:],
                                       bank[:, :].rearrange("p (c t) -> p c t", c=2))

            if v < 2:
                free, tp_free = (x_updated, C_ODD["xu"] - 1 + v), (lhs_ready, C_ODD["lhs"])
            else:
                free, tp_free = (stg_written, 2 * (ODD_STG + v - 1)), (z_ready, ODD_Z + 2 * (v - 1))
            if v in (4, 5):
                tp_free = (sem("gates_read"), 4 * LRU_BLOCKS)
            return dict(n=C_ODD["n"] + v, bank=v % 2, post="z", wide=WIDE, free=free, tp=tp_free, move=move,
                        need=(C_ODD["lhs"] - 4, C_ODD["lhs"]) if v == 0 else None, stg=ODD_STG + v, norm=C_ODD["norm"],
                        tused=C_ODD["tused"][v % 2] + v // 2, func=ACT.Gelu_apprx_tanh if v >= 4 else ACT.Copy)

        def branch_step(role, eng, v, prev):
            step(role, eng, branch(v), od_w_in, 0, (D if v < 4 else 0) + (v % 4) * WIDE, xT, prev)

        def prepare_lambda(role, eng):
            src = par[:, COLS["lam"][0]:COLS["lam"][0] + KT]
            a, e, zz, z2, q, out8 = (lam[:, i, :] for i in range(6))
            if role == "dve":
                own = Own(eng, "lambda_own")
                own(eng.tensor_scalar(zz, src, -1.0, None, ALU.mult))
                own(eng.tensor_tensor(a, src, zz, ALU.max))
                own(eng.tensor_scalar(out8, zz, 0.0, None, ALU.max))
                once(eng, "lambda_exp", 1)
                own(eng.tensor_scalar(q, e, 2.0, None, ALU.add))
                own(eng.reciprocal(q, q))
                own(eng.tensor_tensor(zz, e, q, ALU.mult))
                own(eng.tensor_tensor(z2, zz, zz, ALU.mult))
                own(eng.tensor_scalar(q, z2, 1.0 / 15, None, ALU.mult))
                for odd in (13, 11, 9, 7, 5, 3):
                    own(eng.scalar_tensor_tensor(q, q, 1.0 / odd, z2, ALU.add, ALU.mult))
                own(eng.scalar_tensor_tensor(q, q, 1.0, zz, ALU.add, ALU.mult))
                own(eng.scalar_tensor_tensor(out8, q, 2.0, out8, ALU.mult, ALU.add))
                eng.tensor_scalar(out8, out8, -LRU_C, None, ALU.mult).then_inc(sem("lambda_ready"), 1)
            else:
                once(eng, "lambda_own", 2)
                eng.activation(e, a, ACT.Exp, scale=-1.0).then_inc(sem("lambda_exp"), 1)
                once(eng, "lambda_ready", 1)

        def quad(t, i, n=4):
            return t[:, n * i:n * i + n, :]

        def odd_gates(role, eng):
            if role == "pool":
                for n in range(LRU_BLOCKS):
                    if n >= 2:
                        once(eng, "gates_done", n - 1)
                    else:
                        once(eng, "conv_step", 2)
                    for i, w in enumerate((gx_w, ga_w)):
                        eng.dma_start(gate_w[:, n % 2, i, :, :], w[n].rearrange("(i p) j -> p i j", p=P))\
                           .then_inc(sem(f"gate_w_landed{n % 2}"), 16)
            elif role == "dve":
                with eng.Fori(0, LRU_BLOCKS) as n:
                    def view(t, b, off=0):
                        return t[:, bass.ds(2 * n + b, 1), off:off + T].rearrange("p o t -> p (o t)")

                    def tap(j, b):
                        return par[:, bass.ds(COLS["conv_w"][0] + KT * j + 2 * n + b, 1)]

                    for i, j in enumerate(range(CONV - 1, -1, -1)):
                        for b in range(2):
                            if i == 0:
                                ins = eng.tensor_scalar(view(conv, b), view(x_raw, b, j), tap(j, b),
                                                        par[:, bass.ds(COLS["conv_b"][0] + 2 * n + b, 1)], ALU.mult, ALU.add)
                            else:
                                ins = eng.scalar_tensor_tensor(view(conv, b), view(x_raw, b, j), tap(j, b), view(conv, b),
                                                               ALU.mult, ALU.add)
                            ins.then_inc(sem("conv_step"), 1)
                        eng.wait_ge(sem("conv_step"), 8 * n + 2 * i + 2)
            elif role == "pe":
                for n in range(LRU_BLOCKS):
                    once(eng, "conv_step", 8 * n + 8)
                    once(eng, f"gate_w_landed{n % 2}", 32 * (n // 2 + 1))
                    if n >= 2:
                        once(eng, "gates_read", 4 * (n - 1))
                    for i in range(2):
                        for jh in range(2):
                            for ih in range(2):
                                last = nc.tensor.matmul(tp[2 * (n % 2) + i][:, jh * T:(jh + 1) * T],
                                                        gate_w[:, n % 2, i, ih, jh * P:(jh + 1) * P],
                                                        conv[:, 2 * n + ih, :], start=(ih == 0), stop=(ih == 1))
                    last.then_inc(sem("gates_done"), 1)
            elif role == "act":
                for n in range(LRU_BLOCKS):
                    once(eng, "gates_done", n + 1)
                    for i, (t, bias) in enumerate(((gate_x, "gx_b"), (gate_a, "ga_b"))):
                        for jh in range(2):
                            eng.activation(t[:, 2 * n + jh, :], tp[2 * (n % 2) + i][:, jh * T:(jh + 1) * T], ACT.Sigmoid,
                                           bias=pcol(bias, 2 * n + jh)).then_inc(sem("gates_read"), 1)

        def odd_recurrence(role, eng):
            if role == "act":
                for j in range(UNITS):
                    split_hi(eng, branch(4)["n"], j)
                    once(eng, "bx_ready", j // 2 + 1)
                    for kt in (2 * j, 2 * j + 1):
                        eng.activation(conv[:, kt, :], gate_a[:, kt, :], ACT.Exp, scale=lam[:, 5, kt:kt + 1])\
                           .then_inc(sem("decays_ready"), 1)
                        eng.activation(gate_t[:, kt, :], gate_a[:, kt, :], ACT.Tanh, scale=lam[:, 5, kt:kt + 1])\
                           .then_inc(sem("tangents_ready"), 1)
                for j in range(UNITS):
                    split_hi(eng, branch(5)["n"], j)
                    if j == 2:
                        act_evacuate(eng, branch(4))
                    if j >= 4:
                        once(eng, "root_in", j - 3)
                        eng.activation(quad(gate_t, j - 4), quad(gate_t, j - 4), ACT.Sqrt).then_inc(sem("roots_ready"), 1)
            elif role == "dve":
                own = Own(eng, "odd_own")
                for j in range(UNITS):
                    split_lo(eng, branch(4)["n"], j)
                    i = j % 4
                    if j < 4:
                        once(eng, "gates_read", 4 * LRU_BLOCKS)
                        eng.tensor_tensor(quad(gate_x, i), quad(gate_x, i), quad(conv, i), ALU.mult)\
                           .then_inc(sem("bx_ready"), 1)
                    else:
                        once(eng, "tangents_ready", 4 * i + 4)
                        own(eng.tensor_scalar(quad(gate_a, i), quad(gate_t, i), -1.0, 1.0, ALU.mult, ALU.add))
                        own(eng.reciprocal(quad(gate_a, i), quad(gate_a, i)))
                        eng.scalar_tensor_tensor(quad(gate_t, i), quad(gate_t, i), -2.0, quad(gate_a, i),
                                                 ALU.mult, ALU.mult).then_inc(sem("root_in"), 1)
                own(eng.memset(conv[:, :, 0:1], 0.0))
                for j in range(UNITS):
                    split_lo(eng, branch(5)["n"], j)
                    if j == 5:
                        dve_after_transpose(eng, branch(4))
                    if j >= 4:
                        i = j - 4
                        once(eng, "roots_ready", i + 1)
                        own(eng.tensor_tensor(quad(gate_x, i), quad(gate_x, i), quad(gate_t, i), ALU.mult))
                        flat = lambda t: quad(t, i).rearrange("p c t -> p (c t)")
                        own(eng.tensor_tensor_scan(flat(gate_t), flat(conv), flat(gate_x), 0.0, ALU.mult, ALU.add))
            else:
                branch_step(role, eng, 4, None)
                branch_step(role, eng, 5, branch(4))

        def odd_product(role, eng, i):
            for c in (2 * i, 2 * i + 1):
                hi, lo = (hidA_hi, hidA_lo) if c < 4 else (hidB_hi, hidB_lo)
                k = (2 * c) % 8
                if role == "dve":
                    once(eng, "z_ready", ODD_Z + 8 + 2 * (i + 1))
                    eng.tensor_tensor(quad(gate_t, c, 2), quad(gate_t, c, 2), x_raw[:, 2 * c:2 * c + 2, CONV - 1:],
                                      ALU.mult).then_inc(sem("odd_mixed"), 1)
                elif role == "act":
                    once(eng, "odd_mixed", c + 1)
                    eng.activation(hi[:, k:k + 2, :], quad(gate_t, c, 2), ACT.Copy).then_inc(sem("odd_hi"), 1)
            for c in (2 * i, 2 * i + 1):
                hi, lo = (hidA_hi, hidA_lo) if c < 4 else (hidB_hi, hidB_lo)
                k = (2 * c) % 8
                if role == "dve":
                    once(eng, "odd_hi", c + 1)
                    eng.tensor_tensor(lo[:, k:k + 2, :], quad(gate_t, c, 2), hi[:, k:k + 2, :], ALU.subtract)\
                       .then_inc(sem("odd_split"), 1)

        C_ODD_OUT = dict(C_ODD, n=C_ODD["n"] + 8, tused=[t + 4 for t in C_ODD["tused"]])
        C_MLP1 = dict(n=C_ODD["n"] + 12, tused=[t + 6 for t in C_ODD["tused"]], stg=C_ODD["stg"] + 8, hid=C_ODD["hid"],
                      xu=C_ODD["xu"] + 4, xs=C_ODD["xs"] + 4, thi=C_ODD["thi"] + 16, lhs=C_ODD["lhs"] + 16,
                      norm=C_ODD["norm"] + 1)
        C_END = after_mlp(C_MLP1, None)

        def odd_layer(role, eng, prev):
            for v in range(4):
                branch_step(role, eng, v, prev)
                prev = branch(v)
            finish(role, eng, prev)
            if role == "dve":
                eng.memset(x_raw[:, :, 0:CONV - 1], 0.0).then_inc(sem("odd_zeroed"), 1)
                once(eng, "odd_zeroed", 1)
                once(eng, "z_ready", ODD_Z + 8)
            odd_gates(role, eng)
            odd_recurrence(role, eng)
            branch_step(role, eng, 6, branch(5))
            odd_product(role, eng, 0)
            branch_step(role, eng, 7, branch(6))
            odd_product(role, eng, 1)
            finish(role, eng, branch(7))
            odd_product(role, eng, 2)
            odd_product(role, eng, 3)
            return out_projection(role, eng, C_ODD_OUT, od_w_out, "ff_norm1",
                                  free=lambda k: (stg_written, 2 * (ODD_STG + 7 + k)), tp_first=(z_ready, ODD_Z + 16),
                                  need=lambda pe, j: once(pe, "odd_split", j + 1))

        tables_landed = sem("tables_landed")
        out_ready, out_stored = sem("out_ready"), sem("out_stored")
        gain_landed = sem("gain_landed")
        gain_row = stg[:, :, :, :].rearrange("p a h n -> p (a h n)")

        def program(role, eng):
            posts = load_posts("ev_norm")
            for p in posts[:-1]:
                finish(role, eng, p)
            even_in(role, eng, posts[-1])
            rwkv(role, eng)
            retention(role, eng)
            prev = out_projection(role, eng, C_EVEN_OUT, ev_w_out, "ff_norm0", free=lambda k: None, tp_first=None,
                                  need=even_mixed)
            prev = mlp(role, eng, 0, C_MLP0, prev, "od_norm")
            prev = odd_layer(role, eng, prev)
            prev = mlp(role, eng, 1, C_MLP1, prev, None)
            finish(role, eng, prev)

        block = ctx.enter_context(nc.Block())

        @block.sync
        def _(sp):
            for dst, src in ((con[:, :], consts), (par[:, :], params)):
                sp.dma_start(dst, src).then_inc(tables_landed, 16)
            for h in range(HALVES):
                sp.dma_start(x[:, h, :], x_in[h * P:(h + 1) * P, :]).then_inc(x_landed, 16)
            program("sp", sp)
            sp.wait_ge(squared, C_END["hid"])
            sp.wait_ge(t_done[0], C_END["tused"][0])
            sp.wait_ge(t_done[1], C_END["tused"][1])
            sp.dma_start(gain_row, final_norm.rearrange("(a n) -> a n", a=1).broadcast_to((P, D))).then_inc(gain_landed, 16)
            for k in range(4):
                for h in range(HALVES):
                    sp.wait_ge(out_ready, HALVES * k + h + 1)
                    sp.dma_start(out[h * P:(h + 1) * P, k * WIDE:(k + 1) * WIDE],
                                 x[:, h, k * WIDE:(k + 1) * WIDE]).then_inc(out_stored, 16)
            sp.wait_ge(out_stored, 16 * 4 * HALVES)

        @block.gpsimd
        def _(pool):
            program("pool", pool)

        @block.scalar
        def _(act):
            act.wait_ge(tables_landed, 32)
            prepare_lambda("act", act)
            program("act", act)

        @block.vector
        def _(dve):
            rwkv_zero(dve)
            dve.wait_ge(tables_landed, 32)
            prepare_lambda("dve", dve)
            program("dve", dve)
            dve.wait_ge(rstd_ready, C_END["norm"])
            dve.wait_ge(gain_landed, 16)
            for k in range(4):
                for h in range(HALVES):
                    xs = x[:, h, k * WIDE:(k + 1) * WIDE]
                    dve.scalar_tensor_tensor(xs, xs, rstd[:, h:h + 1], gain_row[:, k * WIDE:(k + 1) * WIDE],
                                             ALU.mult, ALU.mult).then_inc(out_ready, 1)

        @block.tensor
        def _(pe):
            pe.wait_ge(tables_landed, 32)
            program("pe", pe)


def const_table():
    import numpy as np
    i = np.arange(P)
    same = (i[:, None] // CHUNK) == (i[None, :] // CHUNK)
    t = i % CHUNK
    cols = [np.eye(P), same]
    for l in range(LEVELS):
        cols.append(same & ((t[:, None] >> (l + 1)) == (t[None, :] >> (l + 1))) & (((t[:, None] >> l) & 1) == 1)
                    & (((t[None, :] >> l) & 1) == 0))
    cols.append(same & (t[None, :] > t[:, None]))
    cols.append(np.arange(CHUNK)[None, :] >= t[:, None])
    cols.append(np.broadcast_to(np.arange(T)[None, :] % CHUNK != 0, (P, T)))
    return np.concatenate([np.asarray(c, np.float32) for c in cols], axis=1)


def position_tables():
    import numpy as np
    half = 128
    inv = 1.0 / (np.float32(10000.0) ** (np.arange(0, 2 * half, 2, dtype=np.float32) / np.float32(2 * half)))
    ang = (np.arange(T, dtype=np.float32)[:, None] * inv.astype(np.float32)[None, :]).astype(np.float32)
    cossin = np.stack([np.cos(ang), np.sin(ang)], axis=1).astype(np.float32)
    lg = np.log1p(-np.exp2(-5.0 - np.arange(RET_HEADS, dtype=np.float64)))
    n, m = np.arange(T)[None, :], np.arange(T)[:, None]
    seen = (m // CHUNK) <= (n // CHUNK)
    decay = np.where(seen[None], np.exp(lg[:, None, None] * np.abs(n - m)[None]), 0.0) / 16.0
    return cossin, decay.astype(np.float32)


def kernel(**inputs):
    import numpy as np
    import concourse.bacc as bacc
    from concourse.bass_utils import run_bass_kernel_spmd

    a = {k: np.ascontiguousarray(v) for k, v in inputs.items()}

    def blocks(v, n):
        flat = np.zeros((n, P), np.float32)
        flat.reshape(-1)[:v.size] = v.reshape(-1)
        return flat.T

    table = dict(mu=a["rw_mu"], w0=a["rw_w0"], a0=a["rw_a0"], k_k=a["rw_k_k"], k_a=a["rw_k_a"], r_k=a["rw_r_k"],
                 lnx_w=a["rw_lnx_w"], lnx_b=a["rw_lnx_b"], ev_norm=a["ev_norm"], ff_norm0=a["ff_norm"][0],
                 od_norm=a["od_norm"], ff_norm1=a["ff_norm"][1], conv_w=a["od_conv_w"], conv_b=a["od_conv_b"],
                 gx_b=a["od_gx_b"], ga_b=a["od_ga_b"], lam=a["od_lam"])
    params = np.ascontiguousarray(np.concatenate([blocks(table[k], n) for k, (_, n) in COLS.items()], axis=1))
    cossin, rdecay = position_tables()
    arrays = {
        "x_in": a["x"][0], "params": params, "consts": const_table(), "cossin": cossin, "rdecay": rdecay,
        "ev_w_in": a["ev_w_in"][0], "ev_w_out": a["ev_w_out"][0], "rw_w2": a["rw_w2"][0], "rw_a2": a["rw_a2"][0],
        "rw_g2": a["rw_g2"][0], "od_w_in": a["od_w_in"][0], "gx_w": a["od_gx_w"][0], "ga_w": a["od_ga_w"][0],
        "od_w_out": a["od_w_out"][0], "ff_w1": a["ff_w1"], "ff_w2": a["ff_w2"], "final_norm": a["final_norm"],
    }
    nc = bacc.Bacc("TRN2", target_bir_lowering=False, num_devices=1)
    args = {k: nc.dram_tensor(f"in_{k}", v.shape, mybir.dt.from_np(v.dtype), kind="ExternalInput").ap()
            for k, v in arrays.items()}
    out = nc.dram_tensor("out", (T, D), F32, kind="ExternalOutput").ap()
    trunk(nc, **args, out=out)
    r = run_bass_kernel_spmd(nc, [{f"in_{k}": v for k, v in arrays.items()}], core_ids=[0])
    return r.results[0]["out"].reshape(1, T, D)
```

```python
from contextlib import ExitStack

import concourse.bass as bass
from concourse import mybir

ALU = mybir.AluOpType
ACT = mybir.ActivationFunctionType
AX_X = mybir.AxisListType.X
F32 = mybir.dt.float32
F32R = mybir.dt.float32r

P = 128
T = 256
HALVES = T // P
D = 2048
KT = D // P
WIDE = 512
UNITS = 8
KU = KT // UNITS
RING = 4
CHUNK = 64
NCHUNK = T // CHUNK
RET_W = 1024
RET_HEADS = 4
RW_BLOCKS = 8
LEVELS = 6
CONV = 4
SLAB = 212832
LORA_W = 288
FF = 8192
QUARTERS = FF // D
NORM_EPS = 1e-6
RET_EPS = 1e-5
RW_EPS = 64e-5
DECAY_C = 0.6065306597126334
LRU_C = 8.0
LRU_BLOCKS = 8

COLS = {}
for _name, _n in (("mu", 27), ("w0", 8), ("a0", 8), ("k_k", 8), ("k_a", 8), ("r_k", 8), ("lnx_w", 8), ("lnx_b", 8),
                  ("ev_norm", 16), ("ff_norm0", 16), ("od_norm", 16), ("ff_norm1", 16), ("conv_w", 64),
                  ("conv_b", 16), ("gx_b", 16), ("ga_b", 16), ("lam", 16)):
    COLS[_name] = (sum(n for _, n in COLS.values()), _n)
NPAR = sum(n for _, n in COLS.values())
CIDENT, CONES, CLEVEL, CSTRICT, CINCL, CSEG = 0, 128, 256, 256 + 128 * LEVELS, 384 + 128 * LEVELS, 448 + 128 * LEVELS
NCONST = CSEG + 256


def trunk(nc, x_in, params, consts, cossin, rdecay, ev_w_in, ev_w_out, rw_w2, rw_a2, rw_g2, od_w_in, gx_w, ga_w,
          od_w_out, ff_w1, ff_w2, final_norm, out):
    ctx = ExitStack()
    with ctx:
        def sb(name, shape, dt=F32, scope=ctx):
            return scope.enter_context(nc.sbuf_tensor(name, shape, dt))

        sems = {}

        def sem(name):
            if name not in sems:
                sems[name] = ctx.enter_context(nc.semaphore(name))
            return sems[name]

        def nbytes(shape):
            n = 4
            for v in shape[1:]:
                n *= v
            return -(-n // 32) * 32

        slab_start = -(-nc.sbuf_base // 32) * 32
        slab = sb("slab", [P, SLAB // 4])

        class Region:
            def __init__(self, at):
                self.at = at

            def __call__(self, name, shape, dt=F32):
                t = nc.alloc_sbuf_tensor_at(name, shape, dt, offset=slab_start + self.at)
                self.at += nbytes(shape)
                assert self.at <= SLAB, (name, self.at)
                return t

        lasting = Region(0)
        x = lasting("x", [P, HALVES, D])
        xT_hi = lasting("xT_hi", [P, KT, T], F32R)
        xT_lo = lasting("xT_lo", [P, KT, T], F32R)
        raw = lasting("raw", [P, RING, KU, WIDE])
        w_hi = lasting("w_hi", [P, RING, KU, WIDE], F32R)
        w_lo = lasting("w_lo", [P, RING, KU, WIDE], F32R)
        par = lasting("par", [P, NPAR])
        con = lasting("con", [P, NCONST])
        ssq = lasting("ssq", [P, 4, HALVES])
        rstd = lasting("rstd", [P, HALVES])
        lam = lasting("lam", [P, 6, KT])
        stg = lasting("stg", [P, 2, HALVES, WIDE])
        junk = lasting("junk", [P, WIDE])
        ident = con[:, CIDENT:CIDENT + P]
        HALF = KT // 2 * T * 4

        low = lasting.at
        at_a = Region(low)
        hidA_hi, hidA_lo = (at_a(n, [P, KT // 2, T], F32R) for n in ("hidA_hi", "hidA_lo"))
        at_b = Region(low + 4 * HALF)
        hidB_hi, hidB_lo = (at_b(n, [P, KT // 2, T], F32R) for n in ("hidB_hi", "hidB_lo"))
        early = Region(low)
        ret_tok = early("ret_tok", [P, 8, HALVES, WIDE])
        z = early("z", [P, 3 * RW_BLOCKS, T])
        rw = Region(early.at)
        lora_in = rw("lora_in", [P, 4, T])
        lora_w = rw("lora_w", [P, 3, P])
        half_bias = rw("half_bias", [P, 2, RW_BLOCKS])

        def diagonal(name):
            return rw(name, [P, NCHUNK, P])

        v_bd, beta_bd, key_bd, kappa_bd = (diagonal(n) for n in ("v_bd", "beta_bd", "key_bd", "kappa_bd"))
        v_tok, key_tok, beta_tok = (diagonal(n) for n in ("v_tok", "key_tok", "beta_tok"))
        level_a, inv_t, seen_v = (diagonal(n) for n in ("level_a", "inv_t", "seen_v"))
        seen_y = rw("seen_y", [P, 2, NCHUNK, CHUNK])
        state = rw("state", [P, 2, P])
        scaled, rhs_u, u_bd = (rw(n, [P, P]) for n in ("scaled", "rhs_u", "u_bd"))
        decay = rw("decay", [P, NCHUNK, CHUNK + 1])
        decay_end = rw("decay_end", [P, NCHUNK])
        extra = rw("extra", [P, 4, T])
        rt = Region(early.at)
        qT, kT = rt("qT", [P, 8, T]), rt("kT", [P, 8, T])
        table_d = rt("table_d", [P, 2, HALVES, T])
        table_cs = rt("table_cs", [P, HALVES, 2, P])
        rot_q, rot_k = (rt(n, [P, 4, HALVES, P]) for n in ("rot_q", "rot_k"))
        scores, y_ret = (rt(n, [P, 2, HALVES, T]) for n in ("scores", "y_ret"))
        rstat, rmean, rdev = rt("rstat", [P, HALVES, 6]), rt("rmean", [P, HALVES, 2]), rt("rdev", [P, HALVES])
        od_a = Region(low)
        gate_a = od_a("gate_a", [P, KT, T])
        od_b = Region(low + 4 * HALF)
        gate_x = od_b("gate_x", [P, KT, T])
        x_rest = Region(low + 2 * HALF)
        conv = x_rest("conv", [P, KT, T])
        x_raw = od_b("x_raw", [P, KT, T + CONV - 1])
        gate_w = od_b("gate_w", [P, 2, 2, 2, T])
        gate_t = od_b("gate_t", [P, KT, T])

        acc = [ctx.enter_context(nc.psum_tensor(f"acc{i}", [P, WIDE], F32)) for i in range(4)]
        tp = [ctx.enter_context(nc.psum_tensor(f"tp{i}", [P, WIDE], F32)) for i in range(4)]

        def pcol(name, k):
            return par[:, COLS[name][0] + k:COLS[name][0] + k + 1]

        def xT(kt):
            return xT_hi[:, kt, :], xT_lo[:, kt, :]

        def hid(kt):
            a, b = (hidA_hi, hidA_lo) if kt < KT // 2 else (hidB_hi, hidB_lo)
            return a[:, kt % (KT // 2), :], b[:, kt % (KT // 2), :]

        raw_landed = [sem(f"raw_landed{i}") for i in range(RING)]
        hi_ready, lo_ready, unit_used = sem("hi_ready"), sem("lo_ready"), sem("unit_used")
        t_done = [sem("t_done0"), sem("t_done1")]
        x_landed, x_updated, ssq_done = sem("x_landed"), sem("x_updated"), sem("ssq_done")
        stg_written, squared, t_hi, lhs_ready, z_ready = (sem("stg_written"), sem("squared"), sem("t_hi"),
                                                         sem("lhs_ready"), sem("z_ready"))
        var_ready, std_ready, rstd_ready = sem("var_ready"), sem("std_ready"), sem("rstd_ready")

        def wait_count(eng, s, value):
            if not isinstance(value, int) or value > 0:
                eng.wait_ge(s, value)

        def load_unit(sp, n, j, w, row0, col0, wide=WIDE):
            wait_count(sp, lo_ready, 8 * n + j - RING + 1)
            src = w[bass.ds(row0 + j * KU * P, KU * P), bass.ds(col0, wide)].rearrange("(k p) n -> p k n", p=P)
            sp.dma_start(raw[:, j % RING, :, 0:wide], src).then_inc(raw_landed[j % RING], 16)

        def split_hi(act, n, j, wide=WIDE):
            act.wait_ge(raw_landed[j % RING], 16 * (2 * n + j // RING + 1))
            wait_count(act, unit_used, 8 * n + j - RING + 1)
            act.activation(w_hi[:, j % RING, :, 0:wide], raw[:, j % RING, :, 0:wide], ACT.Copy).then_inc(hi_ready, 1)

        def split_lo(dve, n, j, wide=WIDE):
            dve.wait_ge(hi_ready, 8 * n + j + 1)
            dve.tensor_tensor(w_lo[:, j % RING, :, 0:wide], raw[:, j % RING, :, 0:wide],
                              w_hi[:, j % RING, :, 0:wide], ALU.subtract).then_inc(lo_ready, 1)

        def multiply_part(pe, n, part, lhs, bank, wide=WIDE):
            j, kt, h = part // 4, part // 2, part % 2
            if part % 4 == 0:
                pe.wait_ge(lo_ready, 8 * n + j + 1)
            hi, lo = lhs(kt)
            o, tok = acc[2 * bank + h][:, 0:wide], slice(h * P, (h + 1) * P)
            wh, wl = w_hi[:, j % RING, kt % KU, 0:wide], w_lo[:, j % RING, kt % KU, 0:wide]
            nc.tensor.matmul(o, hi[:, tok], wh, start=(kt == 0), stop=False)
            nc.tensor.matmul(o, hi[:, tok], wl, start=False, stop=False)
            last = nc.tensor.matmul(o, lo[:, tok], wh, start=False, stop=(kt == KT - 1))
            if part % 4 == 3:
                last.then_inc(unit_used, 1)

        def multiply_unit(pe, n, j, lhs, bank, wide=WIDE):
            for part in range(4 * j, 4 * j + 4):
                multiply_part(pe, n, part, lhs, bank, wide)

        def sp_group(sp, g, w, row0, col0, side=None):
            for j in range(UNITS):
                load_unit(sp, g["n"], j, w, row0, col0, g["wide"])
                if side:
                    side("sp", sp, j)

        def pe_group(pe, g, lhs, prev=None, side=None):
            if g["free"]:
                pe.wait_ge(*g["free"])
            for j in range(UNITS):
                if j == 2 and prev:
                    pe_post(pe, prev)
                if callable(g["need"]):
                    g["need"](pe, j)
                elif g["need"] is not None and j in (0, 6):
                    pe.wait_ge(lhs_ready, g["need"][j // 6])
                multiply_unit(pe, g["n"], j, lhs, g["bank"], g["wide"])
                if side:
                    side("pe", pe, j)

        def act_group(act, g, prev=None, side=None):
            for j in range(UNITS):
                split_hi(act, g["n"], j, g["wide"])
                if j == 2 and prev:
                    act_evacuate(act, prev)
                if j == 5 and prev:
                    act_after_transpose(act, prev)
                if side:
                    side("act", act, j)

        def dve_group(dve, g, prev=None, side=None):
            for j in range(UNITS):
                split_lo(dve, g["n"], j, g["wide"])
                if j == 2 and prev:
                    dve_evacuate(dve, prev)
                if j == 5 and prev:
                    dve_after_transpose(dve, prev)
                if j == 7 and prev:
                    dve_finish_norm(dve, prev)
                if side:
                    side("dve", dve, j)

        def act_evacuate(act, g):
            if g["post"] in ("square", "z"):
                act.wait_ge(unit_used, 8 * (g["n"] + 1))
                act.wait_ge(rstd_ready, g["norm"])
                wait_count(act, t_done[g["bank"]], g["tused"])
                for h in range(HALVES):
                    last = act.activation(stg[:, g["bank"], h, 0:g["wide"]], acc[2 * g["bank"] + h][:, 0:g["wide"]],
                                          g.get("func", ACT.Relu if g["post"] == "square" else ACT.Copy),
                                          scale=rstd[:, h:h + 1])
                    last.then_inc(stg_written, 1)

        def pool_square(pool, g):
            pool.wait_ge(stg_written, 2 * g["stg"] + 2)
            s = stg[:, g["bank"], :, :]
            pool.tensor_tensor(s, s, s, ALU.mult).then_inc(squared, 1)

        def pe_post(pe, g):
            b = g["bank"]
            if g["post"] == "x":
                if not g["transposed"]:
                    return
                if g.get("loaded"):
                    pe.wait_ge(x_landed, 32)
                else:
                    pe.wait_ge(x_updated, g["xu"] + 1)
                src = lambda h, c: x[:, h, g["col"] + c * P:g["col"] + (c + 1) * P]
            else:
                if g["post"] == "square":
                    pe.wait_ge(squared, g["hid"] + 1)
                else:
                    pe.wait_ge(stg_written, 2 * g["stg"] + 2)
                src = lambda h, c: stg[:, b, h, c * P:min((c + 1) * P, g["wide"])]
            if g["tp"]:
                pe.wait_ge(*g["tp"])
            for c in range(-(-g["wide"] // P)):
                for h in range(HALVES):
                    s = src(h, c)
                    last = nc.tensor.transpose(tp[2 * b + c // 2][0:s.shape[1], (c % 2) * T + h * P:(c % 2) * T + (h + 1) * P],
                                               s, ident)
            last.then_inc(t_done[b], 1)

        def act_after_transpose(act, g):
            b = g["bank"]
            if g["post"] == "x" and g.get("summed", True):
                for h in range(HALVES):
                    if g.get("loaded"):
                        act.wait_ge(x_landed, 32)
                    else:
                        act.wait_ge(x_updated, g["xu"] + 1)
                    wait_count(act, ssq_done, HALVES * g["xs"] + h)
                    act.activation(junk[:, :], x[:, h, g["col"]:g["col"] + WIDE], ACT.Square,
                                   accum_out=ssq[:, g["col"] // WIDE, h:h + 1]).then_inc(ssq_done, 1)
                if g["transposed"]:
                    act.wait_ge(t_done[b], g["tused"] + 1)
                    for c in range(4):
                        kt = g["col"] // P + c
                        act.activation(xT_hi[:, kt, :], tp[2 * b + c // 2][:, (c % 2) * T:(c % 2 + 1) * T], ACT.Copy,
                                       scale=pcol(g["gain"], kt)).then_inc(t_hi, 1)
                if g["col"] == 3 * WIDE and g.get("summed", True):
                    act.wait_ge(var_ready, 2 * g["norm"])
                    act.activation(rstd[:, :], rstd[:, :], ACT.Sqrt).then_inc(std_ready, 1)
            if g["post"] == "square":
                act.wait_ge(t_done[b], g["tused"] + 1)
                for c in range(2):
                    t = (hidA_hi if g["g"] < 2 else hidB_hi)[:, (4 * g["g"] + 2 * c) % 8:(4 * g["g"] + 2 * c) % 8 + 2, :]
                    act.activation(t, tp[2 * b + c][:, :].rearrange("p (c t) -> p c t", c=2), ACT.Copy).then_inc(t_hi, 1)

        def dve_evacuate(dve, g):
            if g["post"] == "x" and not g.get("loaded"):
                dve.wait_ge(unit_used, 8 * (g["n"] + 1))
                for h in range(HALVES):
                    xs = x[:, h, g["col"]:g["col"] + WIDE]
                    last = dve.tensor_tensor(xs, acc[2 * g["bank"] + h][:, :], xs, ALU.add)
                last.then_inc(x_updated, 1)

        def dve_after_transpose(dve, g):
            b = g["bank"]
            if g["post"] == "x":
                if g["transposed"]:
                    for c in range(4):
                        kt = g["col"] // P + c
                        dve.wait_ge(t_hi, g["thi"] + 2 * (c // 2) + 2)
                        last = dve.scalar_tensor_tensor(xT_lo[:, kt, :], tp[2 * b + c // 2][:, (c % 2) * T:(c % 2 + 1) * T],
                                                        pcol(g["gain"], kt), xT_hi[:, kt, :], ALU.mult, ALU.subtract)
                        last.then_inc(lhs_ready, 1)
                if g["col"] == 3 * WIDE and g.get("summed", True):
                    dve.wait_ge(ssq_done, HALVES * (g["xs"] + 1))
                    dve.tensor_reduce(rstd[:, :], ssq[:, :, :].rearrange("p g h -> p h g"), AX_X, ALU.add).then_inc(var_ready, 1)
                    dve.wait_ge(var_ready, 2 * g["norm"] - 1)
                    dve.tensor_scalar(rstd[:, :], rstd[:, :], 1.0 / D, NORM_EPS, ALU.mult, ALU.add).then_inc(var_ready, 1)
            if g["post"] == "square":
                for c in range(2):
                    k = (4 * g["g"] + 2 * c) % 8
                    a, l = (hidA_hi, hidA_lo) if g["g"] < 2 else (hidB_hi, hidB_lo)
                    dve.wait_ge(t_hi, g["thi"] + c + 1)
                    dve.tensor_tensor(l[:, k:k + 2, :], tp[2 * b + c][:, :].rearrange("p (c t) -> p c t", c=2),
                                      a[:, k:k + 2, :], ALU.subtract).then_inc(lhs_ready, 1)
            if g["post"] == "z":
                for c in range(-(-g["wide"] // (2 * P))):
                    dve.wait_ge(t_done[b], g["tused"] + 1)
                    g["move"](dve, c, tp[2 * b + c]).then_inc(z_ready, 1)

        def dve_finish_norm(dve, g):
            if g["post"] == "x" and g["col"] == 3 * WIDE and g.get("summed", True):
                dve.wait_ge(std_ready, g["norm"])
                dve.reciprocal(rstd[:, :], rstd[:, :]).then_inc(rstd_ready, 1)

        def step(role, eng, g, w, row0, col0, lhs, prev, side=None):
            if role == "sp":
                sp_group(eng, g, w, row0, col0, side)
            elif role == "pe":
                pe_group(eng, g, lhs, prev, side)
            elif role == "act":
                act_group(eng, g, prev, side)
            elif role == "dve":
                dve_group(eng, g, prev, side)
            elif prev and prev["post"] == "square":
                pool_square(eng, prev)

        def finish(role, eng, prev):
            if role == "pe":
                pe_post(eng, prev)
            elif role == "act":
                act_evacuate(eng, prev)
                act_after_transpose(eng, prev)
            elif role == "dve":
                dve_evacuate(eng, prev)
                dve_after_transpose(eng, prev)
                dve_finish_norm(eng, prev)
            elif role == "pool" and prev["post"] == "square":
                pool_square(eng, prev)

        def load_posts(gain):
            return [dict(post="x", loaded=True, transposed=True, gain=gain, col=k * WIDE, bank=k % 2, wide=WIDE,
                         tused=k // 2, tp=(lhs_ready, 4 * (k - 1)) if k > 1 else None, xu=0, xs=k, thi=4 * k,
                         lhs=4 * k, norm=1) for k in range(4)]

        def residual(c, k, gain, q=0, last=True):
            return dict(n=c["n"] + k, bank=k % 2, post="x", col=k * WIDE, transposed=last and gain is not None, gain=gain,
                        summed=last, wide=WIDE, tused=c["tused"][k % 2] + k // 2, xu=c["xu"] + k, xs=c["xs"] + k,
                        thi=c["thi"] + 4 * k, lhs=c["lhs"] + 4 * k, tp=(lhs_ready, c["lhs"] + 4 * max(k - 1, 0)),
                        norm=c["norm"] + 1)

        def mlp_group(c, q, g, gain):
            n, lhs0 = c["n"] + 8 * q, c["lhs"] + 8 * q
            if g < 4:
                free = (x_updated, c["xu"] + 4 * (q - 1) + g + 3) if g < 2 else (stg_written, 2 * (c["stg"] + 4 * q + g - 1))
                return dict(n=n + g, bank=g % 2, post="square", g=g, wide=WIDE, free=free, need=(c["lhs"] - 4, c["lhs"]),
                            tused=c["tused"][g % 2] + 2 * q + g // 2, stg=c["stg"] + 4 * q + g, hid=c["hid"] + 4 * q + g,
                            thi=c["thi"] + 8 * q + 2 * g, lhs=lhs0 + 2 * g, tp=(lhs_ready, lhs0 + 2 * max(g - 1, 0)),
                            norm=c["norm"])
            k, last = g - 4, isinstance(q, int) and q == QUARTERS - 1
            at = dict(n=n + 4, tused=[t + 2 * q + 2 for t in c["tused"]], xu=c["xu"] + 4 * q, xs=c["xs"], thi=c["thi"] + 8 * q + 8,
                      lhs=lhs0 + 8, norm=c["norm"])
            r = residual(at, k, gain, last=last)
            r["free"] = (stg_written, 2 * (c["stg"] + 4 * q + g - 1)) if k < 2 else (x_updated, at["xu"] + k - 1)
            r["need"] = (lhs0 + 6, lhs0 + 8)
            return r

        def mlp(role, eng, layer, c, prev, gain):
            w1, w2 = ff_w1[layer], ff_w2[layer]

            def part(q, g, prev):
                if g < 4:
                    step(role, eng, mlp_group(c, q, g, gain), w1, 0, q * D + g * WIDE, xT, prev)
                else:
                    step(role, eng, mlp_group(c, q, g, gain), w2, q * D, (g - 4) * WIDE, hid, prev)

            part(0, 0, prev)
            with eng.Fori(0, QUARTERS - 1) as q:
                for g in range(1, 8):
                    part(q, g, mlp_group(c, q, g - 1, gain))
                part(q + 1, 0, mlp_group(c, q, 7, gain))
            for g in range(1, 8):
                part(QUARTERS - 1, g, mlp_group(c, QUARTERS - 1, g - 1, gain))
            return mlp_group(c, QUARTERS - 1, 7, gain)

        def after_mlp(c, gain):
            t = 4 if gain else 0
            return dict(n=c["n"] + 32, tused=[v + 8 + t // 2 for v in c["tused"]], stg=c["stg"] + 16, hid=c["hid"] + 16,
                        xu=c["xu"] + 16, xs=c["xs"] + 4, thi=c["thi"] + 32 + 4 * t, lhs=c["lhs"] + 32 + 4 * t,
                        norm=c["norm"] + 1)

        z_lora = extra

        def tile(t, i):
            return t[:, i // 4, (i // 2) % 2, (i % 2) * T:(i % 2 + 1) * T]

        out_t, cen_t, csq_t, kk_t, b_t, km_t, sq_t, nrm_t = (tile(stg, i) for i in range(8))
        rho_t, em_t = junk[:, 0:T], junk[:, T:2 * T]
        thw_t, sum_t, iclr_t, bon_t = (extra[:, i, :] for i in range(4))

        def lora_move(dve, c, bank):
            if c == 0:
                return dve.tensor_copy(z_lora[:, 0:2, :], bank[:, :].rearrange("p (c t) -> p c t", c=2))
            return dve.tensor_copy(z_lora[0:32, 2, :], bank[0:32, 0:T])

        LORA = dict(n=0, bank=0, post="z", wide=LORA_W, free=None, need=(12, 16), tused=2, stg=0, norm=1,
                    tp=(lhs_ready, 16), move=lora_move)

        def rkv(i, odd):
            v = 2 * i + odd

            def move(dve, c, bank):
                return dve.tensor_copy(z[:, bass.ds(4 * v + 2 * c, 2), :], bank[:, :].rearrange("p (c t) -> p c t", c=2))

            return dict(n=1 + v, bank=1 - odd, post="z", wide=WIDE, need=None, stg=1 + v, norm=1, move=move,
                        free=None if isinstance(v, int) and v == 0 else (stg_written, 2 * v), tused=2 + odd + i,
                        tp=(z_ready, 2 * v + 2))

        RET_IN = 4 * RET_W

        def even_in(role, eng, prev):
            step(role, eng, LORA, ev_w_in, 0, RET_IN + 3 * RET_W, xT, prev)
            step(role, eng, rkv(0, 0), ev_w_in, 0, RET_IN, xT, LORA)
            with eng.Fori(0, 2) as i:
                step(role, eng, rkv(i, 1), ev_w_in, 0, RET_IN + (2 * i + 1) * WIDE, xT, rkv(i, 0))
                step(role, eng, rkv(i + 1, 0), ev_w_in, 0, RET_IN + (2 * i + 2) * WIDE, xT, rkv(i, 1))
            step(role, eng, rkv(2, 1), ev_w_in, 0, RET_IN + 5 * WIDE, xT, rkv(2, 0))
            finish(role, eng, rkv(2, 1))

        RET_N, RET_STG = 7, 7

        def once(eng, name, count):
            eng.wait_ge(sem(name), count)

        class Own:

            def __init__(self, eng, name, it=0, per=0):
                self.eng, self.sem, self.base, self.per, self.k = eng, sem(name), it * per, per, 0

            def __call__(self, ins):
                self.k += 1
                ins.then_inc(self.sem, 1)
                self.eng.wait_ge(self.sem, self.base + self.k)

            def end(self):
                assert not self.per or self.k == self.per, self.k

        HEADS = ((slice(0, 64), slice(0, 64)), (slice(64, 128), slice(64, 128)))
        R_BLOCK, K_BLOCK, V_BLOCK = 0, RW_BLOCKS, 2 * RW_BLOCKS

        def chunks(t):
            return t.rearrange("p (c t) -> p c t", c=NCHUNK)

        def in_chunks(t):
            return t.rearrange("p (c n) -> p c n", c=NCHUNK)

        def over_chunks(col, wide=P):
            return con[:, col:col + wide].rearrange("p (o n) -> p o n", o=1).broadcast_to((P, NCHUNK, wide))

        def pcol_at(name, p):
            return par[:, bass.ds(p + COLS[name][0], 1)]

        def z_at(p, block):
            return z[:, bass.ds(p + block, 1), :].rearrange("p o t -> p (o t)")

        def mix_difference(dve, own, dst, src, rows=P):
            dve.tensor_tensor(dst[0:rows, 1:T], src[0:rows, 0:T - 1], src[0:rows, 1:T], ALU.subtract).then_inc(own, 1)
            dve.tensor_scalar(dst[0:rows, 0:1], src[0:rows, 0:1], -1.0, None, ALU.mult).then_inc(own, 1)

        def rwkv_zero(dve):
            for t in (v_bd, beta_bd, key_bd, kappa_bd):
                dve.memset(t[:, :, :], 0.0).then_inc(sem("rw_zeroed"), 1)
            for t in (lora_in[64:128, 0, :], lora_in[0:64, 1, :], lora_in[32:64, 3, :], lora_in[64:128, 3, :],
                      lora_w[32:64, 2, :], lora_w[64:128, 2, :]):
                dve.memset(t, 0.0).then_inc(sem("rw_zeroed"), 1)
            dve.memset(decay[:, :, 0:1], 1.0).then_inc(sem("rw_zeroed"), 1)

        def load_front_lora(pool, p):
            cols = bass.ds(p * P, P)
            pool.dma_start(lora_w[0:64, 0, :], rw_w2[:, cols]).then_inc(sem("front_lora_landed"), 16)
            pool.dma_start(lora_w[64:128, 0, :], rw_a2[:, cols]).then_inc(sem("front_lora_landed"), 16)

        def load_gate_lora(pool, p):
            cols = bass.ds(p * P, P)
            pool.dma_start(lora_w[:, 1, :], rw_g2[0:P, cols]).then_inc(sem("gate_lora_landed"), 16)
            pool.dma_start(lora_w[0:32, 2, :], rw_g2[P:P + 32, cols]).then_inc(sem("gate_lora_landed"), 16)

        def rwkv_prepare_dve(dve):
            for i, name in enumerate(("w0", "a0")):
                c0 = COLS[name][0]
                dve.tensor_scalar(half_bias[:, i, :], par[:, c0:c0 + RW_BLOCKS], 0.5, None, ALU.mult)\
                   .then_inc(sem("half_bias_ready"), 1)
            once(dve, "z_ready", 14)
            rows = (P, P, 32)
            for i, (dst, n) in enumerate(zip((kk_t, b_t, km_t), rows)):
                mix_difference(dve, sem("lora_difference"), dst, z_lora[:, i, :], n)
            for i, (dst, dif, n) in enumerate(zip((out_t, cen_t, csq_t), (kk_t, b_t, km_t), rows)):
                once(dve, "lora_difference", 2 * i + 2)
                mu = par[0:n, COLS["mu"][0] + 24 + i:COLS["mu"][0] + 25 + i]
                dve.scalar_tensor_tensor(dst[0:n], dif[0:n], mu, z_lora[0:n, i, :], ALU.mult, ALU.add)\
                   .then_inc(sem("lora_mixed"), 1)

        def rwkv_prepare_act(act):
            once(act, "rw_zeroed", 11)
            once(act, "lora_mixed", 3)
            done = sem("lora_inputs")
            act.activation(lora_in[0:64, 0, :], out_t[0:64], ACT.Tanh).then_inc(done, 1)
            act.activation(lora_in[64:128, 1, :], out_t[64:128], ACT.Copy).then_inc(done, 1)
            act.activation(lora_in[:, 2, :], cen_t, ACT.Sigmoid).then_inc(done, 1)
            act.activation(lora_in[0:32, 3, :], csq_t[0:32], ACT.Sigmoid).then_inc(done, 1)
            once(act, "half_bias_ready", 2)

        def dve_front_mix(dve, q):
            if not isinstance(q, int) or q:
                dve.wait_ge(sem("kappa_ready"), 7 * q)
                dve.wait_ge(sem("bonus_in"), q)
            else:
                once(dve, "lora_mixed", 3)
            dif = sem("difference")
            for t, block in ((kk_t, K_BLOCK), (b_t, R_BLOCK), (km_t, V_BLOCK)):
                mix_difference(dve, dif, t, z_at(q, block))
            for i, (t, block) in enumerate(((kk_t, K_BLOCK), (b_t, R_BLOCK), (km_t, V_BLOCK))):
                dve.wait_ge(dif, 6 * q + 2 * i + 2)
                dve.scalar_tensor_tensor(z_at(q, block), t, pcol_at("mu", q + block), z_at(q, block), ALU.mult, ALU.add)\
                   .then_inc(sem("mixed"), 1)

        def dve_front_decay(dve, own, q):
            dve.wait_ge(sem("tanh_ready"), 2 * q + 1)
            own(dve.tensor_scalar(thw_t, thw_t, 1.0, None, ALU.add))
            dve.tensor_tensor_scan(sum_t, con[:, CSEG:CSEG + T], thw_t, 0.0, ALU.mult, ALU.add)\
               .then_inc(sem("log_decay_ready"), 1)
            dve.wait_ge(sem("tanh_ready"), 2 * q + 2)
            own(dve.tensor_scalar(iclr_t, iclr_t, 0.5, 0.5, ALU.mult, ALU.add))
            dve.wait_ge(sem("mixed"), 3 * q + 3)
            own(dve.tensor_scalar(km_t, iclr_t, -1.0, pcol_at("k_a", q), ALU.add, ALU.mult))
            own(dve.scalar_tensor_tensor(km_t, km_t, 1.0, z_at(q, K_BLOCK), ALU.add, ALU.mult))

        def dve_front_sum(dve, q):
            dve.wait_ge(sem("kk_sum_done"), q + 1)
            dve.tensor_scalar(nrm_t, acc[0][:, 0:T], 1e-24, None, ALU.max).then_inc(sem("kk_sum_read"), 1)

        def dve_front_kk(dve, own, q):
            dve.wait_ge(sem("kk_root_ready"), q + 1)
            own(dve.reciprocal(nrm_t, nrm_t))
            own(dve.scalar_tensor_tensor(kk_t, z_at(q, K_BLOCK), pcol_at("k_k", q), nrm_t, ALU.mult, ALU.mult))
            own(dve.tensor_tensor(b_t, kk_t, iclr_t, ALU.mult))
            own.end()

        def dve_front_keys(dve, q):
            dve.wait_ge(sem("decay_ready"), 2 * q + 2)
            for a, b in HEADS:
                dve.tensor_tensor(beta_bd[a, :, b], chunks(b_t[a]), chunks(em_t[a]), ALU.mult).then_inc(sem("kappa_ready"), 1)
            for a, b in HEADS:
                dve.tensor_tensor(key_bd[a, :, b], chunks(km_t[a]), chunks(em_t[a]), ALU.mult).then_inc(sem("kappa_ready"), 1)
            dve.scalar_tensor_tensor(sq_t, z_at(q, R_BLOCK), pcol_at("r_k", q), km_t, ALU.mult, ALU.mult)\
               .then_inc(sem("bonus_in"), 1)

        def dve_front_kappa(dve, q):
            for a, b in HEADS:
                dve.tensor_tensor(kappa_bd[a, :, b], chunks(kk_t[a]), decay[a, :, 0:CHUNK], ALU.mult).then_inc(sem("kappa_ready"), 1)

        def dve_front_rho(dve, q):
            dve.tensor_tensor(chunks(rho_t), chunks(z_at(q, R_BLOCK)), decay[:, :, 1:CHUNK + 1], ALU.mult)\
               .then_inc(sem("kappa_ready"), 1)

        def act_front_square(act, q):
            act.wait_ge(sem("mixed"), 3 * q + 3)
            act.activation(b_t, z_at(q, K_BLOCK), ACT.Square, scale=pcol_at("k_k", q)).then_inc(sem("kk_square"), 1)

        def act_front_tanh(act, q):
            act.wait_ge(sem("lora_done"), q + 1)
            act.activation(thw_t, acc[1][:, 0:T], ACT.Tanh, scale=0.5,
                           bias=half_bias[:, 0, bass.ds(q, 1)]).then_inc(sem("tanh_ready"), 1)
            act.activation(iclr_t, acc[1][:, T:2 * T], ACT.Tanh, scale=0.5,
                           bias=half_bias[:, 1, bass.ds(q, 1)]).then_inc(sem("tanh_ready"), 1)

        def act_front_exp(act, q):
            act.wait_ge(sem("log_decay_ready"), q + 1)
            act.activation(decay[:, :, 1:CHUNK + 1], chunks(sum_t), ACT.Exp, scale=-DECAY_C / 2).then_inc(sem("decay_ready"), 1)
            act.activation(em_t, sum_t, ACT.Exp, scale=DECAY_C / 2).then_inc(sem("decay_ready"), 1)

        def act_front_root(act, q):
            act.wait_ge(sem("kk_sum_read"), q + 1)
            act.activation(nrm_t, nrm_t, ACT.Sqrt).then_inc(sem("kk_root_ready"), 1)

        def act_front_v(act, q):
            for a, b in HEADS:
                act.activation(v_bd[a, :, b], chunks(z_at(q, V_BLOCK)[a]), ACT.Copy).then_inc(sem("v_ready"), 1)

        def mm(out, lhsT, rhs, first=True, last=True):
            return nc.tensor.matmul(out, lhsT, rhs, start=first, stop=last)

        ones = con[:, CONES:CONES + P]

        def pe_front_lora(pe, q):
            pe.wait_ge(sem("front_lora_landed"), 32 * (q + 1))
            if not isinstance(q, int) or q:
                pe.wait_ge(sem("tanh_ready"), 2 * q)
            mm(acc[1][:, 0:T], lora_w[:, 0, :], lora_in[:, 0, :])
            mm(acc[1][:, T:2 * T], lora_w[:, 0, :], lora_in[:, 1, :]).then_inc(sem("lora_done"), 1)

        def pe_front_sum(pe, q):
            if not isinstance(q, int) or q > 1:
                pe.wait_ge(sem("gated"), q - 1)
            pe.wait_ge(sem("kk_square"), q + 1)
            mm(acc[0][:, 0:T], ones, b_t).then_inc(sem("kk_sum_done"), 1)

        def pe_mean(pe, n):
            pe.wait_ge(sem("bonus_ready"), n + 1)
            pe.wait_ge(sem("out_copied"), n + 1)
            mm(acc[0][:, 0:T], ones, out_t).then_inc(sem("mean_done"), 1)

        def pe_variance(pe, n):
            pe.wait_ge(sem("gate_lora_landed"), 32 * (n + 1))
            pe.wait_ge(sem("centred_square"), n + 1)
            mm(acc[0][:, 0:T], ones, csq_t)
            mm(acc[0][:, T:2 * T], lora_w[:, 1, :], lora_in[:, 2, :], last=False)
            mm(acc[0][:, T:2 * T], lora_w[:, 2, :], lora_in[:, 3, :], first=False).then_inc(sem("variance_done"), 1)

        def dve_centre(dve, n):
            dve.wait_ge(sem("mean_done"), n + 1)
            dve.scalar_tensor_tensor(cen_t, acc[0][:, 0:T], -1.0 / CHUNK, out_t, ALU.mult, ALU.add).then_inc(sem("centred"), 1)

        def act_centre_square(act, n):
            act.wait_ge(sem("centred"), n + 1)
            act.activation(csq_t, cen_t, ACT.Square).then_inc(sem("centred_square"), 1)

        def dve_variance(dve, n):
            dve.wait_ge(sem("variance_done"), n + 1)
            dve.tensor_scalar(csq_t, acc[0][:, 0:T], 1.0 / CHUNK, RW_EPS, ALU.mult, ALU.add).then_inc(sem("variance_ready"), 1)

        def act_deviation(act, n):
            act.wait_ge(sem("variance_ready"), n + 1)
            act.activation(csq_t, csq_t, ACT.Sqrt).then_inc(sem("deviation_ready"), 1)

        def dve_inverse_deviation(dve, own, n):
            dve.wait_ge(sem("deviation_ready"), n + 1)
            own(dve.reciprocal(csq_t, csq_t))

            own(dve.tensor_tensor(cen_t, cen_t, csq_t, ALU.mult))

        def dve_affine(dve, own, n):
            own(dve.tensor_scalar(cen_t, cen_t, pcol_at("lnx_w", n), pcol_at("lnx_b", n), ALU.mult, ALU.add))
            dve.wait_ge(sem("bonus_ready"), n + 1)
            own(dve.tensor_tensor(cen_t, cen_t, bon_t, ALU.add))

        def dve_gate(dve, own, n):
            dve.tensor_tensor(cen_t, cen_t, acc[0][:, T:2 * T], ALU.mult).then_inc(sem("gated"), 1)
            own.end()

        def act_result_hi(act, n):
            act.wait_ge(sem("gated"), n + 1)
            act.activation(hidB_hi[:, bass.ds(n, 1), :].rearrange("p o t -> p (o t)"), cen_t, ACT.Copy).then_inc(sem("rw_hi"), 1)

        def dve_result_lo(dve, n):
            dve.wait_ge(sem("rw_hi"), n + 1)
            dve.tensor_tensor(hidB_lo[:, bass.ds(n, 1), :].rearrange("p o t -> p (o t)"), cen_t,
                              hidB_hi[:, bass.ds(n, 1), :].rearrange("p o t -> p (o t)"), ALU.subtract)\
               .then_inc(sem("rw_split"), 1)
            dve.wait_ge(sem("rw_split"), n + 1)

        def rwkv_pool(pool, p, gate, front):
            for l in range(1, LEVELS):
                if l == 1:
                    pool.wait_ge(sem("inv_start"), p + 1)
                else:
                    pool.wait_ge(sem("y_done"), 5 * p + l - 1)
                pool.tensor_tensor(level_a[:, :, :], v_bd[:, :, :], over_chunks(CLEVEL + l * P), ALU.mult)\
                    .then_inc(sem("level_ready"), 1)
                if l == 2 and gate:
                    pool.wait_ge(sem("variance_done"), p)
                    load_gate_lora(pool, p)
                if l == 4 and front:
                    pool.wait_ge(sem("lora_done"), p + 2)
                    load_front_lora(pool, p + 2)

        def rwkv_dve(dve, p, norm, front):
            g, q = RET_N + p, p + 1
            own = Own(dve, "dve_own", p, 4)
            front_own = Own(dve, "front_own", q, 7)
            norm_own = Own(dve, "norm_own", p - 1, 4)
            if norm:
                dve_centre(dve, p - 1)
                dve.wait_ge(sem("state_ready"), 3 * p)
            own(dve.tensor_copy(decay_end[:, :], decay[:, :, CHUNK]))
            if front:
                dve_front_mix(dve, q)
            dve.wait_ge(sem("products_done"), p + 1)
            dve.tensor_tensor(seen_v[:, :, :], in_chunks(tp[2][:, :]), over_chunks(CSTRICT), ALU.mult)\
               .then_inc(sem("seen_ready"), 1)
            dve.scalar_tensor_tensor(seen_y[:, 0, :, :], chunks(tp[3][:, 0:T]), -1.0, over_chunks(CINCL, CHUNK),
                                     ALU.mult, ALU.mult).then_inc(sem("seen_ready"), 1)
            dve.tensor_tensor(seen_y[:, 1, :, :], chunks(tp[3][:, T:2 * T]), over_chunks(CINCL, CHUNK),
                              ALU.mult).then_inc(sem("seen_ready"), 1)
            dve.wait_ge(sem("a_copied"), p + 1)
            own(dve.tensor_tensor(level_a[:, :, :], v_bd[:, :, :], over_chunks(CLEVEL), ALU.mult))
            dve.wait_ge(sem("tokens_done"), 3 * p + 2)
            dve.tensor_tensor(key_bd[:, :, :], over_chunks(CIDENT), level_a[:, :, :], ALU.subtract).then_inc(sem("inv_start"), 1)
            if norm:
                dve_variance(dve, p - 1)
            split_lo(dve, g, 2)
            split_lo(dve, g, 3)
            for l in range(1, LEVELS):
                dve.wait_ge(sem("y_done"), 5 * p + l)
                if l == 1:
                    dve.wait_ge(sem("tokens_done"), 3 * p + 3)
                dve.tensor_tensor(beta_bd[:, :, :], over_chunks(CIDENT), in_chunks(tp[2][:, :]), ALU.subtract)\
                   .then_inc(sem("w_ready"), 1)
                if l < LEVELS - 1:
                    dve.wait_ge(sem("inv_done"), 4 * p + l)
                    dve.tensor_copy(key_bd[:, :, :], in_chunks(tp[0][:, :])).then_inc(sem("inv_ready"), 1)
                if l == 1 and norm:
                    dve_inverse_deviation(dve, norm_own, p - 1)
                if l == 2:
                    split_lo(dve, g, 4)
                    if norm:
                        dve_affine(dve, norm_own, p - 1)
                if l == 3:
                    if norm:
                        dve_gate(dve, norm_own, p - 1)
                    if front:
                        dve_front_decay(dve, front_own, q)
                if l == 4:
                    split_lo(dve, g, 5)
                    if front:
                        dve_front_sum(dve, q)
            if norm:
                dve_result_lo(dve, p - 1)
            split_lo(dve, g, 6)
            for c in range(NCHUNK - 1):
                if c == 0:
                    dve.wait_ge(sem("bonus_done"), p + 1)
                    dve.tensor_tensor(bon_t, acc[0][:, 0:T], z_at(p, V_BLOCK), ALU.mult).then_inc(sem("bonus_ready"), 1)
                dve.wait_ge(sem("state_done"), 3 * p + c + 1)
                new, end = state[:, (c + 1) % 2, :], decay_end[:, c:c + 1]
                if c == 0:
                    dve.tensor_scalar(new, tp[0][:, 0:P], end, None, ALU.mult).then_inc(sem("state_ready"), 1)
                else:
                    dve.scalar_tensor_tensor(new, tp[0][:, 0:P], end, scaled[:, :], ALU.mult, ALU.add)\
                       .then_inc(sem("state_ready"), 1)
                if c < NCHUNK - 2:
                    dve.wait_ge(sem("state_ready"), 3 * p + c + 1)
                    own(dve.tensor_scalar(scaled[:, :], new, decay_end[:, c + 1:c + 2], None, ALU.mult))
                if c == 0:
                    split_lo(dve, g, 7)
                if c == 1 and front:
                    dve_front_kk(dve, front_own, q)
            if front:
                dve.wait_ge(sem("inv_t_done"), LEVELS * (p + 1))
                dve_front_keys(dve, q)
                split_lo(dve, g + 1, 0)
                dve.wait_ge(sem("rhs_done"), NCHUNK * (p + 1))
                dve_front_kappa(dve, q)
                dve.wait_ge(sem("out_done"), p + 1)
                dve_front_rho(dve, q)
                split_lo(dve, g + 1, 1)
            own.end()

        def rwkv_act(act, p, norm, front):
            g, q = RET_N + p, p + 1
            act.wait_ge(sem("tokens_done"), 3 * p + 1)
            act.activation(v_tok[:, :, :], in_chunks(tp[0][:, :]), ACT.Copy).then_inc(sem("tokens_ready"), 1)
            if norm:
                act_centre_square(act, p - 1)
            split_hi(act, g, 2)
            split_hi(act, g, 3)
            act.wait_ge(sem("products_done"), p + 1)
            act.activation(v_bd[:, :, :], in_chunks(tp[1][:, :]), ACT.Copy).then_inc(sem("a_copied"), 1)
            act.wait_ge(sem("tokens_done"), 3 * p + 2)
            act.activation(key_tok[:, :, :], in_chunks(tp[0][:, :]), ACT.Copy).then_inc(sem("tokens_ready"), 1)
            if front:
                act_front_square(act, q)
            act.wait_ge(sem("tokens_done"), 3 * p + 3)
            act.activation(beta_tok[:, :, :], in_chunks(tp[3][:, :]), ACT.Copy, scale=-1.0).then_inc(sem("tokens_ready"), 1)
            for l in range(LEVELS):
                act.wait_ge(sem("inv_t_done"), LEVELS * p + l + 1)
                act.activation(inv_t[:, :, :], in_chunks(tp[1][:, :]), ACT.Copy).then_inc(sem("inv_t_ready"), 1)
                if l == 0:
                    if norm:
                        act_deviation(act, p - 1)
                if l == 1:
                    split_hi(act, g, 4)
                    if front:
                        act_front_tanh(act, q)
                if l == 2:
                    split_hi(act, g, 5)
                if l == 3:
                    if norm:
                        act_result_hi(act, p - 1)
                    split_hi(act, g, 6)
                if l == 4:
                    if front:
                        act_front_exp(act, q)
            for c in range(NCHUNK):
                act.wait_ge(sem("rhs_done"), NCHUNK * p + c + 1)
                act.activation(rhs_u[:, :], tp[2][:, 0:P], ACT.Copy).then_inc(sem("rhs_ready"), 1)
                act.wait_ge(sem("u_done"), NCHUNK * p + c + 1)
                act.activation(u_bd[:, :], tp[3][:, 0:P], ACT.Copy).then_inc(sem("u_ready"), 1)
                if c == 0:
                    split_hi(act, g, 7)
                    if front:
                        act_front_root(act, q)
                if front:
                    if c == 1:
                        act.wait_ge(sem("level_ready"), 5 * (p + 1))
                        act_front_v(act, q)
                    if c == 2:
                        split_hi(act, g + 1, 0)
            act.wait_ge(sem("out_done"), p + 1)
            act.activation(out_t, tp[1][:, 0:T], ACT.Copy).then_inc(sem("out_copied"), 1)
            act.wait_ge(unit_used, 8 * (g + 1))
            for h in range(HALVES):
                act.activation(ret_tok[:, bass.ds(p, 1), h, :].rearrange("p o n -> p (o n)"), acc[2 + h][:, :], ACT.Copy,
                               scale=rstd[:, h:h + 1]).then_inc(stg_written, 1)
            if front:
                split_hi(act, g + 1, 1)

        def more(pe, p, parts, m):
            due = min(32, parts[0] + m)
            for part in range(parts[1], due):
                multiply_part(pe, RET_N + p, part, xT, 1)
            parts[:] = due, max(due, parts[1])

        def rwkv_pe(pe, p, norm, front, parts):
            pe.wait_ge(sem("v_ready"), 2 * p + 2)
            for c in range(NCHUNK):
                last = nc.tensor.transpose(tp[0][:, c * P:(c + 1) * P], v_bd[:, c, :], ident)
            last.then_inc(sem("tokens_done"), 1)
            if norm:
                pe_mean(pe, p - 1)
            pe.wait_ge(stg_written, 2 * (RET_STG + p))
            more(pe, p, parts, 3)
            pe.wait_ge(sem("kappa_ready"), 7 * p + 7)
            for c in range(NCHUNK):
                rho = chunks(rho_t)[:, c, :]
                mm(tp[1][:, c * P:(c + 1) * P], kappa_bd[:, c, :], beta_bd[:, c, :])
                mm(tp[2][:, c * P:(c + 1) * P], key_bd[:, c, :], kappa_bd[:, c, :])
                mm(tp[3][:, c * CHUNK:(c + 1) * CHUNK], beta_bd[:, c, :], rho)
                last = mm(tp[3][:, T + c * CHUNK:T + (c + 1) * CHUNK], key_bd[:, c, :], rho)
            last.then_inc(sem("products_done"), 1)
            pe.wait_ge(sem("tokens_ready"), 3 * p + 1)
            for c in range(NCHUNK):
                last = nc.tensor.transpose(tp[0][:, c * P:(c + 1) * P], key_bd[:, c, :], ident)
            last.then_inc(sem("tokens_done"), 1)
            if norm:
                pe_variance(pe, p - 1)
            more(pe, p, parts, 2)
            pe.wait_ge(sem("seen_ready"), 3 * p + 3)
            for c in range(NCHUNK):
                last = nc.tensor.transpose(tp[3][:, c * P:(c + 1) * P], beta_bd[:, c, :], ident)
            last.then_inc(sem("tokens_done"), 1)
            more(pe, p, parts, 2)
            pe.wait_ge(sem("inv_start"), p + 1)
            for c in range(NCHUNK):
                last = nc.tensor.transpose(tp[1][:, c * P:(c + 1) * P], key_bd[:, c, :], ident)
            last.then_inc(sem("inv_t_done"), 1)
            if front:
                pe_front_lora(pe, p + 1)
            pe.wait_ge(sem("tokens_ready"), 3 * p + 2)
            for l in range(1, LEVELS):
                more(pe, p, parts, 1)
                pe.wait_ge(sem("level_ready"), 5 * p + l)
                pe.wait_ge(sem("inv_t_ready"), LEVELS * p + l)
                for c in range(NCHUNK):
                    last = mm(tp[2][:, c * P:(c + 1) * P], level_a[:, c, :], inv_t[:, c, :])
                last.then_inc(sem("y_done"), 1)
                more(pe, p, parts, 2)
                pe.wait_ge(sem("w_ready"), 5 * p + l)
                if l > 1:
                    pe.wait_ge(sem("inv_ready"), 4 * p + l - 1)
                for c in range(NCHUNK):
                    last = mm(tp[1][:, c * P:(c + 1) * P], key_bd[:, c, :], beta_bd[:, c, :])
                last.then_inc(sem("inv_t_done"), 1)
                if l < LEVELS - 1:
                    for c in range(NCHUNK):
                        last = mm(tp[0][:, c * P:(c + 1) * P], beta_bd[:, c, :], key_bd[:, c, :])
                    last.then_inc(sem("inv_done"), 1)
                if l == 3 and front:
                    pe_front_sum(pe, p + 1)
            pe.wait_ge(sem("tokens_ready"), 3 * p + 3)
            pe.wait_ge(sem("inv_t_ready"), LEVELS * (p + 1))
            for c in range(NCHUNK):
                s, v = state[:, c % 2, :], v_tok[:, c, :]
                if c:
                    pe.wait_ge(sem("state_ready"), 3 * p + c)
                    mm(tp[2][:, 0:P], kappa_bd[:, c, :], s, last=False)
                mm(tp[2][:, 0:P], seen_v[:, c, :], v, first=(c == 0)).then_inc(sem("rhs_done"), 1)
                if c == 0:
                    if front:
                        pe.wait_ge(sem("kk_sum_read"), p + 2)
                    else:
                        pe.wait_ge(sem("gated"), p)
                    mm(acc[0][:, 0:T], ones, sq_t).then_inc(sem("bonus_done"), 1)
                more(pe, p, parts, 1)
                pe.wait_ge(sem("rhs_ready"), NCHUNK * p + c + 1)
                mm(tp[3][:, 0:P], inv_t[:, c, :], rhs_u[:, :]).then_inc(sem("u_done"), 1)
                more(pe, p, parts, 1)
                pe.wait_ge(sem("u_ready"), NCHUNK * p + c + 1)
                if c < NCHUNK - 1:
                    mm(tp[0][:, 0:P], key_tok[:, c, :], v, last=False)
                    mm(tp[0][:, 0:P], beta_tok[:, c, :], u_bd[:, :], first=False).then_inc(sem("state_done"), 1)
                y = tp[1][:, c * CHUNK:(c + 1) * CHUNK]
                if c:
                    mm(y, s, chunks(rho_t)[:, c, :], last=False)
                mm(y, v, seen_y[:, 1, c, :], first=(c == 0), last=False)
                last = mm(y, u_bd[:, :], seen_y[:, 0, c, :], first=False)
            last.then_inc(sem("out_done"), 1)
            more(pe, p, parts, 32)

        def rwkv(role, eng):
            LAST = RW_BLOCKS - 1
            if role == "sp":
                with eng.Fori(0, RW_BLOCKS) as p:
                    for j in range(UNITS):
                        load_unit(eng, RET_N + p, j, ev_w_in, 0, p * WIDE)
            elif role == "pool":
                once(eng, "rw_zeroed", 11)
                load_front_lora(eng, 0)
                load_gate_lora(eng, 0)
                once(eng, "lora_done", 1)
                load_front_lora(eng, 1)
                rwkv_pool(eng, 0, False, True)
                with eng.Fori(1, LAST - 1) as p:
                    rwkv_pool(eng, p, True, True)
                for p in (LAST - 1, LAST):
                    rwkv_pool(eng, p, True, False)
            elif role == "dve":
                for j in range(2):
                    split_lo(eng, RET_N, j)
                rwkv_prepare_dve(eng)
                dve_front_mix(eng, 0)
                own = Own(eng, "front_own", 0, 7)
                dve_front_sum(eng, 0)
                dve_front_decay(eng, own, 0)
                dve_front_kk(eng, own, 0)
                dve_front_keys(eng, 0)
                dve_front_kappa(eng, 0)
                dve_front_rho(eng, 0)
                rwkv_dve(eng, 0, False, True)
                with eng.Fori(1, LAST) as p:
                    rwkv_dve(eng, p, True, True)
                rwkv_dve(eng, LAST, True, False)
                dve_centre(eng, LAST)
                dve_variance(eng, LAST)
                own = Own(eng, "norm_own", LAST, 4)
                dve_inverse_deviation(eng, own, LAST)
                dve_affine(eng, own, LAST)
                dve_gate(eng, own, LAST)
                dve_result_lo(eng, LAST)
            elif role == "act":
                for j in range(2):
                    split_hi(eng, RET_N, j)
                rwkv_prepare_act(eng)
                act_front_square(eng, 0)
                act_front_v(eng, 0)
                act_front_tanh(eng, 0)
                act_front_exp(eng, 0)
                act_front_root(eng, 0)
                rwkv_act(eng, 0, False, True)
                with eng.Fori(1, LAST) as p:
                    rwkv_act(eng, p, True, True)
                rwkv_act(eng, LAST, True, False)
                act_centre_square(eng, LAST)
                act_deviation(eng, LAST)
                act_result_hi(eng, LAST)
            elif role == "pe":
                parts = [0, 0]
                eng.wait_ge(stg_written, 2 * RET_STG)
                more(eng, 0, parts, 4)
                eng.wait_ge(sem("lora_inputs"), 4)
                pe_front_sum(eng, 0)
                pe_front_lora(eng, 0)
                more(eng, 0, parts, 4)
                parts[0] = 0
                rwkv_pe(eng, 0, False, True, parts)
                with eng.Fori(1, LAST) as p:
                    rwkv_pe(eng, p, True, True, [0, 0])
                rwkv_pe(eng, LAST, True, False, [0, 0])
                pe_mean(eng, LAST)
                pe_variance(eng, LAST)

        def ret_view(kind, h, half=None, part=None):
            group, c0 = 2 * kind + h // 2, (h % 2) * 2 * P + (part or 0) * P
            c1 = c0 + (2 * P if part is None else P)
            return ret_tok[:, group, :, c0:c1] if half is None else ret_tok[:, group, half, c0:c1]

        def rotate(eng, kind, rot, name):
            cos, sin = table_cs[:, :, 0, :], table_cs[:, :, 1, :]
            products, done = sem(name + "_products"), sem(name + "_rotated")
            for h in range(RET_HEADS):
                t1, t2 = ret_view(kind, h, part=0), ret_view(kind, h, part=1)
                if h:
                    eng.wait_ge(done, 2 * h)
                for i, (a, b) in enumerate(((t1, cos), (t2, sin), (t2, cos), (t1, sin))):
                    eng.tensor_tensor(rot[:, i, :, :], a, b, ALU.mult).then_inc(products, 1)
                eng.wait_ge(products, 4 * h + 4)
                eng.tensor_tensor(t1, rot[:, 0, :, :], rot[:, 1, :, :], ALU.subtract).then_inc(done, 1)
                eng.tensor_tensor(t2, rot[:, 2, :, :], rot[:, 3, :, :], ALU.add).then_inc(done, 1)

        RET_DONE = 2 * (RET_STG + 8)

        def retention(role, eng):
            if role == "sp":
                once(eng, "rw_split", RW_BLOCKS)
                eng.dma_start(table_cs[:, :, :, :], cossin.rearrange("(h p) a c -> p h a c", p=P)).then_inc(sem("cs_landed"), 16)
                for h in range(RET_HEADS):
                    if h >= 2:
                        once(eng, "scores_ready", h - 1)
                    eng.dma_start(table_d[:, h % 2, :, :], rdecay[h].rearrange("(m p) n -> p m n", p=P))\
                       .then_inc(sem(f"decay_landed{h % 2}"), 16)
            elif role == "pool":
                once(eng, "cs_landed", 16)
                once(eng, "stg_written", RET_DONE)
                rotate(eng, 1, rot_k, "k")
            elif role == "dve":
                once(eng, "cs_landed", 16)
                once(eng, "stg_written", RET_DONE)
                rotate(eng, 0, rot_q, "q")
                for s in range(RET_HEADS + 2):
                    if s < RET_HEADS:
                        if s >= 2:
                            once(eng, "ret_out_done", s - 1)
                        once(eng, "scores_done", s + 1)
                        once(eng, f"decay_landed{s % 2}", 16 * (s // 2 + 1))
                        eng.tensor_tensor(scores[:, s % 2, :, :], acc[s % 2][:, :].rearrange("p (m n) -> p m n", m=HALVES),
                                          table_d[:, s % 2, :, :], ALU.mult).then_inc(sem("scores_ready"), 1)
                    h = s - 1
                    if 0 <= h < RET_HEADS:
                        once(eng, "ret_out_done", h + 1)
                        own = Own(eng, "ret_own", h, 8)
                        for i in range(HALVES):
                            own(eng.bn_stats(rstat[:, i, :], acc[2 + h % 2][:, i * T:(i + 1) * T]))
                        for i in range(HALVES):
                            own(eng.bn_aggr(rmean[:, i, :], rstat[:, i, :]))
                        eng.tensor_scalar(rdev[:, :], rmean[:, :, 1], RET_EPS, None, ALU.add).then_inc(sem("ret_variance"), 1)
                        once(eng, "ret_deviation", h + 1)
                        own(eng.reciprocal(rdev[:, :], rdev[:, :]))
                        for i in range(HALVES):
                            own(eng.tensor_scalar(y_ret[:, h % 2, i, :], acc[2 + h % 2][:, i * T:(i + 1) * T],
                                                  rmean[:, i, 0:1], rdev[:, i:i + 1], ALU.subtract, ALU.mult))
                        once(eng, "ret_gate", 2)
                        own(eng.tensor_tensor(y_ret[:, h % 2, :, :], y_ret[:, h % 2, :, :], ret_view(3, h), ALU.mult))
                        own.end()
                    h = s - 2
                    if h >= 0:
                        once(eng, "ret_hi", h + 1)
                        eng.tensor_tensor(hidA_lo[:, 2 * h:2 * h + 2, :],
                                          tp[2 * (h % 2)][:, :].rearrange("p (c t) -> p c t", c=2),
                                          hidA_hi[:, 2 * h:2 * h + 2, :], ALU.subtract).then_inc(sem("ret_split"), 1)
            elif role == "act":
                once(eng, "stg_written", RET_DONE)
                for i in range(2):
                    g = ret_tok[:, 6 + i, :, :]
                    eng.activation(g, g, ACT.Silu).then_inc(sem("ret_gate"), 1)
                for h in range(RET_HEADS):
                    for i, (t, name) in enumerate(((qT, "q_turned"), (kT, "k_turned"))):
                        once(eng, name, h + 1)
                        eng.activation(t[:, 2 * h:2 * h + 2, :],
                                       tp[2 * (h % 2) + i][:, :].rearrange("p (c t) -> p c t", c=2), ACT.Copy)\
                           .then_inc(sem("qk_ready"), 1)
                for s in range(1, RET_HEADS + 2):
                    if s - 1 < RET_HEADS:
                        once(eng, "ret_variance", s)
                        eng.activation(rdev[:, :], rdev[:, :], ACT.Sqrt).then_inc(sem("ret_deviation"), 1)
                    h = s - 2
                    if h >= 0:
                        once(eng, "y_turned", h + 1)
                        eng.activation(hidA_hi[:, 2 * h:2 * h + 2, :],
                                       tp[2 * (h % 2)][:, :].rearrange("p (c t) -> p c t", c=2), ACT.Copy)\
                           .then_inc(sem("ret_hi"), 1)
            elif role == "pe":
                def turn(bank, view, name):
                    for part in range(2):
                        for half in range(HALVES):
                            last = nc.tensor.transpose(tp[bank][:, part * T + half * P:part * T + (half + 1) * P],
                                                       view(half, part), ident)
                    last.then_inc(sem(name), 1)

                once(eng, "bonus_ready", RW_BLOCKS)
                once(eng, "variance_ready", RW_BLOCKS)
                once(eng, "out_copied", RW_BLOCKS)
                once(eng, "centred", RW_BLOCKS)
                for h in range(RET_HEADS):
                    if h >= 2:
                        once(eng, "qk_ready", 2 * (h - 1))
                    once(eng, "q_rotated", 2 * h + 2)
                    turn(2 * (h % 2), lambda half, part: ret_view(0, h, half, part), "q_turned")
                    once(eng, "k_rotated", 2 * h + 2)
                    turn(2 * (h % 2) + 1, lambda half, part: ret_view(1, h, half, part), "k_turned")
                for s in range(RET_HEADS + 2):
                    if s < RET_HEADS:
                        if s >= 2:
                            once(eng, "scores_ready", s - 1)
                        once(eng, "qk_ready", 2 * s + 2)
                        for m in range(HALVES):
                            for d in range(2):
                                last = nc.tensor.matmul(acc[s % 2][:, m * T:(m + 1) * T],
                                                        kT[:, 2 * s + d, m * P:(m + 1) * P], qT[:, 2 * s + d, :],
                                                        start=(d == 0), stop=(d == 1))
                        last.then_inc(sem("scores_done"), 1)
                    h = s - 1
                    if 0 <= h < RET_HEADS:
                        once(eng, "scores_ready", h + 1)
                        for i in range(HALVES):
                            for m in range(i + 1):
                                last = nc.tensor.matmul(acc[2 + h % 2][:, i * T:(i + 1) * T],
                                                        scores[:, h % 2, m, i * P:(i + 1) * P], ret_view(2, h, m),
                                                        start=(m == 0), stop=(m == i))
                        last.then_inc(sem("ret_out_done"), 1)
                    h = s - 2
                    if h >= 0:
                        if h >= 2:
                            once(eng, "ret_split", h - 1)
                        once(eng, "ret_own", 8 * h + 8)
                        turn(2 * (h % 2), lambda half, part: y_ret[:, h % 2, half, part * P:(part + 1) * P], "y_turned")

        C_EVEN_OUT = dict(n=15, tused=(6, 5), xu=0, xs=4, thi=16, lhs=16, norm=1)

        def out_projection(role, eng, c, w, gain, free, tp_first, need, prev=None, side=None):
            def g(k):
                r = residual(c, k, gain)
                r["free"] = free(k) if k < 2 else (x_updated, c["xu"] + k - 1)
                r["need"] = need if k == 0 else None
                if k < 2 and tp_first:
                    r["tp"] = tp_first
                return r

            for k in range(4):
                step(role, eng, g(k), w, 0, k * WIDE, hid, prev, side if k == 0 else None)
                prev = g(k)
            return prev

        def even_mixed(pe, j):
            once(pe, "ret_split", min(j + 1, RET_HEADS))
            once(pe, "rw_split", RW_BLOCKS)

        C_MLP0 = dict(n=19, tused=(8, 7), stg=15, hid=0, xu=4, xs=8, thi=32, lhs=32, norm=2)

        C_ODD = after_mlp(C_MLP0, "od_norm")
        ODD_STG, ODD_Z = C_ODD["stg"], 14

        def branch(v):
            k = v % 4

            def move(dve, c, bank):
                return dve.tensor_copy(x_raw[:, 4 * k + 2 * c:4 * k + 2 * c + 2, CONV - 1:],
                                       bank[:, :].rearrange("p (c t) -> p c t", c=2))

            if v < 2:
                free, tp_free = (x_updated, C_ODD["xu"] - 1 + v), (lhs_ready, C_ODD["lhs"])
            else:
                free, tp_free = (stg_written, 2 * (ODD_STG + v - 1)), (z_ready, ODD_Z + 2 * (v - 1))
            if 3 <= v <= 6:
                tp_free = (sem("gates_read"), 8 * (v - 2))
            if 4 <= v <= 7:
                free = (sem("gates_read"), 8 * (v - 3))
            return dict(n=C_ODD["n"] + v, bank=v % 2, post="z", wide=WIDE, free=free, tp=tp_free, move=move,
                        need=(C_ODD["lhs"] - 4, C_ODD["lhs"]) if v == 0 else None, stg=ODD_STG + v, norm=C_ODD["norm"],
                        tused=C_ODD["tused"][v % 2] + v // 2, func=ACT.Gelu_apprx_tanh if v >= 4 else ACT.Copy)

        def branch_step(role, eng, v, prev):
            step(role, eng, branch(v), od_w_in, 0, (D if v < 4 else 0) + (v % 4) * WIDE, xT, prev,
                 odd_side(v) if v >= 2 else None)

        def prepare_lambda(role, eng):
            src = par[:, COLS["lam"][0]:COLS["lam"][0] + KT]
            a, e, zz, z2, q, out8 = (lam[:, i, :] for i in range(6))
            if role == "dve":
                own = Own(eng, "lambda_own")
                own(eng.tensor_scalar(zz, src, -1.0, None, ALU.mult))
                own(eng.tensor_tensor(a, src, zz, ALU.max))
                own(eng.tensor_scalar(out8, zz, 0.0, None, ALU.max))
                once(eng, "lambda_exp", 1)
                own(eng.tensor_scalar(q, e, 2.0, None, ALU.add))
                own(eng.reciprocal(q, q))
                own(eng.tensor_tensor(zz, e, q, ALU.mult))
                own(eng.tensor_tensor(z2, zz, zz, ALU.mult))
                own(eng.tensor_scalar(q, z2, 1.0 / 15, None, ALU.mult))
                for odd in (13, 11, 9, 7, 5, 3):
                    own(eng.scalar_tensor_tensor(q, q, 1.0 / odd, z2, ALU.add, ALU.mult))
                own(eng.scalar_tensor_tensor(q, q, 1.0, zz, ALU.add, ALU.mult))
                own(eng.scalar_tensor_tensor(out8, q, 2.0, out8, ALU.mult, ALU.add))
                eng.tensor_scalar(out8, out8, -LRU_C, None, ALU.mult).then_inc(sem("lambda_ready"), 1)
            else:
                once(eng, "lambda_own", 2)
                eng.activation(e, a, ACT.Exp, scale=-1.0).then_inc(sem("lambda_exp"), 1)
                once(eng, "lambda_ready", 1)

        def quad(t, i, n=4):
            return t[:, n * i:n * i + n, :]

        def odd_conv(dve, n, taps):
            for i in taps:
                j = CONV - 1 - i
                for b in (2 * n, 2 * n + 1):
                    view, tap = x_raw[:, b, j:j + T], par[:, COLS["conv_w"][0] + KT * j + b:COLS["conv_w"][0] + KT * j + b + 1]
                    if i == 0:
                        ins = dve.tensor_scalar(conv[:, b, :], view, tap, pcol("conv_b", b), ALU.mult, ALU.add)
                    else:
                        ins = dve.scalar_tensor_tensor(conv[:, b, :], view, tap, conv[:, b, :], ALU.mult, ALU.add)
                    ins.then_inc(sem("conv_step"), 1)
                once(dve, "conv_step", 8 * n + 2 * i + 2)

        def odd_gate_banks(v, n):
            b = v % 2
            return (tp[2 * b], tp[2 * b + 1]) if n % 2 == 0 else (acc[2 - 2 * b], acc[3 - 2 * b])

        def odd_gates_pe(pe, v, n):
            once(pe, "conv_step", 8 * n + 8)
            once(pe, f"gate_w_landed{n % 2}", 32 * (n // 2 + 1))
            if n % 2 == 0:
                once(pe, "z_ready", ODD_Z + 2 * (v - 1))
            else:
                once(pe, "stg_written", 2 * (ODD_STG + v))
            for i in range(2):
                for jh in range(2):
                    for ih in range(2):
                        last = nc.tensor.matmul(odd_gate_banks(v, n)[i][:, jh * T:(jh + 1) * T],
                                                gate_w[:, n % 2, i, ih, jh * P:(jh + 1) * P],
                                                conv[:, 2 * n + ih, :], start=(ih == 0), stop=(ih == 1))
            last.then_inc(sem("gates_done"), 1)

        def odd_gates_act(act, v, n):
            once(act, "gates_done", n + 1)
            for i, (t, bias) in enumerate(((gate_x, "gx_b"), (gate_a, "ga_b"))):
                for jh in range(2):
                    act.activation(t[:, 2 * n + jh, :], odd_gate_banks(v, n)[i][:, jh * T:(jh + 1) * T], ACT.Sigmoid,
                                   bias=pcol(bias, 2 * n + jh)).then_inc(sem("gates_read"), 1)

        def load_gate_w(sp, n):
            if n >= 2:
                once(sp, "gates_done", n - 1)
            for i, w in enumerate((gx_w, ga_w)):
                sp.dma_start(gate_w[:, n % 2, i, :, :], w[n].rearrange("(i p) j -> p i j", p=P))\
                   .then_inc(sem(f"gate_w_landed{n % 2}"), 16)

        def odd_product(role, eng, k):
            a, c = ((hidA_hi, hidA_lo) if k < 2 else (hidB_hi, hidB_lo)), 4 * (k % 2)
            if role == "pool":
                once(eng, "scanned", k + 1)
                once(eng, "z_ready", ODD_Z + 8 + 2 * (k + 1))
                eng.tensor_tensor(quad(gate_t, k), quad(gate_t, k), x_raw[:, 4 * k:4 * k + 4, CONV - 1:], ALU.mult)\
                   .then_inc(sem("odd_mixed"), 1)
            elif role == "act":
                once(eng, *(("root_in", k + 3) if k < 2 else ("scanned", k + 1)))
                once(eng, "odd_mixed", k + 1)
                eng.activation(a[0][:, c:c + 4, :], quad(gate_t, k), ACT.Copy).then_inc(sem("odd_hi"), 1)
            elif role == "dve":
                once(eng, "odd_hi", k + 1)
                eng.tensor_tensor(a[1][:, c:c + 4, :], quad(gate_t, k), a[0][:, c:c + 4, :], ALU.subtract)\
                   .then_inc(sem("odd_split"), 1)

        def odd_decays(act, k):
            once(act, "bx_ready", k + 1)
            for t, func, name in ((conv, ACT.Exp, "decays_ready"), (gate_t, ACT.Tanh, "tangents_ready")):
                for kt in range(4 * k, 4 * k + 4):
                    act.activation(t[:, kt, :], gate_a[:, kt, :], func, scale=lam[:, 5, kt:kt + 1]).then_inc(sem(name), 1)

        def odd_roots(act, k):
            once(act, "root_in", k + 1)
            act.activation(quad(gate_t, k), quad(gate_t, k), ACT.Sqrt, scale=-1.0).then_inc(sem("roots_ready"), 1)

        def odd_root_input(dve, k):
            once(dve, "squares_ready", k + 1)
            dve.scalar_tensor_tensor(quad(gate_t, k), quad(gate_a, k), 1.0, quad(gate_t, k), ALU.add, ALU.mult)\
               .then_inc(sem("root_in"), 1)
            dve.memset(quad(conv, k)[:, :, 0:1], 0.0).then_inc(sem("restarts_set"), 1)

        def odd_scan(dve, k):
            once(dve, "inputs_ready", k + 1)
            once(dve, "restarts_set", k + 1)
            flat = lambda t: quad(t, k).rearrange("p c t -> p (c t)")
            dve.tensor_tensor_scan(flat(gate_t), flat(conv), flat(gate_x), 0.0, ALU.mult, ALU.add).then_inc(sem("scanned"), 1)

        def odd_pool(pool):
            def bx(k):
                once(pool, "gates_read", 8 * (k + 1))
                pool.tensor_tensor(quad(gate_x, k), quad(gate_x, k), quad(conv, k), ALU.mult).then_inc(sem("bx_ready"), 1)

            for k in range(4):
                bx(k)
                once(pool, "decays_ready", 4 * k + 4)
                once(pool, "tangents_ready", 4 * k + 4)
                pool.tensor_tensor(quad(gate_a, k), quad(conv, k), quad(conv, k), ALU.mult).then_inc(sem("squares_ready"), 1)
                once(pool, "roots_ready", k + 1)
                pool.tensor_tensor(quad(gate_x, k), quad(gate_x, k), quad(gate_t, k), ALU.mult).then_inc(sem("inputs_ready"), 1)
                if k == 3:
                    odd_product("pool", pool, 0)
                    odd_product("pool", pool, 1)
            for k in (2, 3):
                odd_product("pool", pool, k)

        def odd_side(v):
            def side(role, eng, j):
                if role == "dve":
                    if v == 2 and j == 0:
                        eng.memset(x_raw[:, :, 0:CONV - 1], 0.0).then_inc(sem("odd_zeroed"), 1)
                        once(eng, "odd_zeroed", 1)
                    if v <= 5 and j in (0, 1, 3, 4):
                        once(eng, "z_ready", ODD_Z + 2 * (v - 1))
                        odd_conv(eng, 2 * (v - 2) + j // 3, (0, 1) if j % 3 == 0 else (2, 3))
                    if 4 <= v <= 7 and j == 6 - (v == 7):
                        odd_root_input(eng, v - 4)
                    if 5 <= v <= 7 and j == 2:
                        odd_scan(eng, v - 5)
                    if v == 7 and j == 7:
                        odd_scan(eng, 3)
                    if v == 8 and j in (0, 1, 3, 6):
                        odd_product("dve", eng, (0, 1, 3, 6).index(j))
                elif role == "act":
                    if 3 <= v <= 6 and j == 7:
                        for n in (2 * (v - 3), 2 * (v - 3) + 1):
                            odd_gates_act(eng, v, n)
                    if 4 <= v <= 7 and j == 3:
                        odd_decays(eng, v - 4)
                    if 5 <= v <= 7 and j == 0:
                        odd_roots(eng, v - 5)
                    if v == 7 and j == 6:
                        odd_roots(eng, 3)
                    if v == 7 and j == 7:
                        odd_product("act", eng, 0)
                    if v == 8 and j in (0, 1, 6):
                        odd_product("act", eng, (0, 1, 6).index(j) + 1)
                elif role == "pe":
                    if 3 <= v <= 6 and j in (1, 4):
                        odd_gates_pe(eng, v, 2 * (v - 3) + j // 4)
                elif role == "sp":
                    if v == 2 and j in (0, 1):
                        load_gate_w(eng, j)
                    if 3 <= v <= 5 and j == 6 or 4 <= v <= 6 and j == 1:
                        load_gate_w(eng, 2 * (v - 2) if j == 6 else 2 * (v - 3) + 1)
            return side

        C_ODD_OUT = dict(C_ODD, n=C_ODD["n"] + 8, tused=[t + 4 for t in C_ODD["tused"]])
        C_MLP1 = dict(n=C_ODD["n"] + 12, tused=[t + 6 for t in C_ODD["tused"]], stg=C_ODD["stg"] + 8, hid=C_ODD["hid"],
                      xu=C_ODD["xu"] + 4, xs=C_ODD["xs"] + 4, thi=C_ODD["thi"] + 16, lhs=C_ODD["lhs"] + 16,
                      norm=C_ODD["norm"] + 1)
        C_END = after_mlp(C_MLP1, None)

        def odd_layer(role, eng, prev):
            for v in range(8):
                branch_step(role, eng, v, prev)
                prev = branch(v)
                if role == "pool" and v == 1:
                    odd_pool(eng)
            return out_projection(role, eng, C_ODD_OUT, od_w_out, "ff_norm1",
                                  free=lambda k: (stg_written, 2 * (ODD_STG + 7 + k)), tp_first=(z_ready, ODD_Z + 16),
                                  need=lambda pe, j: once(pe, "odd_split", j // 2 + 1), prev=prev, side=odd_side(8))

        tables_landed = sem("tables_landed")
        out_ready, out_stored = sem("out_ready"), sem("out_stored")
        gain_landed = sem("gain_landed")
        gain_row = stg[:, :, :, :].rearrange("p a h n -> p (a h n)")

        def program(role, eng):
            posts = load_posts("ev_norm")
            for p in posts[:-1]:
                finish(role, eng, p)
            even_in(role, eng, posts[-1])
            rwkv(role, eng)
            retention(role, eng)
            prev = out_projection(role, eng, C_EVEN_OUT, ev_w_out, "ff_norm0", free=lambda k: None, tp_first=None,
                                  need=even_mixed)
            prev = mlp(role, eng, 0, C_MLP0, prev, "od_norm")
            prev = odd_layer(role, eng, prev)
            prev = mlp(role, eng, 1, C_MLP1, prev, None)
            finish(role, eng, prev)

        block = ctx.enter_context(nc.Block())

        @block.sync
        def _(sp):
            for dst, src in ((con[:, :], consts), (par[:, :], params)):
                sp.dma_start(dst, src).then_inc(tables_landed, 16)
            for h in range(HALVES):
                sp.dma_start(x[:, h, :], x_in[h * P:(h + 1) * P, :]).then_inc(x_landed, 16)
            program("sp", sp)
            sp.wait_ge(squared, C_END["hid"])
            sp.wait_ge(t_done[0], C_END["tused"][0])
            sp.wait_ge(t_done[1], C_END["tused"][1])
            sp.dma_start(gain_row, final_norm.rearrange("(a n) -> a n", a=1).broadcast_to((P, D))).then_inc(gain_landed, 16)
            for k in range(4):
                for h in range(HALVES):
                    sp.wait_ge(out_ready, HALVES * k + h + 1)
                    sp.dma_start(out[h * P:(h + 1) * P, k * WIDE:(k + 1) * WIDE],
                                 x[:, h, k * WIDE:(k + 1) * WIDE]).then_inc(out_stored, 16)
            sp.wait_ge(out_stored, 16 * 4 * HALVES)

        @block.gpsimd
        def _(pool):
            program("pool", pool)

        @block.scalar
        def _(act):
            act.wait_ge(tables_landed, 32)
            prepare_lambda("act", act)
            program("act", act)

        @block.vector
        def _(dve):
            rwkv_zero(dve)
            dve.wait_ge(tables_landed, 32)
            prepare_lambda("dve", dve)
            program("dve", dve)
            dve.wait_ge(rstd_ready, C_END["norm"])
            dve.wait_ge(gain_landed, 16)
            for k in range(4):
                for h in range(HALVES):
                    xs = x[:, h, k * WIDE:(k + 1) * WIDE]
                    dve.scalar_tensor_tensor(xs, xs, rstd[:, h:h + 1], gain_row[:, k * WIDE:(k + 1) * WIDE],
                                             ALU.mult, ALU.mult).then_inc(out_ready, 1)

        @block.tensor
        def _(pe):
            pe.wait_ge(tables_landed, 32)
            program("pe", pe)


def const_table():
    import numpy as np
    i = np.arange(P)
    same = (i[:, None] // CHUNK) == (i[None, :] // CHUNK)
    t = i % CHUNK
    cols = [np.eye(P), same]
    for l in range(LEVELS):
        cols.append(same & ((t[:, None] >> (l + 1)) == (t[None, :] >> (l + 1))) & (((t[:, None] >> l) & 1) == 1)
                    & (((t[None, :] >> l) & 1) == 0))
    cols.append(same & (t[None, :] > t[:, None]))
    cols.append(np.arange(CHUNK)[None, :] >= t[:, None])
    cols.append(np.broadcast_to(np.arange(T)[None, :] % CHUNK != 0, (P, T)))
    return np.concatenate([np.asarray(c, np.float32) for c in cols], axis=1)


def position_tables():
    import numpy as np
    half = 128
    inv = 1.0 / (np.float32(10000.0) ** (np.arange(0, 2 * half, 2, dtype=np.float32) / np.float32(2 * half)))
    ang = (np.arange(T, dtype=np.float32)[:, None] * inv.astype(np.float32)[None, :]).astype(np.float32)
    cossin = np.stack([np.cos(ang), np.sin(ang)], axis=1).astype(np.float32)
    lg = np.log1p(-np.exp2(-5.0 - np.arange(RET_HEADS, dtype=np.float64)))
    n, m = np.arange(T)[None, :], np.arange(T)[:, None]
    seen = (m // CHUNK) <= (n // CHUNK)
    decay = np.where(seen[None], np.exp(lg[:, None, None] * np.abs(n - m)[None]), 0.0) / 16.0
    return cossin, decay.astype(np.float32)


def kernel(**inputs):
    import numpy as np
    import concourse.bacc as bacc
    from concourse.bass_utils import run_bass_kernel_spmd

    a = {k: np.ascontiguousarray(v) for k, v in inputs.items()}

    def blocks(v, n):
        flat = np.zeros((n, P), np.float32)
        flat.reshape(-1)[:v.size] = v.reshape(-1)
        return flat.T

    table = dict(mu=a["rw_mu"], w0=a["rw_w0"], a0=a["rw_a0"], k_k=a["rw_k_k"], k_a=a["rw_k_a"], r_k=a["rw_r_k"],
                 lnx_w=a["rw_lnx_w"], lnx_b=a["rw_lnx_b"], ev_norm=a["ev_norm"], ff_norm0=a["ff_norm"][0],
                 od_norm=a["od_norm"], ff_norm1=a["ff_norm"][1], conv_w=a["od_conv_w"], conv_b=a["od_conv_b"],
                 gx_b=a["od_gx_b"], ga_b=a["od_ga_b"], lam=a["od_lam"])
    params = np.ascontiguousarray(np.concatenate([blocks(table[k], n) for k, (_, n) in COLS.items()], axis=1))
    cossin, rdecay = position_tables()
    arrays = {
        "x_in": a["x"][0], "params": params, "consts": const_table(), "cossin": cossin, "rdecay": rdecay,
        "ev_w_in": a["ev_w_in"][0], "ev_w_out": a["ev_w_out"][0], "rw_w2": a["rw_w2"][0], "rw_a2": a["rw_a2"][0],
        "rw_g2": a["rw_g2"][0], "od_w_in": a["od_w_in"][0], "gx_w": a["od_gx_w"][0], "ga_w": a["od_ga_w"][0],
        "od_w_out": a["od_w_out"][0], "ff_w1": a["ff_w1"], "ff_w2": a["ff_w2"], "final_norm": a["final_norm"],
    }
    nc = bacc.Bacc("TRN2", target_bir_lowering=False, num_devices=1)
    args = {k: nc.dram_tensor(f"in_{k}", v.shape, mybir.dt.from_np(v.dtype), kind="ExternalInput").ap()
            for k, v in arrays.items()}
    out = nc.dram_tensor("out", (T, D), F32, kind="ExternalOutput").ap()
    trunk(nc, **args, out=out)
    r = run_bass_kernel_spmd(nc, [{f"in_{k}": v for k, v in arrays.items()}], core_ids=[0])
    return r.results[0]["out"].reshape(1, T, D)
```

```python
from contextlib import ExitStack

import concourse.bass as bass
from concourse import mybir

ALU = mybir.AluOpType
ACT = mybir.ActivationFunctionType
AX_X = mybir.AxisListType.X
F32 = mybir.dt.float32
F32R = mybir.dt.float32r

P = 128
T = 256
HALVES = T // P
D = 2048
KT = D // P
WIDE = 512
UNITS = 8
KU = KT // UNITS
RING = 4
CHUNK = 64
NCHUNK = T // CHUNK
RET_W = 1024
RET_HEADS = 4
RW_BLOCKS = 8
LEVELS = 6
CONV = 4
SLAB = 212832
LORA_W = 288
FF = 8192
QUARTERS = FF // D
NORM_EPS = 1e-6
RET_EPS = 1e-5
RW_EPS = 64e-5
DECAY_C = 0.6065306597126334
LRU_C = 8.0
LRU_BLOCKS = 8

COLS = {}
for _name, _n in (("mu", 27), ("w0", 8), ("a0", 8), ("k_k", 8), ("k_a", 8), ("r_k", 8), ("lnx_w", 8), ("lnx_b", 8),
                  ("ev_norm", 16), ("ff_norm0", 16), ("od_norm", 16), ("ff_norm1", 16), ("conv_w", 64),
                  ("conv_b", 16), ("gx_b", 16), ("ga_b", 16), ("lam", 16)):
    COLS[_name] = (sum(n for _, n in COLS.values()), _n)
NPAR = sum(n for _, n in COLS.values())
CIDENT, CONES, CLEVEL, CSTRICT, CINCL, CSEG = 0, 128, 256, 256 + 128 * LEVELS, 384 + 128 * LEVELS, 448 + 128 * LEVELS
NCONST = CSEG + 256


def trunk(nc, x_in, params, consts, cossin, rdecay, ev_w_in, ev_w_out, rw_w2, rw_a2, rw_g2, od_w_in, gx_w, ga_w,
          od_w_out, ff_w1, ff_w2, final_norm, out):
    ctx = ExitStack()
    with ctx:
        def sb(name, shape, dt=F32, scope=ctx):
            return scope.enter_context(nc.sbuf_tensor(name, shape, dt))

        sems = {}

        def sem(name):
            if name not in sems:
                sems[name] = ctx.enter_context(nc.semaphore(name))
            return sems[name]

        def nbytes(shape):
            n = 4
            for v in shape[1:]:
                n *= v
            return -(-n // 32) * 32

        slab_start = -(-nc.sbuf_base // 32) * 32
        slab = sb("slab", [P, SLAB // 4])

        class Region:
            def __init__(self, at):
                self.at = at

            def __call__(self, name, shape, dt=F32):
                t = nc.alloc_sbuf_tensor_at(name, shape, dt, offset=slab_start + self.at)
                self.at += nbytes(shape)
                assert self.at <= SLAB, (name, self.at)
                return t

        lasting = Region(0)
        x = lasting("x", [P, HALVES, D])
        xT_hi = lasting("xT_hi", [P, KT, T], F32R)
        xT_lo = lasting("xT_lo", [P, KT, T], F32R)
        raw = lasting("raw", [P, RING, KU, WIDE])
        w_hi = lasting("w_hi", [P, RING, KU, WIDE], F32R)
        w_lo = lasting("w_lo", [P, RING, KU, WIDE], F32R)
        par = lasting("par", [P, NPAR])
        con = lasting("con", [P, NCONST])
        ssq = lasting("ssq", [P, 4, HALVES])
        rstd = lasting("rstd", [P, HALVES])
        lam = lasting("lam", [P, 6, KT])
        stg = lasting("stg", [P, 2, HALVES, WIDE])
        junk = lasting("junk", [P, WIDE])
        ident = con[:, CIDENT:CIDENT + P]
        HALF = KT // 2 * T * 4

        low = lasting.at
        at_a = Region(low)
        hidA_hi, hidA_lo = (at_a(n, [P, KT // 2, T], F32R) for n in ("hidA_hi", "hidA_lo"))
        at_b = Region(low + 4 * HALF)
        hidB_hi, hidB_lo = (at_b(n, [P, KT // 2, T], F32R) for n in ("hidB_hi", "hidB_lo"))
        early = Region(low)
        ret_tok = early("ret_tok", [P, 8, HALVES, WIDE])
        z = early("z", [P, 3 * RW_BLOCKS, T])
        rw = Region(early.at)
        lora_in = rw("lora_in", [P, 4, T])
        lora_w = rw("lora_w", [P, 3, P])
        half_bias = rw("half_bias", [P, 2, RW_BLOCKS])
        rw_matrices = rw.at

        def diagonal(name):
            return rw(name, [P, NCHUNK, P])

        v_bd, beta_bd, key_bd, kappa_bd = (diagonal(n) for n in ("v_bd", "beta_bd", "key_bd", "kappa_bd"))
        v_tok, key_tok, beta_tok = (diagonal(n) for n in ("v_tok", "key_tok", "beta_tok"))
        level_a, inv_t, seen_v = (diagonal(n) for n in ("level_a", "inv_t", "seen_v"))
        seen_y = rw("seen_y", [P, 2, NCHUNK, CHUNK])
        state = rw("state", [P, 2, P])
        scaled, rhs_u, u_bd = (rw(n, [P, P]) for n in ("scaled", "rhs_u", "u_bd"))
        decay = rw("decay", [P, NCHUNK, CHUNK + 1])
        decay_end = rw("decay_end", [P, NCHUNK])
        extra = rw("extra", [P, 4, T])
        rt = Region(rw_matrices)
        qT, kT = rt("qT", [P, 8, T]), rt("kT", [P, 8, T])
        table_d = rt("table_d", [P, RET_HEADS, HALVES, T])
        scores = rt("scores", [P, 2, HALVES, T])
        rstat, rmean, rdev = (rw("rstat", [P, HALVES, 6]), rw("rmean", [P, RET_HEADS, HALVES, 2]),
                              rw("rdev", [P, RET_HEADS, HALVES]))
        od_a = Region(low)
        gate_a = od_a("gate_a", [P, KT, T])
        od_b = Region(low + 4 * HALF)
        gate_x = od_b("gate_x", [P, KT, T])
        x_rest = Region(low + 2 * HALF)
        conv = x_rest("conv", [P, KT, T])
        x_raw = od_b("x_raw", [P, KT, T + CONV - 1])
        gate_w = od_b("gate_w", [P, 2, 2, 2, T])
        gate_t = od_b("gate_t", [P, KT, T])

        acc = [ctx.enter_context(nc.psum_tensor(f"acc{i}", [P, WIDE], F32)) for i in range(4)]
        tp = [ctx.enter_context(nc.psum_tensor(f"tp{i}", [P, WIDE], F32)) for i in range(4)]

        def pcol(name, k):
            return par[:, COLS[name][0] + k:COLS[name][0] + k + 1]

        def xT(kt):
            return xT_hi[:, kt, :], xT_lo[:, kt, :]

        def hid(kt):
            a, b = (hidA_hi, hidA_lo) if kt < KT // 2 else (hidB_hi, hidB_lo)
            return a[:, kt % (KT // 2), :], b[:, kt % (KT // 2), :]

        raw_landed = [sem(f"raw_landed{i}") for i in range(RING)]
        hi_ready, lo_ready, unit_used = sem("hi_ready"), sem("lo_ready"), sem("unit_used")
        t_done = [sem("t_done0"), sem("t_done1")]
        x_landed = [sem(f"x_landed{k}") for k in range(4)]
        x_updated, ssq_done = sem("x_updated"), sem("ssq_done")
        stg_written, squared, t_hi, lhs_ready, z_ready = (sem("stg_written"), sem("squared"), sem("t_hi"),
                                                         sem("lhs_ready"), sem("z_ready"))
        var_ready, std_ready, rstd_ready = sem("var_ready"), sem("std_ready"), sem("rstd_ready")

        def wait_count(eng, s, value):
            if not isinstance(value, int) or value > 0:
                eng.wait_ge(s, value)

        def load_unit(sp, n, j, w, row0, col0, wide=WIDE):
            wait_count(sp, lo_ready, 8 * n + j - RING + 1)
            src = w[bass.ds(row0 + j * KU * P, KU * P), bass.ds(col0, wide)].rearrange("(k p) n -> p k n", p=P)
            sp.dma_start(raw[:, j % RING, :, 0:wide], src).then_inc(raw_landed[j % RING], 16)

        def split_hi(act, n, j, wide=WIDE):
            act.wait_ge(raw_landed[j % RING], 16 * (2 * n + j // RING + 1))
            wait_count(act, unit_used, 8 * n + j - RING + 1)
            act.activation(w_hi[:, j % RING, :, 0:wide], raw[:, j % RING, :, 0:wide], ACT.Copy).then_inc(hi_ready, 1)

        def split_lo(dve, n, j, wide=WIDE):
            dve.wait_ge(hi_ready, 8 * n + j + 1)
            dve.tensor_tensor(w_lo[:, j % RING, :, 0:wide], raw[:, j % RING, :, 0:wide],
                              w_hi[:, j % RING, :, 0:wide], ALU.subtract).then_inc(lo_ready, 1)

        def multiply_part(pe, n, part, lhs, bank, wide=WIDE):
            j, kt, h = part // 4, part // 2, part % 2
            if part % 4 == 0:
                pe.wait_ge(lo_ready, 8 * n + j + 1)
            hi, lo = lhs(kt)
            o, tok = acc[2 * bank + h][:, 0:wide], slice(h * P, (h + 1) * P)
            wh, wl = w_hi[:, j % RING, kt % KU, 0:wide], w_lo[:, j % RING, kt % KU, 0:wide]
            nc.tensor.matmul(o, hi[:, tok], wh, start=(kt == 0), stop=False)
            nc.tensor.matmul(o, hi[:, tok], wl, start=False, stop=False)
            last = nc.tensor.matmul(o, lo[:, tok], wh, start=False, stop=(kt == KT - 1))
            if part % 4 == 3:
                last.then_inc(unit_used, 1)

        def multiply_unit(pe, n, j, lhs, bank, wide=WIDE):
            for part in range(4 * j, 4 * j + 4):
                multiply_part(pe, n, part, lhs, bank, wide)

        def sp_group(sp, g, w, row0, col0, side=None):
            for j in range(UNITS):
                row = row0 + (D // 2 if j < UNITS // 2 else -(D // 2)) if g.get("swap") else row0
                load_unit(sp, g["n"], j, w, row, col0, g["wide"])
                if side:
                    side("sp", sp, j)

        def pe_group(pe, g, lhs, prev=None, side=None):
            if g["free"]:
                pe.wait_ge(*g["free"])
            for j in range(UNITS):
                if j == 2 and prev:
                    pe_post(pe, prev)
                if callable(g["need"]):
                    g["need"](pe, j)
                elif g["need"] is not None and j in (0, 6):
                    pe.wait_ge(lhs_ready, g["need"][j // 6])
                multiply_unit(pe, g["n"], j, lhs, g["bank"], g["wide"])
                if side:
                    side("pe", pe, j)

        def act_group(act, g, prev=None, side=None):
            for j in range(UNITS):
                split_hi(act, g["n"], j, g["wide"])
                if j == 2 and prev:
                    act_evacuate(act, prev)
                if j == 5 and prev:
                    act_after_transpose(act, prev)
                if side:
                    side("act", act, j)

        def dve_group(dve, g, prev=None, side=None):
            for j in range(UNITS):
                split_lo(dve, g["n"], j, g["wide"])
                if j == 2 and prev:
                    dve_evacuate(dve, prev)
                if j == 5 and prev:
                    dve_after_transpose(dve, prev)
                if j == 7 and prev:
                    dve_finish_norm(dve, prev)
                if side:
                    side("dve", dve, j)

        def act_evacuate(act, g):
            if g["post"] in ("square", "z"):
                act.wait_ge(unit_used, 8 * (g["n"] + 1))
                act.wait_ge(rstd_ready, g["norm"])
                wait_count(act, t_done[g["bank"]], g["tused"])
                for h in range(HALVES):
                    last = act.activation(stg[:, g["bank"], h, 0:g["wide"]], acc[2 * g["bank"] + h][:, 0:g["wide"]],
                                          g.get("func", ACT.Relu if g["post"] == "square" else ACT.Copy),
                                          scale=rstd[:, h:h + 1])
                    last.then_inc(stg_written, 1)

        def pool_square(pool, g):
            pool.wait_ge(stg_written, 2 * g["stg"] + 2)
            s = stg[:, g["bank"], :, :]
            pool.tensor_tensor(s, s, s, ALU.mult).then_inc(squared, 1)

        def pe_post(pe, g):
            b = g["bank"]
            if g["post"] == "x":
                if not g["transposed"]:
                    return
                if g.get("loaded"):
                    pe.wait_ge(x_landed[g["col"] // WIDE], 16)
                else:
                    pe.wait_ge(x_updated, g["xu"] + 1)
                src = lambda h, c: x[:, h, g["col"] + c * P:g["col"] + (c + 1) * P]
            else:
                if g["post"] == "square":
                    pe.wait_ge(squared, g["hid"] + 1)
                else:
                    pe.wait_ge(stg_written, 2 * g["stg"] + 2)
                src = lambda h, c: stg[:, b, h, c * P:min((c + 1) * P, g["wide"])]
            if g["tp"]:
                pe.wait_ge(*g["tp"])
            for c in range(-(-g["wide"] // P)):
                for h in range(HALVES):
                    s = src(h, c)
                    last = nc.tensor.transpose(tp[2 * b + c // 2][0:s.shape[1], (c % 2) * T + h * P:(c % 2) * T + (h + 1) * P],
                                               s, ident)
            last.then_inc(t_done[b], 1)

        def act_squares(act, g, col):
            for h in range(HALVES):
                if g.get("loaded"):
                    act.wait_ge(x_landed[col // WIDE], 16)
                else:
                    act.wait_ge(x_updated, g["xu"] + 1)
                wait_count(act, ssq_done, HALVES * g["xs"] + h)
                act.activation(junk[:, :], x[:, h, col:col + WIDE], ACT.Square,
                               accum_out=ssq[:, col // WIDE, h:h + 1]).then_inc(ssq_done, 1)

        def act_deviation_of_x(act, g):
            act.wait_ge(var_ready, 2 * g["norm"])
            act.activation(rstd[:, :], rstd[:, :], ACT.Sqrt).then_inc(std_ready, 1)

        def dve_variance_of_x(dve, g):
            dve.wait_ge(ssq_done, HALVES * (g["xs"] + 1))
            dve.tensor_reduce(rstd[:, :], ssq[:, :, :].rearrange("p g h -> p h g"), AX_X, ALU.add).then_inc(var_ready, 1)
            dve.wait_ge(var_ready, 2 * g["norm"] - 1)
            dve.tensor_scalar(rstd[:, :], rstd[:, :], 1.0 / D, NORM_EPS, ALU.mult, ALU.add).then_inc(var_ready, 1)

        def act_after_transpose(act, g):
            b = g["bank"]
            if g["post"] == "x" and g.get("summed", True):
                if not g.get("loaded"):
                    act_squares(act, g, g["col"])
                if g["transposed"]:
                    act.wait_ge(t_done[b], g["tused"] + 1)
                    for c in range(4):
                        kt = g["col"] // P + c
                        act.activation(xT_hi[:, kt, :], tp[2 * b + c // 2][:, (c % 2) * T:(c % 2 + 1) * T], ACT.Copy,
                                       scale=pcol(g["gain"], kt)).then_inc(t_hi, 1)
                if g["col"] == 3 * WIDE and not g.get("loaded"):
                    act_deviation_of_x(act, g)
            if g["post"] == "square":
                act.wait_ge(t_done[b], g["tused"] + 1)
                for c in range(2):
                    t = (hidA_hi if g["g"] < 2 else hidB_hi)[:, (4 * g["g"] + 2 * c) % 8:(4 * g["g"] + 2 * c) % 8 + 2, :]
                    act.activation(t, tp[2 * b + c][:, :].rearrange("p (c t) -> p c t", c=2), ACT.Copy).then_inc(t_hi, 1)

        def dve_evacuate(dve, g):
            if g["post"] == "x" and not g.get("loaded"):
                dve.wait_ge(unit_used, 8 * (g["n"] + 1))
                for h in range(HALVES):
                    xs = x[:, h, g["col"]:g["col"] + WIDE]
                    last = dve.tensor_tensor(xs, acc[2 * g["bank"] + h][:, :], xs, ALU.add)
                last.then_inc(x_updated, 1)

        def dve_after_transpose(dve, g):
            b = g["bank"]
            if g["post"] == "x":
                if g["transposed"]:
                    for c in range(4):
                        kt = g["col"] // P + c
                        dve.wait_ge(t_hi, g["thi"] + 2 * (c // 2) + 2)
                        last = dve.scalar_tensor_tensor(xT_lo[:, kt, :], tp[2 * b + c // 2][:, (c % 2) * T:(c % 2 + 1) * T],
                                                        pcol(g["gain"], kt), xT_hi[:, kt, :], ALU.mult, ALU.subtract)
                        last.then_inc(lhs_ready, 1)
                if g["col"] == 3 * WIDE and g.get("summed", True) and not g.get("loaded"):
                    dve_variance_of_x(dve, g)
            if g["post"] == "square":
                for c in range(2):
                    k = (4 * g["g"] + 2 * c) % 8
                    a, l = (hidA_hi, hidA_lo) if g["g"] < 2 else (hidB_hi, hidB_lo)
                    dve.wait_ge(t_hi, g["thi"] + c + 1)
                    dve.tensor_tensor(l[:, k:k + 2, :], tp[2 * b + c][:, :].rearrange("p (c t) -> p c t", c=2),
                                      a[:, k:k + 2, :], ALU.subtract).then_inc(lhs_ready, 1)
            if g["post"] == "z":
                for c in range(-(-g["wide"] // (2 * P))):
                    dve.wait_ge(t_done[b], g["tused"] + 1)
                    g["move"](dve, c, tp[2 * b + c]).then_inc(z_ready, 1)

        def dve_finish_norm(dve, g, late=False):
            if g["post"] == "x" and g["col"] == 3 * WIDE and g.get("summed", True) and (late or not g.get("loaded")):
                dve.wait_ge(std_ready, g["norm"])
                dve.reciprocal(rstd[:, :], rstd[:, :]).then_inc(rstd_ready, 1)

        def step(role, eng, g, w, row0, col0, lhs, prev, side=None):
            if role == "sp":
                sp_group(eng, g, w, row0, col0, side)
            elif role == "pe":
                pe_group(eng, g, lhs, prev, side)
            elif role == "act":
                act_group(eng, g, prev, side)
            elif role == "dve":
                dve_group(eng, g, prev, side)
            elif prev and prev["post"] == "square":
                pool_square(eng, prev)

        def finish(role, eng, prev):
            if role == "pe":
                pe_post(eng, prev)
            elif role == "act":
                act_evacuate(eng, prev)
                act_after_transpose(eng, prev)
            elif role == "dve":
                dve_evacuate(eng, prev)
                dve_after_transpose(eng, prev)
                dve_finish_norm(eng, prev)
            elif role == "pool" and prev["post"] == "square":
                pool_square(eng, prev)

        def load_posts(gain):
            return [dict(post="x", loaded=True, transposed=True, gain=gain, col=k * WIDE, bank=k % 2, wide=WIDE,
                         tused=k // 2, tp=(lhs_ready, 4 * (k - 1)) if k > 1 else None, xu=0, xs=k, thi=4 * k,
                         lhs=4 * k, norm=1) for k in range(4)]

        def residual(c, k, gain, q=0, last=True):
            return dict(n=c["n"] + k, bank=k % 2, post="x", col=k * WIDE, transposed=last and gain is not None, gain=gain,
                        summed=last, wide=WIDE, tused=c["tused"][k % 2] + k // 2, xu=c["xu"] + k, xs=c["xs"] + k,
                        thi=c["thi"] + 4 * k, lhs=c["lhs"] + 4 * k, tp=(lhs_ready, c["lhs"] + 4 * max(k - 1, 0)),
                        norm=c["norm"] + 1)

        def mlp_group(c, q, g, gain):
            n, lhs0 = c["n"] + 8 * q, c["lhs"] + 8 * q
            if g < 4:
                free = (x_updated, c["xu"] + 4 * (q - 1) + g + 3) if g < 2 else (stg_written, 2 * (c["stg"] + 4 * q + g - 1))
                return dict(n=n + g, bank=g % 2, post="square", g=g, wide=WIDE, free=free, need=(c["lhs"] - 4, c["lhs"]),
                            tused=c["tused"][g % 2] + 2 * q + g // 2, stg=c["stg"] + 4 * q + g, hid=c["hid"] + 4 * q + g,
                            thi=c["thi"] + 8 * q + 2 * g, lhs=lhs0 + 2 * g, tp=(lhs_ready, lhs0 + 2 * max(g - 1, 0)),
                            norm=c["norm"])
            k, last = g - 4, isinstance(q, int) and q == QUARTERS - 1
            at = dict(n=n + 4, tused=[t + 2 * q + 2 for t in c["tused"]], xu=c["xu"] + 4 * q, xs=c["xs"], thi=c["thi"] + 8 * q + 8,
                      lhs=lhs0 + 8, norm=c["norm"])
            r = residual(at, k, gain, last=last)
            r["free"] = (stg_written, 2 * (c["stg"] + 4 * q + g - 1)) if k < 2 else (x_updated, at["xu"] + k - 1)
            r["need"] = (lhs0 + 6, lhs0 + 8)
            return r

        def mlp(role, eng, layer, c, prev, gain):
            w1, w2 = ff_w1[layer], ff_w2[layer]

            def part(q, g, prev):
                if g < 4:
                    step(role, eng, mlp_group(c, q, g, gain), w1, 0, q * D + g * WIDE, xT, prev)
                else:
                    step(role, eng, mlp_group(c, q, g, gain), w2, q * D, (g - 4) * WIDE, hid, prev)

            part(0, 0, prev)
            with eng.Fori(0, QUARTERS - 1) as q:
                for g in range(1, 8):
                    part(q, g, mlp_group(c, q, g - 1, gain))
                part(q + 1, 0, mlp_group(c, q, 7, gain))
            for g in range(1, 8):
                part(QUARTERS - 1, g, mlp_group(c, QUARTERS - 1, g - 1, gain))
            return mlp_group(c, QUARTERS - 1, 7, gain)

        def after_mlp(c, gain):
            t = 4 if gain else 0
            return dict(n=c["n"] + 32, tused=[v + 8 + t // 2 for v in c["tused"]], stg=c["stg"] + 16, hid=c["hid"] + 16,
                        xu=c["xu"] + 16, xs=c["xs"] + 4, thi=c["thi"] + 32 + 4 * t, lhs=c["lhs"] + 32 + 4 * t,
                        norm=c["norm"] + 1)

        z_lora = extra

        def tile(t, i):
            return t[:, i // 4, (i // 2) % 2, (i % 2) * T:(i % 2 + 1) * T]

        out_t, cen_t, csq_t, sq_t, kk_t, b_t, km_t, nrm_t = (tile(stg, i) for i in range(8))
        rho_t, em_t = junk[:, 0:T], junk[:, T:2 * T]
        thw_t, sum_t, iclr_t, bon_t = (extra[:, i, :] for i in range(4))

        def lora_move(dve, c, bank):
            if c == 0:
                return dve.tensor_copy(z_lora[:, 0:2, :], bank[:, :].rearrange("p (c t) -> p c t", c=2))
            return dve.tensor_copy(z_lora[0:32, 2, :], bank[0:32, 0:T])

        LORA = dict(n=0, bank=0, post="z", wide=LORA_W, free=None, need=(12, 16), tused=2, stg=0, norm=1,
                    tp=(lhs_ready, 16), move=lora_move)

        def rkv(i, odd):
            v = 2 * i + odd

            def move(dve, c, bank):
                return dve.tensor_copy(z[:, bass.ds(4 * v + 2 * c, 2), :], bank[:, :].rearrange("p (c t) -> p c t", c=2))

            return dict(n=1 + v, bank=1 - odd, post="z", wide=WIDE, need=None, stg=1 + v, norm=1, move=move,
                        free=None if isinstance(v, int) and v == 0 else (stg_written, 2 * v), tused=2 + odd + i,
                        tp=(z_ready, 2 * v + 2))

        RET_IN = 4 * RET_W

        RET_N, RET_STG = 7, 7

        def once(eng, name, count):
            eng.wait_ge(sem(name), count)

        class Own:

            def __init__(self, eng, name, it=0, per=0):
                self.eng, self.sem, self.base, self.per, self.k = eng, sem(name), it * per, per, 0

            def __call__(self, ins):
                self.k += 1
                ins.then_inc(self.sem, 1)
                self.eng.wait_ge(self.sem, self.base + self.k)

            def end(self):
                assert not self.per or self.k == self.per, self.k

        HEADS = ((slice(0, 64), slice(0, 64)), (slice(64, 128), slice(64, 128)))
        R_BLOCK, K_BLOCK, V_BLOCK = 0, RW_BLOCKS, 2 * RW_BLOCKS

        def chunks(t):
            return t.rearrange("p (c t) -> p c t", c=NCHUNK)

        def in_chunks(t):
            return t.rearrange("p (c n) -> p c n", c=NCHUNK)

        def over_chunks(col, wide=P):
            return con[:, col:col + wide].rearrange("p (o n) -> p o n", o=1).broadcast_to((P, NCHUNK, wide))

        def pcol_at(name, p):
            return par[:, bass.ds(p + COLS[name][0], 1)]

        def z_at(p, block):
            return z[:, bass.ds(p + block, 1), :].rearrange("p o t -> p (o t)")

        def mix_difference(dve, own, dst, src, rows=P):
            dve.tensor_tensor(dst[0:rows, 1:T], src[0:rows, 0:T - 1], src[0:rows, 1:T], ALU.subtract).then_inc(own, 1)
            dve.tensor_scalar(dst[0:rows, 0:1], src[0:rows, 0:1], -1.0, None, ALU.mult).then_inc(own, 1)

        def rwkv_zero(dve):
            for t in (v_bd, beta_bd, key_bd, kappa_bd):
                dve.memset(t[:, :, :], 0.0).then_inc(sem("rw_zeroed"), 1)
            for t in (lora_in[64:128, 0, :], lora_in[0:64, 1, :], lora_in[32:64, 3, :], lora_in[64:128, 3, :],
                      lora_w[32:64, 2, :], lora_w[64:128, 2, :]):
                dve.memset(t, 0.0).then_inc(sem("rw_zeroed"), 1)
            dve.memset(decay[:, :, 0:1], 1.0).then_inc(sem("rw_zeroed"), 1)

        def load_front_lora(pool, p):
            cols = bass.ds(p * P, P)
            pool.dma_start(lora_w[0:64, 0, :], rw_w2[:, cols]).then_inc(sem("front_lora_landed"), 16)
            pool.dma_start(lora_w[64:128, 0, :], rw_a2[:, cols]).then_inc(sem("front_lora_landed"), 16)

        def load_gate_lora(pool, p):
            cols = bass.ds(p * P, P)
            pool.dma_start(lora_w[:, 1, :], rw_g2[0:P, cols]).then_inc(sem("gate_lora_landed"), 16)
            pool.dma_start(lora_w[0:32, 2, :], rw_g2[P:P + 32, cols]).then_inc(sem("gate_lora_landed"), 16)

        def rwkv_prepare_dve(dve):
            for i, name in enumerate(("w0", "a0")):
                c0 = COLS[name][0]
                dve.tensor_scalar(half_bias[:, i, :], par[:, c0:c0 + RW_BLOCKS], 0.5, None, ALU.mult)\
                   .then_inc(sem("half_bias_ready"), 1)
            once(dve, "z_ready", 2)
            rows = (P, P, 32)
            for i, (dst, n) in enumerate(zip((rho_t, em_t, bon_t), rows)):
                mix_difference(dve, sem("lora_difference"), dst, z_lora[:, i, :], n)
            for i, (dst, dif, n) in enumerate(zip((out_t, cen_t, csq_t), (rho_t, em_t, bon_t), rows)):
                once(dve, "lora_difference", 2 * i + 2)
                mu = par[0:n, COLS["mu"][0] + 24 + i:COLS["mu"][0] + 25 + i]
                dve.scalar_tensor_tensor(dst[0:n], dif[0:n], mu, z_lora[0:n, i, :], ALU.mult, ALU.add)\
                   .then_inc(sem("lora_mixed"), 1)

        def rwkv_prepare_act(act):
            once(act, "rw_zeroed", 11)
            once(act, "lora_mixed", 3)
            done = sem("lora_inputs")
            act.activation(lora_in[0:64, 0, :], out_t[0:64], ACT.Tanh).then_inc(done, 1)
            act.activation(lora_in[64:128, 1, :], out_t[64:128], ACT.Copy).then_inc(done, 1)
            act.activation(lora_in[:, 2, :], cen_t, ACT.Sigmoid).then_inc(done, 1)
            act.activation(lora_in[0:32, 3, :], csq_t[0:32], ACT.Sigmoid).then_inc(done, 1)
            once(act, "half_bias_ready", 2)

        def dve_front_mix(dve, q):
            if not isinstance(q, int) or q:
                dve.wait_ge(sem("kappa_ready"), 7 * q)
                dve.wait_ge(sem("bonus_in"), q)
            dif = sem("difference")
            for t, block in ((kk_t, K_BLOCK), (b_t, R_BLOCK), (km_t, V_BLOCK)):
                mix_difference(dve, dif, t, z_at(q, block))
            for i, (t, block) in enumerate(((kk_t, K_BLOCK), (b_t, R_BLOCK), (km_t, V_BLOCK))):
                dve.wait_ge(dif, 6 * q + 2 * i + 2)
                dve.scalar_tensor_tensor(z_at(q, block), t, pcol_at("mu", q + block), z_at(q, block), ALU.mult, ALU.add)\
                   .then_inc(sem("mixed"), 1)

        def dve_front_decay(dve, own, q):
            dve.wait_ge(sem("tanh_ready"), 2 * q + 1)
            own(dve.tensor_scalar(thw_t, thw_t, 1.0, None, ALU.add))
            dve.tensor_tensor_scan(sum_t, con[:, CSEG:CSEG + T], thw_t, 0.0, ALU.mult, ALU.add)\
               .then_inc(sem("log_decay_ready"), 1)
            dve.wait_ge(sem("tanh_ready"), 2 * q + 2)
            own(dve.tensor_scalar(iclr_t, iclr_t, 0.5, 0.5, ALU.mult, ALU.add))

        def dve_front_key(dve, own, q):
            dve.wait_ge(sem("mixed"), 3 * q + 3)
            own(dve.tensor_scalar(km_t, iclr_t, -1.0, pcol_at("k_a", q), ALU.add, ALU.mult))
            own(dve.scalar_tensor_tensor(km_t, km_t, 1.0, z_at(q, K_BLOCK), ALU.add, ALU.mult))

        def dve_front_sum(dve, q, bank=acc[0]):
            dve.wait_ge(sem("kk_sum_done"), q + 1)
            dve.tensor_scalar(nrm_t, bank[:, 0:T], 1e-24, None, ALU.max).then_inc(sem("kk_sum_read"), 1)

        def dve_front_kk(dve, own, q):
            dve.wait_ge(sem("kk_root_ready"), q + 1)
            own(dve.reciprocal(nrm_t, nrm_t))
            own(dve.scalar_tensor_tensor(kk_t, z_at(q, K_BLOCK), pcol_at("k_k", q), nrm_t, ALU.mult, ALU.mult))
            own(dve.tensor_tensor(b_t, kk_t, iclr_t, ALU.mult))
            own.end()

        def dve_front_keys(dve, q):
            dve.wait_ge(sem("decay_ready"), 2 * q + 2)
            for a, b in HEADS:
                dve.tensor_tensor(beta_bd[a, :, b], chunks(b_t[a]), chunks(em_t[a]), ALU.mult).then_inc(sem("kappa_ready"), 1)
            for a, b in HEADS:
                dve.tensor_tensor(key_bd[a, :, b], chunks(km_t[a]), chunks(em_t[a]), ALU.mult).then_inc(sem("kappa_ready"), 1)
            dve.scalar_tensor_tensor(sq_t, z_at(q, R_BLOCK), pcol_at("r_k", q), km_t, ALU.mult, ALU.mult)\
               .then_inc(sem("bonus_in"), 1)

        def dve_front_kappa(dve, q):
            for a, b in HEADS:
                dve.tensor_tensor(kappa_bd[a, :, b], chunks(kk_t[a]), decay[a, :, 0:CHUNK], ALU.mult).then_inc(sem("kappa_ready"), 1)

        def dve_front_rho(dve, q):
            dve.tensor_tensor(chunks(rho_t), chunks(z_at(q, R_BLOCK)), decay[:, :, 1:CHUNK + 1], ALU.mult)\
               .then_inc(sem("kappa_ready"), 1)

        def act_front_square(act, q):
            act.wait_ge(sem("mixed"), 3 * q + 3)
            act.activation(b_t, z_at(q, K_BLOCK), ACT.Square, scale=pcol_at("k_k", q)).then_inc(sem("kk_square"), 1)

        def act_front_tanh(act, q, bank=acc[1]):
            act.wait_ge(sem("lora_done"), q + 1)
            act.activation(thw_t, bank[:, 0:T], ACT.Tanh, scale=0.5,
                           bias=half_bias[:, 0, bass.ds(q, 1)]).then_inc(sem("tanh_ready"), 1)
            act.activation(iclr_t, bank[:, T:2 * T], ACT.Tanh, scale=0.5,
                           bias=half_bias[:, 1, bass.ds(q, 1)]).then_inc(sem("tanh_ready"), 1)

        def act_front_exp(act, q):
            act.wait_ge(sem("log_decay_ready"), q + 1)
            act.activation(decay[:, :, 1:CHUNK + 1], chunks(sum_t), ACT.Exp, scale=-DECAY_C / 2).then_inc(sem("decay_ready"), 1)
            act.activation(em_t, sum_t, ACT.Exp, scale=DECAY_C / 2).then_inc(sem("decay_ready"), 1)

        def act_front_root(act, q):
            act.wait_ge(sem("kk_sum_read"), q + 1)
            act.activation(nrm_t, nrm_t, ACT.Sqrt).then_inc(sem("kk_root_ready"), 1)

        def act_front_v(act, q):
            for a, b in HEADS:
                act.activation(v_bd[a, :, b], chunks(z_at(q, V_BLOCK)[a]), ACT.Copy).then_inc(sem("v_ready"), 1)

        def mm(out, lhsT, rhs, first=True, last=True):
            return nc.tensor.matmul(out, lhsT, rhs, start=first, stop=last)

        ones = con[:, CONES:CONES + P]

        def pe_front_lora(pe, q, bank=acc[1]):
            pe.wait_ge(sem("front_lora_landed"), 32 * (q + 1))
            if not isinstance(q, int) or q:
                pe.wait_ge(sem("tanh_ready"), 2 * q)
            mm(bank[:, 0:T], lora_w[:, 0, :], lora_in[:, 0, :])
            mm(bank[:, T:2 * T], lora_w[:, 0, :], lora_in[:, 1, :]).then_inc(sem("lora_done"), 1)

        def pe_front_sum(pe, q, bank=acc[0]):
            if not isinstance(q, int) or q > 1:
                pe.wait_ge(sem("gated"), q - 1)
            pe.wait_ge(sem("kk_square"), q + 1)
            mm(bank[:, 0:T], ones, b_t).then_inc(sem("kk_sum_done"), 1)

        def pe_mean(pe, n, bank=acc[0]):
            pe.wait_ge(sem("bonus_ready"), n + 1)
            pe.wait_ge(sem("out_copied"), n + 1)
            mm(bank[:, 0:T], ones, out_t).then_inc(sem("mean_done"), 1)

        def pe_variance(pe, n, bank=acc[0]):
            pe.wait_ge(sem("gate_lora_landed"), 32 * (n + 1))
            pe.wait_ge(sem("centred_square"), n + 1)
            mm(bank[:, 0:T], ones, csq_t)
            mm(bank[:, T:2 * T], lora_w[:, 1, :], lora_in[:, 2, :], last=False)
            mm(bank[:, T:2 * T], lora_w[:, 2, :], lora_in[:, 3, :], first=False).then_inc(sem("variance_done"), 1)

        def dve_centre(dve, n, bank=acc[0]):
            dve.wait_ge(sem("mean_done"), n + 1)
            dve.scalar_tensor_tensor(cen_t, bank[:, 0:T], -1.0 / CHUNK, out_t, ALU.mult, ALU.add).then_inc(sem("centred"), 1)

        def act_centre_square(act, n):
            act.wait_ge(sem("centred"), n + 1)
            act.activation(csq_t, cen_t, ACT.Square).then_inc(sem("centred_square"), 1)

        def dve_variance(dve, n, bank=acc[0]):
            dve.wait_ge(sem("variance_done"), n + 1)
            dve.tensor_scalar(csq_t, bank[:, 0:T], 1.0 / CHUNK, RW_EPS, ALU.mult, ALU.add).then_inc(sem("variance_ready"), 1)

        def act_deviation(act, n):
            act.wait_ge(sem("variance_ready"), n + 1)
            act.activation(csq_t, csq_t, ACT.Sqrt).then_inc(sem("deviation_ready"), 1)

        def dve_inverse_deviation(dve, own, n):
            dve.wait_ge(sem("deviation_ready"), n + 1)
            own(dve.reciprocal(csq_t, csq_t))


        def dve_affine(dve, own, n):
            own(dve.tensor_tensor(cen_t, cen_t, csq_t, ALU.mult))
            own(dve.tensor_scalar(cen_t, cen_t, pcol_at("lnx_w", n), pcol_at("lnx_b", n), ALU.mult, ALU.add))

        def dve_add_bonus(dve, own, n):
            dve.wait_ge(sem("bonus_ready"), n + 1)
            own(dve.tensor_tensor(cen_t, cen_t, bon_t, ALU.add))

        def dve_gate(dve, own, n, bank=acc[0]):
            dve.tensor_tensor(cen_t, cen_t, bank[:, T:2 * T], ALU.mult).then_inc(sem("gated"), 1)
            own.end()

        def act_result_hi(act, n):
            act.wait_ge(sem("gated"), n + 1)
            act.activation(hidB_hi[:, bass.ds(n, 1), :].rearrange("p o t -> p (o t)"), cen_t, ACT.Copy).then_inc(sem("rw_hi"), 1)

        def dve_result_lo(dve, n):
            dve.wait_ge(sem("rw_hi"), n + 1)
            dve.tensor_tensor(hidB_lo[:, bass.ds(n, 1), :].rearrange("p o t -> p (o t)"), cen_t,
                              hidB_hi[:, bass.ds(n, 1), :].rearrange("p o t -> p (o t)"), ALU.subtract)\
               .then_inc(sem("rw_split"), 1)
            dve.wait_ge(sem("rw_split"), n + 1)

        def rwkv_pool(pool, p, gate, front, turns=None):
            for l in range(1, LEVELS):
                if l == 1:
                    pool.wait_ge(sem("inv_start"), p + 1)
                else:
                    pool.wait_ge(sem("y_done"), 5 * p + l - 1)
                pool.tensor_tensor(level_a[:, :, :], v_bd[:, :, :], over_chunks(CLEVEL + l * P), ALU.mult)\
                    .then_inc(sem("level_ready"), 1)
                if turns is not None and l < 5:
                    for i in range(3 * (l - 1), 3 * l):
                        rotate_step(pool, turns + i // 6, i % 6)
            if gate:
                pool.wait_ge(sem("variance_done"), p)
                load_gate_lora(pool, p)
            if front:
                pool.wait_ge(sem("lora_done"), p + 2)
                load_front_lora(pool, p + 2)

        def rwkv_dve(dve, p, norm, front):
            g, q = RET_N + p, p + 1
            own = Own(dve, "dve_own", p, 4)
            front_own = Own(dve, "front_own", q, 7)
            norm_own = Own(dve, "norm_own", p - 1, 4)
            if norm:
                dve_centre(dve, p - 1)
                dve.wait_ge(sem("state_ready"), 3 * p)
            own(dve.tensor_copy(decay_end[:, :], decay[:, :, CHUNK]))
            if front:
                dve_front_mix(dve, q)
            dve.wait_ge(sem("products_done"), p + 1)
            dve.tensor_tensor(seen_v[:, :, :], in_chunks(tp[2][:, :]), over_chunks(CSTRICT), ALU.mult)\
               .then_inc(sem("seen_ready"), 1)
            dve.scalar_tensor_tensor(seen_y[:, 0, :, :], chunks(tp[3][:, 0:T]), -1.0, over_chunks(CINCL, CHUNK),
                                     ALU.mult, ALU.mult).then_inc(sem("seen_ready"), 1)
            dve.tensor_tensor(seen_y[:, 1, :, :], chunks(tp[3][:, T:2 * T]), over_chunks(CINCL, CHUNK),
                              ALU.mult).then_inc(sem("seen_ready"), 1)
            dve.wait_ge(sem("a_copied"), p + 1)
            own(dve.tensor_tensor(level_a[:, :, :], v_bd[:, :, :], over_chunks(CLEVEL), ALU.mult))
            dve.wait_ge(sem("tokens_done"), 3 * p + 2)
            dve.tensor_tensor(key_bd[:, :, :], over_chunks(CIDENT), level_a[:, :, :], ALU.subtract).then_inc(sem("inv_start"), 1)
            if norm:
                dve_variance(dve, p - 1)
            split_lo(dve, g, 2)
            split_lo(dve, g, 3)
            for l in range(1, LEVELS):
                dve.wait_ge(sem("y_done"), 5 * p + l)
                if l == 1:
                    dve.wait_ge(sem("tokens_done"), 3 * p + 3)
                dve.tensor_tensor(beta_bd[:, :, :], over_chunks(CIDENT), in_chunks(tp[2][:, :]), ALU.subtract)\
                   .then_inc(sem("w_ready"), 1)
                if l == 1 and norm:
                    dve_inverse_deviation(dve, norm_own, p - 1)
                if l == 2:
                    split_lo(dve, g, 4)
                    if norm:
                        dve_affine(dve, norm_own, p - 1)
                if l == 3:
                    if norm:
                        dve_add_bonus(dve, norm_own, p - 1)
                        dve_gate(dve, norm_own, p - 1)
                    if front:
                        dve_front_decay(dve, front_own, q)
                if l == 4:
                    split_lo(dve, g, 5)
                    if front:
                        dve_front_key(dve, front_own, q)
                if l < LEVELS - 1:
                    dve.wait_ge(sem("inv_done"), 4 * p + l)
                    dve.tensor_copy(key_bd[:, :, :], in_chunks(tp[0][:, :])).then_inc(sem("inv_ready"), 1)
            if front:
                dve_front_sum(dve, q)
            split_lo(dve, g, 6)
            if norm:
                dve_result_lo(dve, p - 1)
            for c in range(NCHUNK - 1):
                if c == 0:
                    dve.wait_ge(sem("bonus_done"), p + 1)
                    dve.tensor_tensor(bon_t, acc[0][:, 0:T], z_at(p, V_BLOCK), ALU.mult).then_inc(sem("bonus_ready"), 1)
                dve.wait_ge(sem("state_done"), 3 * p + c + 1)
                new, end = state[:, (c + 1) % 2, :], decay_end[:, c:c + 1]
                if c == 0:
                    dve.tensor_scalar(new, tp[0][:, 0:P], end, None, ALU.mult).then_inc(sem("state_ready"), 1)
                else:
                    dve.scalar_tensor_tensor(new, tp[0][:, 0:P], end, scaled[:, :], ALU.mult, ALU.add)\
                       .then_inc(sem("state_ready"), 1)
                if c < NCHUNK - 2:
                    dve.wait_ge(sem("state_ready"), 3 * p + c + 1)
                    own(dve.tensor_scalar(scaled[:, :], new, decay_end[:, c + 1:c + 2], None, ALU.mult))
                if c == 0:
                    split_lo(dve, g, 7)
                if c == 1 and front:
                    dve_front_kk(dve, front_own, q)
            if front:
                dve.wait_ge(sem("inv_t_done"), LEVELS * (p + 1))
                dve_front_keys(dve, q)
                split_lo(dve, g + 1, 0)
                dve.wait_ge(sem("rhs_done"), NCHUNK * (p + 1))
                dve_front_kappa(dve, q)
                dve.wait_ge(sem("out_done"), p + 1)
                dve_front_rho(dve, q)
            else:
                split_lo(dve, g + 1, 0)
            split_lo(dve, g + 1, 1)
            own.end()

        def rwkv_act(act, p, norm, front):
            g, q = RET_N + p, p + 1
            act.wait_ge(sem("tokens_done"), 3 * p + 1)
            act.activation(v_tok[:, :, :], in_chunks(tp[0][:, :]), ACT.Copy).then_inc(sem("tokens_ready"), 1)
            if norm:
                act_centre_square(act, p - 1)
            split_hi(act, g, 2)
            split_hi(act, g, 3)
            act.wait_ge(sem("products_done"), p + 1)
            act.activation(v_bd[:, :, :], in_chunks(tp[1][:, :]), ACT.Copy).then_inc(sem("a_copied"), 1)
            act.wait_ge(sem("tokens_done"), 3 * p + 2)
            act.activation(key_tok[:, :, :], in_chunks(tp[0][:, :]), ACT.Copy).then_inc(sem("tokens_ready"), 1)
            if front:
                act_front_square(act, q)
            act.wait_ge(sem("tokens_done"), 3 * p + 3)
            act.activation(beta_tok[:, :, :], in_chunks(tp[3][:, :]), ACT.Copy, scale=-1.0).then_inc(sem("tokens_ready"), 1)
            for l in range(LEVELS):
                act.wait_ge(sem("inv_t_done"), LEVELS * p + l + 1)
                act.activation(inv_t[:, :, :], in_chunks(tp[1][:, :]), ACT.Copy).then_inc(sem("inv_t_ready"), 1)
                if l == 0:
                    if norm:
                        act_deviation(act, p - 1)
                if l == 1:
                    split_hi(act, g, 4)
                    if front:
                        act_front_tanh(act, q)
                if l == 2:
                    split_hi(act, g, 5)
                if l == 3:
                    if norm:
                        act_result_hi(act, p - 1)
                    split_hi(act, g, 6)
                if l == 4:
                    if front:
                        act_front_exp(act, q)
            for c in range(NCHUNK):
                act.wait_ge(sem("rhs_done"), NCHUNK * p + c + 1)
                act.activation(rhs_u[:, :], tp[2][:, 0:P], ACT.Copy).then_inc(sem("rhs_ready"), 1)
                act.wait_ge(sem("u_done"), NCHUNK * p + c + 1)
                act.activation(u_bd[:, :], tp[3][:, 0:P], ACT.Copy).then_inc(sem("u_ready"), 1)
                if c == 0:
                    split_hi(act, g, 7)
                    if front:
                        act_front_root(act, q)
                if c == 1 and front:
                    act.wait_ge(sem("level_ready"), 5 * (p + 1))
                    act_front_v(act, q)
                if c == 2:
                    split_hi(act, g + 1, 0)
            act.wait_ge(sem("out_done"), p + 1)
            act.activation(out_t, tp[1][:, 0:T], ACT.Copy).then_inc(sem("out_copied"), 1)
            act.wait_ge(unit_used, 8 * (g + 1))
            for h in range(HALVES):
                act.activation(ret_tok[:, bass.ds(p, 1), h, :].rearrange("p o n -> p (o n)"), acc[2 + h][:, :], ACT.Copy,
                               scale=rstd[:, h:h + 1]).then_inc(stg_written, 1)
            split_hi(act, g + 1, 1)

        def more(pe, p, parts, m):
            due = min(32, parts[0] + m)
            for part in range(parts[1], due):
                multiply_part(pe, RET_N + p, part, xT, 1)
            parts[:] = due, max(due, parts[1])

        def rwkv_pe(pe, p, norm, front, parts):
            pe.wait_ge(sem("v_ready"), 2 * p + 2)
            for c in range(NCHUNK):
                last = nc.tensor.transpose(tp[0][:, c * P:(c + 1) * P], v_bd[:, c, :], ident)
            last.then_inc(sem("tokens_done"), 1)
            if norm:
                pe_mean(pe, p - 1)
            pe.wait_ge(sem("kappa_ready"), 7 * p + 7)
            for c in range(NCHUNK):
                rho = chunks(rho_t)[:, c, :]
                mm(tp[1][:, c * P:(c + 1) * P], kappa_bd[:, c, :], beta_bd[:, c, :])
                mm(tp[2][:, c * P:(c + 1) * P], key_bd[:, c, :], kappa_bd[:, c, :])
                mm(tp[3][:, c * CHUNK:(c + 1) * CHUNK], beta_bd[:, c, :], rho)
                last = mm(tp[3][:, T + c * CHUNK:T + (c + 1) * CHUNK], key_bd[:, c, :], rho)
            last.then_inc(sem("products_done"), 1)
            pe.wait_ge(stg_written, 2 * (RET_STG + p))
            more(pe, p, parts, 3)
            pe.wait_ge(sem("tokens_ready"), 3 * p + 1)
            for c in range(NCHUNK):
                last = nc.tensor.transpose(tp[0][:, c * P:(c + 1) * P], key_bd[:, c, :], ident)
            last.then_inc(sem("tokens_done"), 1)
            if norm:
                pe_variance(pe, p - 1)
            more(pe, p, parts, 2)
            pe.wait_ge(sem("seen_ready"), 3 * p + 3)
            for c in range(NCHUNK):
                last = nc.tensor.transpose(tp[3][:, c * P:(c + 1) * P], beta_bd[:, c, :], ident)
            last.then_inc(sem("tokens_done"), 1)
            more(pe, p, parts, 2)
            pe.wait_ge(sem("inv_start"), p + 1)
            for c in range(NCHUNK):
                last = nc.tensor.transpose(tp[1][:, c * P:(c + 1) * P], key_bd[:, c, :], ident)
            last.then_inc(sem("inv_t_done"), 1)
            if front:
                pe_front_lora(pe, p + 1)
            pe.wait_ge(sem("tokens_ready"), 3 * p + 2)
            for l in range(1, LEVELS):
                more(pe, p, parts, 1)
                pe.wait_ge(sem("level_ready"), 5 * p + l)
                pe.wait_ge(sem("inv_t_ready"), LEVELS * p + l)
                for c in range(NCHUNK):
                    last = mm(tp[2][:, c * P:(c + 1) * P], level_a[:, c, :], inv_t[:, c, :])
                last.then_inc(sem("y_done"), 1)
                more(pe, p, parts, 2)
                pe.wait_ge(sem("w_ready"), 5 * p + l)
                if l > 1:
                    pe.wait_ge(sem("inv_ready"), 4 * p + l - 1)
                for c in range(NCHUNK):
                    last = mm(tp[1][:, c * P:(c + 1) * P], key_bd[:, c, :], beta_bd[:, c, :])
                last.then_inc(sem("inv_t_done"), 1)
                if l < LEVELS - 1:
                    for c in range(NCHUNK):
                        last = mm(tp[0][:, c * P:(c + 1) * P], beta_bd[:, c, :], key_bd[:, c, :])
                    last.then_inc(sem("inv_done"), 1)
                if l == 3 and front:
                    pe_front_sum(pe, p + 1)
            pe.wait_ge(sem("tokens_ready"), 3 * p + 3)
            for c in range(NCHUNK):
                s, v = state[:, c % 2, :], v_tok[:, c, :]
                if c:
                    pe.wait_ge(sem("state_ready"), 3 * p + c)
                    mm(tp[2][:, 0:P], kappa_bd[:, c, :], s, last=False)
                mm(tp[2][:, 0:P], seen_v[:, c, :], v, first=(c == 0)).then_inc(sem("rhs_done"), 1)
                if c == 0:
                    if front:
                        pe.wait_ge(sem("kk_sum_read"), p + 2)
                    else:
                        pe.wait_ge(sem("gated"), p)
                    mm(acc[0][:, 0:T], ones, sq_t).then_inc(sem("bonus_done"), 1)
                more(pe, p, parts, 1)
                if c == 0:
                    pe.wait_ge(sem("inv_t_ready"), LEVELS * (p + 1))
                pe.wait_ge(sem("rhs_ready"), NCHUNK * p + c + 1)
                mm(tp[3][:, 0:P], inv_t[:, c, :], rhs_u[:, :]).then_inc(sem("u_done"), 1)
                more(pe, p, parts, 1)
                pe.wait_ge(sem("u_ready"), NCHUNK * p + c + 1)
                if c < NCHUNK - 1:
                    mm(tp[0][:, 0:P], key_tok[:, c, :], v, last=False)
                    mm(tp[0][:, 0:P], beta_tok[:, c, :], u_bd[:, :], first=False).then_inc(sem("state_done"), 1)
                y = tp[1][:, c * CHUNK:(c + 1) * CHUNK]
                if c:
                    mm(y, s, chunks(rho_t)[:, c, :], last=False)
                mm(y, v, seen_y[:, 1, c, :], first=(c == 0), last=False)
                last = mm(y, u_bd[:, :], seen_y[:, 0, c, :], first=False)
            last.then_inc(sem("out_done"), 1)
            more(pe, p, parts, 32)

        def first_front(role, eng, j):
            if role == "dve":
                if j == 0:
                    once(eng, "masks_landed", 16)
                    rwkv_prepare_dve(eng)
                if j == 5:
                    once(eng, "z_ready", 12)
                    dve_front_mix(eng, 0)
                if j == 7:
                    split_lo(eng, RET_N, 0)
                    own = Own(eng, "front_own", 0, 7)
                    dve_front_sum(eng, 0, acc[2])
                    dve_front_decay(eng, own, 0)
                    dve_front_key(eng, own, 0)
                    dve_front_kk(eng, own, 0)
            elif role == "act":
                if j == 3:
                    rwkv_prepare_act(eng)
                if j == 6:
                    act_front_square(eng, 0)
                    act_front_v(eng, 0)
                if j == 7:
                    split_hi(eng, RET_N, 0)
                    act_front_tanh(eng, 0, acc[3])
                    act_front_exp(eng, 0)
                    act_front_root(eng, 0)
            elif role == "pe":
                if j == 6:
                    once(eng, "masks_landed", 16)
                    once(eng, "lora_inputs", 4)
                    eng.wait_ge(stg_written, 12)
                    pe_front_sum(eng, 0, acc[2])
                    pe_front_lora(eng, 0, acc[3])

        def even_in(role, eng, prev, parts):
            def first_norm(role, eng, j):
                if role == "act":
                    if j in (1, 2, 3, 6):
                        k = min(j - 1, 3)
                        act_squares(eng, dict(prev, xs=k), k * WIDE)
                    if j == 7:
                        act_deviation_of_x(eng, prev)
                elif role == "dve" and j == 7:
                    dve_variance_of_x(eng, prev)
                    dve_finish_norm(eng, prev, late=True)

            step(role, eng, LORA, ev_w_in, 0, RET_IN + 3 * RET_W, xT, prev, first_norm)
            if role == "sp":
                eng.dma_start(con[:, P:], consts[:, P:]).then_inc(sem("masks_landed"), 16)
            step(role, eng, rkv(0, 0), ev_w_in, 0, RET_IN, xT, LORA)
            with eng.Fori(0, 2) as i:
                step(role, eng, rkv(i, 1), ev_w_in, 0, RET_IN + (2 * i + 1) * WIDE, xT, rkv(i, 0))
                step(role, eng, rkv(i + 1, 0), ev_w_in, 0, RET_IN + (2 * i + 2) * WIDE, xT, rkv(i, 1))
            step(role, eng, rkv(2, 1), ev_w_in, 0, RET_IN + 5 * WIDE, xT, rkv(2, 0), first_front)
            if role == "act":
                split_hi(eng, RET_N, 1)
            elif role == "dve":
                split_lo(eng, RET_N, 1)
            elif role == "pe":
                eng.wait_ge(sem("kk_sum_read"), 1)
                eng.wait_ge(sem("tanh_ready"), 2)
                more(eng, 0, parts, 4)
            finish(role, eng, rkv(2, 1))
            if role == "pe":
                more(eng, 0, parts, 4)

        def rwkv(role, eng, parts):
            LAST = RW_BLOCKS - 1
            if role == "sp":
                with eng.Fori(0, RW_BLOCKS) as p:
                    for j in range(UNITS):
                        load_unit(eng, RET_N + p, j, ev_w_in, 0, p * WIDE)
            elif role == "pool":
                once(eng, "rw_zeroed", 11)
                once(eng, "masks_landed", 16)
                load_front_lora(eng, 0)
                load_gate_lora(eng, 0)
                once(eng, "lora_done", 1)
                load_front_lora(eng, 1)
                rwkv_pool(eng, 0, False, True)
                with eng.Fori(1, 4) as p:
                    rwkv_pool(eng, p, True, True)
                load_cos_sin(eng)
                for p in range(4, RW_BLOCKS):
                    rwkv_pool(eng, p, True, p < LAST - 1, turns=2 * (p - 4))
            elif role == "dve":
                once(eng, "z_ready", 14)
                dve_front_keys(eng, 0)
                dve_front_kappa(eng, 0)
                dve_front_rho(eng, 0)
                rwkv_dve(eng, 0, False, True)
                with eng.Fori(1, LAST) as p:
                    rwkv_dve(eng, p, True, True)
                rwkv_dve(eng, LAST, True, False)
            elif role == "act":
                rwkv_act(eng, 0, False, True)
                with eng.Fori(1, LAST) as p:
                    rwkv_act(eng, p, True, True)
                rwkv_act(eng, LAST, True, False)
            elif role == "pe":
                parts[0] = 0
                once(eng, "z_ready", 14)
                rwkv_pe(eng, 0, False, True, parts)
                with eng.Fori(1, LAST) as p:
                    rwkv_pe(eng, p, True, True, [0, 0])
                rwkv_pe(eng, LAST, True, False, [0, 0])

        def ret_view(kind, h, half=None, part=None):
            group, c0 = 2 * kind + h // 2, (h % 2) * 2 * P + (part or 0) * P
            c1 = c0 + (2 * P if part is None else P)
            return ret_tok[:, group, :, c0:c1] if half is None else ret_tok[:, group, half, c0:c1]

        ret_cos, ret_sin = z[:, V_BLOCK:V_BLOCK + 2, 0:P], z[:, V_BLOCK:V_BLOCK + 2, P:2 * P]
        rot_a, rot_b = (z[:, V_BLOCK + i, :].rearrange("p (h n) -> p h n", h=HALVES) for i in (2, 3))

        def load_cos_sin(pool):
            once(pool, "bonus_ready", 2)
            pool.dma_start(z[:, V_BLOCK:V_BLOCK + 2, :], cossin.rearrange("(h p) a c -> p h (a c)", p=P))\
                .then_inc(sem("cs_landed"), 16)

        def rotate_step(pool, item, i):
            t1, t2 = (ret_view(item % 2, item // 2, part=part) for part in range(2))
            products, rotated = sem("rotation_products"), sem("rotated")
            if item == 0 and i == 0:
                once(pool, "bonus_ready", 4)
                once(pool, "stg_written", 2 * (RET_STG + 4))
                once(pool, "cs_landed", 16)
            if i == 0 and item:
                pool.wait_ge(rotated, 2 * item)
            if i in (2, 3):
                pool.wait_ge(products, 4 * item + i - 1)
            if i == 4:
                pool.wait_ge(products, 4 * item + 4)
            out, a, b, op = ((rot_a, t1, ret_sin, ALU.mult), (rot_b, t2, ret_sin, ALU.mult), (t1, t1, ret_cos, ALU.mult),
                             (t2, t2, ret_cos, ALU.mult), (t1, t1, rot_b, ALU.subtract), (t2, t2, rot_a, ALU.add))[i]
            pool.tensor_tensor(out, a, b, op).then_inc(products if i < 4 else rotated, 1)

        RET_DONE = 2 * (RET_STG + 8)
        LAST = RW_BLOCKS - 1
        QK_BANKS = ((2, 3), (0, 1), (2, 3), (0, 1))
        OUT_BANKS = (tp[2], tp[3], tp[0], tp[1])
        SCORE_BANKS = (acc[3], acc[2], acc[3], acc[2])
        Y_BANKS = (acc[2], acc[3], tp[2], tp[3])

        def y_ret(h, half=None):
            return qT[:, 2 * h:2 * h + 2, :] if half is None else qT[:, 2 * h + half, :]

        def retention(role, eng, g, w):
            n = g["n"]
            if role == "sp":
                sp_group(eng, g, w, 0, 0)
            elif role == "pool":
                once(eng, "out_done", RW_BLOCKS)
                for h in range(RET_HEADS):
                    eng.dma_start(table_d[:, h, :, :], rdecay[h].rearrange("(m p) n -> p m n", p=P))\
                       .then_inc(sem(f"decay_landed{h}"), 16)
                once(eng, "ret_gate", 2)
                for h in range(RET_HEADS):
                    once(eng, "ret_normed", 2 * h + 2)
                    eng.tensor_tensor(y_ret(h), y_ret(h), ret_view(3, h), ALU.mult).then_inc(sem("y_gated"), 1)
            elif role == "dve":
                def mask(h):
                    if h >= 2:
                        once(eng, "ret_out_done", h - 1)
                    once(eng, "scores_done", h + 1)
                    once(eng, f"decay_landed{h}", 16)
                    eng.tensor_tensor(scores[:, h % 2, :, :], SCORE_BANKS[h][:, :].rearrange("p (m n) -> p m n", m=HALVES),
                                      table_d[:, h, :, :], ALU.mult).then_inc(sem("scores_ready"), 1)

                def stats(h):
                    once(eng, "ret_out_done", h + 1)
                    for i in range(HALVES):
                        eng.bn_stats(rstat[:, i, :], OUT_BANKS[h][:, i * T:(i + 1) * T]).then_inc(sem("ret_stats"), 1)
                    once(eng, "ret_stats", 4 * h + 2)
                    for i in range(HALVES):
                        eng.bn_aggr(rmean[:, h, i, :], rstat[:, i, :]).then_inc(sem("ret_stats"), 1)
                    once(eng, "ret_stats", 4 * h + 4)
                    if h % 2:
                        eng.tensor_scalar(rdev[:, h - 1:h + 1, :], rmean[:, h - 1:h + 1, :, 1], RET_EPS, None, ALU.add)\
                           .then_inc(sem("ret_variance"), 1)

                def norm(a):
                    once(eng, "ret_deviation", a + 1)
                    eng.reciprocal(rdev[:, 2 * a:2 * a + 2, :], rdev[:, 2 * a:2 * a + 2, :]).then_inc(sem("ret_scale"), 1)
                    once(eng, "ret_scale", a + 1)
                    for h in (2 * a, 2 * a + 1):
                        for i in range(HALVES):
                            eng.tensor_scalar(y_ret(h, i), OUT_BANKS[h][:, i * T:(i + 1) * T], rmean[:, h, i, 0:1],
                                              rdev[:, h, i:i + 1], ALU.subtract, ALU.mult).then_inc(sem("ret_normed"), 1)

                own = Own(eng, "norm_own", LAST, 4)
                dve_centre(eng, LAST, acc[2])
                dve_variance(eng, LAST, acc[2])
                split_lo(eng, n, 2)
                dve_inverse_deviation(eng, own, LAST)
                mask(0)
                dve_affine(eng, own, LAST)
                dve_add_bonus(eng, own, LAST)
                dve_gate(eng, own, LAST, acc[2])
                split_lo(eng, n, 3)
                mask(1)
                dve_result_lo(eng, LAST)
                mask(2)
                stats(0)
                mask(3)
                stats(1)
                split_lo(eng, n, 4)
                stats(2)
                norm(0)
                stats(3)
                split_lo(eng, n, 5)
                norm(1)
                split_lo(eng, n, 6)
                for h in range(RET_HEADS):
                    once(eng, "ret_hi", h + 1)
                    eng.tensor_tensor(hidA_lo[:, 2 * h:2 * h + 2, :], Y_BANKS[h][:, :].rearrange("p (c t) -> p c t", c=2),
                                      hidA_hi[:, 2 * h:2 * h + 2, :], ALU.subtract).then_inc(sem("ret_split"), 1)
                split_lo(eng, n, 7)
            elif role == "act":
                def copy_qk(h):
                    for i, t in enumerate((qT, kT)):
                        once(eng, "qk_turned", 2 * h + i + 1)
                        eng.activation(t[:, 2 * h:2 * h + 2, :],
                                       tp[QK_BANKS[h][i]][:, :].rearrange("p (c t) -> p c t", c=2), ACT.Copy)\
                           .then_inc(sem("qk_ready"), 1)

                copy_qk(0)
                copy_qk(1)
                act_centre_square(eng, LAST)
                split_hi(eng, n, 2)
                act_deviation(eng, LAST)
                copy_qk(2)
                copy_qk(3)
                split_hi(eng, n, 3)
                act_result_hi(eng, LAST)
                for i in range(2):
                    gates = ret_tok[:, 6 + i, :, :]
                    eng.activation(gates, gates, ACT.Silu).then_inc(sem("ret_gate"), 1)
                split_hi(eng, n, 4)
                for a in range(2):
                    once(eng, "ret_variance", a + 1)
                    eng.activation(rdev[:, 2 * a:2 * a + 2, :], rdev[:, 2 * a:2 * a + 2, :], ACT.Sqrt)\
                       .then_inc(sem("ret_deviation"), 1)
                    split_hi(eng, n, 5 + a)
                for h in range(RET_HEADS):
                    once(eng, "y_turned", h + 1)
                    eng.activation(hidA_hi[:, 2 * h:2 * h + 2, :], Y_BANKS[h][:, :].rearrange("p (c t) -> p c t", c=2),
                                   ACT.Copy).then_inc(sem("ret_hi"), 1)
                split_hi(eng, n, 7)
            elif role == "pe":
                def turn(bank, view, name):
                    for part in range(2):
                        for half in range(HALVES):
                            last = nc.tensor.transpose(bank[:, part * T + half * P:part * T + (half + 1) * P],
                                                       view(half, part), ident)
                    last.then_inc(sem(name), 1)

                def turn_qk(h):
                    once(eng, "rotated", 4 * h + 4)
                    for kind in range(2):
                        turn(tp[QK_BANKS[h][kind]], lambda half, part: ret_view(kind, h, half, part), "qk_turned")

                def score(h):
                    once(eng, "qk_ready", 2 * h + 2)
                    for m in range(HALVES):
                        for d in range(2):
                            last = mm(SCORE_BANKS[h][:, m * T:(m + 1) * T], kT[:, 2 * h + d, m * P:(m + 1) * P],
                                      qT[:, 2 * h + d, :], first=(d == 0), last=(d == 1))
                    last.then_inc(sem("scores_done"), 1)

                def weigh(h):
                    once(eng, "scores_ready", h + 1)
                    for i in range(HALVES):
                        for m in range(i + 1):
                            last = mm(OUT_BANKS[h][:, i * T:(i + 1) * T], scores[:, h % 2, m, i * P:(i + 1) * P],
                                      ret_view(2, h, m), first=(m == 0), last=(m == i))
                    last.then_inc(sem("ret_out_done"), 1)

                parts = [0]

                def project(m):
                    for part in range(parts[0], min(16, parts[0] + m)):
                        if part % 4 == 0:
                            once(eng, "rw_split", part // 2 + 2)
                        multiply_part(eng, n, part, mixed, 0)
                    parts[0] = min(16, parts[0] + m)

                turn_qk(0)
                once(eng, "out_copied", RW_BLOCKS)
                turn_qk(1)
                once(eng, "stg_written", RET_DONE)
                pe_mean(eng, LAST, acc[2])
                once(eng, "tanh_ready", 2 * RW_BLOCKS)
                project(3)
                pe_variance(eng, LAST, acc[2])
                project(1)
                score(0)
                once(eng, "qk_ready", 2)
                turn_qk(2)
                project(2)
                once(eng, "qk_ready", 4)
                turn_qk(3)
                project(1)
                once(eng, "qk_ready", 6)
                weigh(0)
                once(eng, "gated", RW_BLOCKS)
                score(1)
                once(eng, "scores_ready", 1)
                score(2)
                project(1)
                weigh(1)
                score(3)
                project(1)
                once(eng, "qk_ready", 8)
                weigh(2)
                project(1)
                weigh(3)
                project(16)
                for h in range(RET_HEADS):
                    once(eng, "y_gated", h + 1)
                    turn(Y_BANKS[h], lambda half, part: y_ret(h, half)[:, part * P:(part + 1) * P], "y_turned")
                for j in range(4, UNITS):
                    once(eng, "ret_split", j - 3)
                    multiply_unit(eng, n, j, mixed, 0)

        C_EVEN_OUT = dict(n=15, tused=(6, 5), xu=0, xs=4, thi=16, lhs=16, norm=1)

        def mixed(kt):
            return hid((kt + KT // 2) % KT)

        def even_out_group(k):
            return dict(residual(C_EVEN_OUT, k, "ff_norm0"), swap=True, need=None,
                        free=None if k < 2 else (x_updated, C_EVEN_OUT["xu"] + k - 1))

        def even_projection(role, eng):
            retention(role, eng, even_out_group(0), ev_w_out)
            for k in range(1, 4):
                step(role, eng, even_out_group(k), ev_w_out, 0, k * WIDE, mixed, even_out_group(k - 1))
            return even_out_group(3)

        def out_projection(role, eng, c, w, gain, free, tp_first, need, prev=None, side=None):
            def g(k):
                r = residual(c, k, gain)
                r["free"] = free(k) if k < 2 else (x_updated, c["xu"] + k - 1)
                r["need"] = need if k == 0 else None
                if k < 2 and tp_first:
                    r["tp"] = tp_first
                return r

            for k in range(4):
                step(role, eng, g(k), w, 0, k * WIDE, hid, prev, side if k == 0 else None)
                prev = g(k)
            return prev

        C_MLP0 = dict(n=19, tused=(8, 7), stg=15, hid=0, xu=4, xs=8, thi=32, lhs=32, norm=2)

        C_ODD = after_mlp(C_MLP0, "od_norm")
        ODD_STG, ODD_Z = C_ODD["stg"], 14

        def branch(v):
            k = v % 4

            def move(dve, c, bank):
                return dve.tensor_copy(x_raw[:, 4 * k + 2 * c:4 * k + 2 * c + 2, CONV - 1:],
                                       bank[:, :].rearrange("p (c t) -> p c t", c=2))

            if v < 2:
                free, tp_free = (x_updated, C_ODD["xu"] - 1 + v), (lhs_ready, C_ODD["lhs"])
            else:
                free, tp_free = (stg_written, 2 * (ODD_STG + v - 1)), (z_ready, ODD_Z + 2 * (v - 1))
            if 3 <= v <= 6:
                tp_free = (sem("gates_read"), 8 * (v - 2))
            if 4 <= v <= 7:
                free = (sem("gates_read"), 8 * (v - 3))
            return dict(n=C_ODD["n"] + v, bank=v % 2, post="z", wide=WIDE, free=free, tp=tp_free, move=move,
                        need=(C_ODD["lhs"] - 4, C_ODD["lhs"]) if v == 0 else None, stg=ODD_STG + v, norm=C_ODD["norm"],
                        tused=C_ODD["tused"][v % 2] + v // 2, func=ACT.Gelu_apprx_tanh if v >= 4 else ACT.Copy)

        def branch_step(role, eng, v, prev):
            step(role, eng, branch(v), od_w_in, 0, (D if v < 4 else 0) + (v % 4) * WIDE, xT, prev,
                 odd_side(v) if v >= 2 else None)

        def prepare_lambda(role, eng):
            src = par[:, COLS["lam"][0]:COLS["lam"][0] + KT]
            a, e, zz, z2, q, out8 = (lam[:, i, :] for i in range(6))
            if role == "dve":
                own = Own(eng, "lambda_own")
                own(eng.tensor_scalar(zz, src, -1.0, None, ALU.mult))
                own(eng.tensor_tensor(a, src, zz, ALU.max))
                own(eng.tensor_scalar(out8, zz, 0.0, None, ALU.max))
                once(eng, "lambda_exp", 1)
                own(eng.tensor_scalar(q, e, 2.0, None, ALU.add))
                own(eng.reciprocal(q, q))
                own(eng.tensor_tensor(zz, e, q, ALU.mult))
                own(eng.tensor_tensor(z2, zz, zz, ALU.mult))
                own(eng.tensor_scalar(q, z2, 1.0 / 15, None, ALU.mult))
                for odd in (13, 11, 9, 7, 5, 3):
                    own(eng.scalar_tensor_tensor(q, q, 1.0 / odd, z2, ALU.add, ALU.mult))
                own(eng.scalar_tensor_tensor(q, q, 1.0, zz, ALU.add, ALU.mult))
                own(eng.scalar_tensor_tensor(out8, q, 2.0, out8, ALU.mult, ALU.add))
                eng.tensor_scalar(out8, out8, -LRU_C, None, ALU.mult).then_inc(sem("lambda_ready"), 1)
            else:
                once(eng, "lambda_own", 2)
                eng.activation(e, a, ACT.Exp, scale=-1.0).then_inc(sem("lambda_exp"), 1)

        def quad(t, i, n=4):
            return t[:, n * i:n * i + n, :]

        def odd_conv(dve, n, taps):
            for i in taps:
                j = CONV - 1 - i
                for b in (2 * n, 2 * n + 1):
                    view, tap = x_raw[:, b, j:j + T], par[:, COLS["conv_w"][0] + KT * j + b:COLS["conv_w"][0] + KT * j + b + 1]
                    if i == 0:
                        ins = dve.tensor_scalar(conv[:, b, :], view, tap, pcol("conv_b", b), ALU.mult, ALU.add)
                    else:
                        ins = dve.scalar_tensor_tensor(conv[:, b, :], view, tap, conv[:, b, :], ALU.mult, ALU.add)
                    ins.then_inc(sem("conv_step"), 1)
                once(dve, "conv_step", 8 * n + 2 * i + 2)

        def odd_gate_banks(v, n):
            b = v % 2
            return (tp[2 * b], tp[2 * b + 1]) if n % 2 == 0 else (acc[2 - 2 * b], acc[3 - 2 * b])

        def odd_gates_pe(pe, v, n):
            once(pe, "conv_step", 8 * n + 8)
            once(pe, f"gate_w_landed{n % 2}", 32 * (n // 2 + 1))
            if n % 2 == 0:
                once(pe, "z_ready", ODD_Z + 2 * (v - 1))
            else:
                once(pe, "stg_written", 2 * (ODD_STG + v))
            for i in range(2):
                for jh in range(2):
                    for ih in range(2):
                        last = nc.tensor.matmul(odd_gate_banks(v, n)[i][:, jh * T:(jh + 1) * T],
                                                gate_w[:, n % 2, i, ih, jh * P:(jh + 1) * P],
                                                conv[:, 2 * n + ih, :], start=(ih == 0), stop=(ih == 1))
            last.then_inc(sem("gates_done"), 1)

        def odd_gates_act(act, v, n):
            once(act, "gates_done", n + 1)
            for i, (t, bias) in enumerate(((gate_x, "gx_b"), (gate_a, "ga_b"))):
                for jh in range(2):
                    act.activation(t[:, 2 * n + jh, :], odd_gate_banks(v, n)[i][:, jh * T:(jh + 1) * T], ACT.Sigmoid,
                                   bias=pcol(bias, 2 * n + jh)).then_inc(sem("gates_read"), 1)

        def load_gate_w(sp, n):
            if n >= 2:
                once(sp, "gates_done", n - 1)
            for i, w in enumerate((gx_w, ga_w)):
                sp.dma_start(gate_w[:, n % 2, i, :, :], w[n].rearrange("(i p) j -> p i j", p=P))\
                   .then_inc(sem(f"gate_w_landed{n % 2}"), 16)

        def odd_product(role, eng, k):
            a, c = ((hidA_hi, hidA_lo) if k < 2 else (hidB_hi, hidB_lo)), 4 * (k % 2)
            if role == "pool":
                once(eng, "scanned", k + 1)
                once(eng, "z_ready", ODD_Z + 8 + 2 * (k + 1))
                eng.tensor_tensor(quad(gate_t, k), quad(gate_t, k), x_raw[:, 4 * k:4 * k + 4, CONV - 1:], ALU.mult)\
                   .then_inc(sem("odd_mixed"), 1)
            elif role == "act":
                once(eng, *(("root_in", k + 3) if k < 2 else ("scanned", k + 1)))
                once(eng, "odd_mixed", k + 1)
                eng.activation(a[0][:, c:c + 4, :], quad(gate_t, k), ACT.Copy).then_inc(sem("odd_hi"), 1)
            elif role == "dve":
                once(eng, "odd_hi", k + 1)
                eng.tensor_tensor(a[1][:, c:c + 4, :], quad(gate_t, k), a[0][:, c:c + 4, :], ALU.subtract)\
                   .then_inc(sem("odd_split"), 1)

        def odd_decays(act, k):
            once(act, "lambda_ready", 1)
            once(act, "bx_ready", k + 1)
            for t, func, name in ((conv, ACT.Exp, "decays_ready"), (gate_t, ACT.Tanh, "tangents_ready")):
                for kt in range(4 * k, 4 * k + 4):
                    act.activation(t[:, kt, :], gate_a[:, kt, :], func, scale=lam[:, 5, kt:kt + 1]).then_inc(sem(name), 1)

        def odd_roots(act, k):
            once(act, "root_in", k + 1)
            act.activation(quad(gate_t, k), quad(gate_t, k), ACT.Sqrt, scale=-1.0).then_inc(sem("roots_ready"), 1)

        def odd_root_input(dve, k):
            once(dve, "squares_ready", k + 1)
            dve.scalar_tensor_tensor(quad(gate_t, k), quad(gate_a, k), 1.0, quad(gate_t, k), ALU.add, ALU.mult)\
               .then_inc(sem("root_in"), 1)
            dve.memset(quad(conv, k)[:, :, 0:1], 0.0).then_inc(sem("restarts_set"), 1)

        def odd_scan(dve, k):
            once(dve, "inputs_ready", k + 1)
            once(dve, "restarts_set", k + 1)
            flat = lambda t: quad(t, k).rearrange("p c t -> p (c t)")
            dve.tensor_tensor_scan(flat(gate_t), flat(conv), flat(gate_x), 0.0, ALU.mult, ALU.add).then_inc(sem("scanned"), 1)

        def odd_pool(pool):
            def bx(k):
                once(pool, "gates_read", 8 * (k + 1))
                pool.tensor_tensor(quad(gate_x, k), quad(gate_x, k), quad(conv, k), ALU.mult).then_inc(sem("bx_ready"), 1)

            for k in range(4):
                bx(k)
                once(pool, "decays_ready", 4 * k + 4)
                once(pool, "tangents_ready", 4 * k + 4)
                pool.tensor_tensor(quad(gate_a, k), quad(conv, k), quad(conv, k), ALU.mult).then_inc(sem("squares_ready"), 1)
                once(pool, "roots_ready", k + 1)
                pool.tensor_tensor(quad(gate_x, k), quad(gate_x, k), quad(gate_t, k), ALU.mult).then_inc(sem("inputs_ready"), 1)
                if k == 3:
                    odd_product("pool", pool, 0)
                    odd_product("pool", pool, 1)
            for k in (2, 3):
                odd_product("pool", pool, k)

        def odd_side(v):
            def side(role, eng, j):
                if role == "dve":
                    if v == 2 and j == 0:
                        eng.memset(x_raw[:, :, 0:CONV - 1], 0.0).then_inc(sem("odd_zeroed"), 1)
                        once(eng, "odd_zeroed", 1)
                    if v <= 5 and j in (0, 1, 3, 4):
                        once(eng, "z_ready", ODD_Z + 2 * (v - 1))
                        odd_conv(eng, 2 * (v - 2) + j // 3, (0, 1) if j % 3 == 0 else (2, 3))
                    if 4 <= v <= 7 and j == 6 - (v == 7):
                        odd_root_input(eng, v - 4)
                    if 5 <= v <= 7 and j == 2:
                        odd_scan(eng, v - 5)
                    if v == 7 and j == 7:
                        odd_scan(eng, 3)
                    if v == 8 and j in (0, 1, 3, 6):
                        odd_product("dve", eng, (0, 1, 3, 6).index(j))
                elif role == "act":
                    if 3 <= v <= 6 and j == 7:
                        for n in (2 * (v - 3), 2 * (v - 3) + 1):
                            odd_gates_act(eng, v, n)
                    if 4 <= v <= 7 and j == 3:
                        odd_decays(eng, v - 4)
                    if 5 <= v <= 7 and j == 0:
                        odd_roots(eng, v - 5)
                    if v == 7 and j == 6:
                        odd_roots(eng, 3)
                    if v == 7 and j == 7:
                        odd_product("act", eng, 0)
                    if v == 8 and j in (0, 1, 6):
                        odd_product("act", eng, (0, 1, 6).index(j) + 1)
                elif role == "pe":
                    if 3 <= v <= 6 and j in (1, 4):
                        odd_gates_pe(eng, v, 2 * (v - 3) + j // 4)
                elif role == "sp":
                    if v == 2 and j in (0, 1):
                        load_gate_w(eng, j)
                    if 3 <= v <= 5 and j == 6 or 4 <= v <= 6 and j == 1:
                        load_gate_w(eng, 2 * (v - 2) if j == 6 else 2 * (v - 3) + 1)
            return side

        C_ODD_OUT = dict(C_ODD, n=C_ODD["n"] + 8, tused=[t + 4 for t in C_ODD["tused"]])
        C_MLP1 = dict(n=C_ODD["n"] + 12, tused=[t + 6 for t in C_ODD["tused"]], stg=C_ODD["stg"] + 8, hid=C_ODD["hid"],
                      xu=C_ODD["xu"] + 4, xs=C_ODD["xs"] + 4, thi=C_ODD["thi"] + 16, lhs=C_ODD["lhs"] + 16,
                      norm=C_ODD["norm"] + 1)
        C_END = after_mlp(C_MLP1, None)

        def odd_layer(role, eng, prev):
            for v in range(8):
                branch_step(role, eng, v, prev)
                prev = branch(v)
                if role == "pool" and v == 1:
                    odd_pool(eng)
            return out_projection(role, eng, C_ODD_OUT, od_w_out, "ff_norm1",
                                  free=lambda k: (stg_written, 2 * (ODD_STG + 7 + k)), tp_first=(z_ready, ODD_Z + 16),
                                  need=lambda pe, j: once(pe, "odd_split", j // 2 + 1), prev=prev, side=odd_side(8))

        tables_landed = sem("tables_landed")
        out_ready, out_stored = [sem(f"out_ready{k}") for k in range(4)], sem("out_stored")
        gain_landed, gained = sem("gain_landed"), sem("gained")
        gain_row = stg[:, :, :, :].rearrange("p a h n -> p (a h n)")

        def program(role, eng):
            posts = load_posts("ev_norm")
            for p in posts[:-1]:
                finish(role, eng, p)
            parts = [0, 0]
            even_in(role, eng, posts[-1], parts)
            rwkv(role, eng, parts)
            prev = even_projection(role, eng)
            prev = mlp(role, eng, 0, C_MLP0, prev, "od_norm")
            prev = odd_layer(role, eng, prev)
            prev = mlp(role, eng, 1, C_MLP1, prev, None)
            finish(role, eng, prev)

        block = ctx.enter_context(nc.Block())

        @block.sync
        def _(sp):
            sp.dma_start(ident, consts[:, CIDENT:CIDENT + P]).then_inc(tables_landed, 16)
            for k in range(4):
                sp.dma_start(x[:, :, k * WIDE:(k + 1) * WIDE],
                             x_in[:, k * WIDE:(k + 1) * WIDE].rearrange("(h p) n -> p h n", p=P)).then_inc(x_landed[k], 16)
                if k == 0:
                    sp.dma_start(par[:, :], params).then_inc(tables_landed, 16)
            program("sp", sp)
            sp.wait_ge(squared, C_END["hid"])
            sp.wait_ge(t_done[0], C_END["tused"][0])
            sp.wait_ge(t_done[1], C_END["tused"][1])
            sp.dma_start(gain_row, final_norm.rearrange("(a n) -> a n", a=1).broadcast_to((P, D))).then_inc(gain_landed, 16)
            for k in (0, 3, 1, 2):
                for h in range(HALVES):
                    sp.wait_ge(out_ready[k], h + 1)
                    sp.dma_start(out[h * P:(h + 1) * P, k * WIDE:(k + 1) * WIDE],
                                 x[:, h, k * WIDE:(k + 1) * WIDE]).then_inc(out_stored, 16)
            sp.wait_ge(out_stored, 16 * 4 * HALVES)

        @block.gpsimd
        def _(pool):
            program("pool", pool)
            pool.wait_ge(gain_landed, 16)
            for k in range(3):
                pool.wait_ge(ssq_done, HALVES * (C_END["xs"] - 3 + k))
                xs = x[:, :, k * WIDE:(k + 1) * WIDE]
                gains = gain_row[:, k * WIDE:(k + 1) * WIDE].rearrange("p (o n) -> p o n", o=1).broadcast_to((P, HALVES, WIDE))
                pool.tensor_tensor(xs, xs, gains, ALU.mult).then_inc(gained, 1)

        @block.scalar
        def _(act):
            act.wait_ge(tables_landed, 32)
            prepare_lambda("act", act)
            program("act", act)
            act.wait_ge(rstd_ready, C_END["norm"])
            act.wait_ge(gained, 2)
            for k in range(2):
                for h in range(HALVES):
                    xs = x[:, h, k * WIDE:(k + 1) * WIDE]
                    act.activation(xs, xs, ACT.Copy, scale=rstd[:, h:h + 1]).then_inc(out_ready[k], 1)

        @block.vector
        def _(dve):
            rwkv_zero(dve)
            dve.wait_ge(tables_landed, 32)
            prepare_lambda("dve", dve)
            program("dve", dve)
            dve.wait_ge(rstd_ready, C_END["norm"])
            dve.wait_ge(gain_landed, 16)
            for h in range(HALVES):
                xs = x[:, h, 3 * WIDE:D]
                dve.scalar_tensor_tensor(xs, xs, rstd[:, h:h + 1], gain_row[:, 3 * WIDE:D], ALU.mult, ALU.mult)\
                   .then_inc(out_ready[3], 1)
            dve.wait_ge(gained, 3)
            for h in range(HALVES):
                xs = x[:, h, 2 * WIDE:3 * WIDE]
                dve.tensor_scalar(xs, xs, rstd[:, h:h + 1], None, ALU.mult).then_inc(out_ready[2], 1)

        @block.tensor
        def _(pe):
            pe.wait_ge(tables_landed, 32)
            program("pe", pe)


def const_table():
    import numpy as np
    i = np.arange(P)
    same = (i[:, None] // CHUNK) == (i[None, :] // CHUNK)
    t = i % CHUNK
    cols = [np.eye(P), same]
    for l in range(LEVELS):
        cols.append(same & ((t[:, None] >> (l + 1)) == (t[None, :] >> (l + 1))) & (((t[:, None] >> l) & 1) == 1)
                    & (((t[None, :] >> l) & 1) == 0))
    cols.append(same & (t[None, :] > t[:, None]))
    cols.append(np.arange(CHUNK)[None, :] >= t[:, None])
    cols.append(np.broadcast_to(np.arange(T)[None, :] % CHUNK != 0, (P, T)))
    return np.concatenate([np.asarray(c, np.float32) for c in cols], axis=1)


def position_tables():
    import numpy as np
    half = 128
    inv = 1.0 / (np.float32(10000.0) ** (np.arange(0, 2 * half, 2, dtype=np.float32) / np.float32(2 * half)))
    ang = (np.arange(T, dtype=np.float32)[:, None] * inv.astype(np.float32)[None, :]).astype(np.float32)
    cossin = np.stack([np.cos(ang), np.sin(ang)], axis=1).astype(np.float32)
    lg = np.log1p(-np.exp2(-5.0 - np.arange(RET_HEADS, dtype=np.float64)))
    n, m = np.arange(T)[None, :], np.arange(T)[:, None]
    seen = (m // CHUNK) <= (n // CHUNK)
    decay = np.where(seen[None], np.exp(lg[:, None, None] * np.abs(n - m)[None]), 0.0) / 16.0
    return cossin, decay.astype(np.float32)


def kernel(**inputs):
    import numpy as np
    import concourse.bacc as bacc
    from concourse.bass_utils import run_bass_kernel_spmd

    a = {k: np.ascontiguousarray(v) for k, v in inputs.items()}

    def blocks(v, n):
        flat = np.zeros((n, P), np.float32)
        flat.reshape(-1)[:v.size] = v.reshape(-1)
        return flat.T

    table = dict(mu=a["rw_mu"], w0=a["rw_w0"], a0=a["rw_a0"], k_k=a["rw_k_k"], k_a=a["rw_k_a"], r_k=a["rw_r_k"],
                 lnx_w=a["rw_lnx_w"], lnx_b=a["rw_lnx_b"], ev_norm=a["ev_norm"], ff_norm0=a["ff_norm"][0],
                 od_norm=a["od_norm"], ff_norm1=a["ff_norm"][1], conv_w=a["od_conv_w"], conv_b=a["od_conv_b"],
                 gx_b=a["od_gx_b"], ga_b=a["od_ga_b"], lam=a["od_lam"])
    params = np.ascontiguousarray(np.concatenate([blocks(table[k], n) for k, (_, n) in COLS.items()], axis=1))
    cossin, rdecay = position_tables()
    arrays = {
        "x_in": a["x"][0], "params": params, "consts": const_table(), "cossin": cossin, "rdecay": rdecay,
        "ev_w_in": a["ev_w_in"][0], "ev_w_out": a["ev_w_out"][0], "rw_w2": a["rw_w2"][0], "rw_a2": a["rw_a2"][0],
        "rw_g2": a["rw_g2"][0], "od_w_in": a["od_w_in"][0], "gx_w": a["od_gx_w"][0], "ga_w": a["od_ga_w"][0],
        "od_w_out": a["od_w_out"][0], "ff_w1": a["ff_w1"], "ff_w2": a["ff_w2"], "final_norm": a["final_norm"],
    }
    nc = bacc.Bacc("TRN2", target_bir_lowering=False, num_devices=1)
    args = {k: nc.dram_tensor(f"in_{k}", v.shape, mybir.dt.from_np(v.dtype), kind="ExternalInput").ap()
            for k, v in arrays.items()}
    out = nc.dram_tensor("out", (T, D), F32, kind="ExternalOutput").ap()
    trunk(nc, **args, out=out)
    r = run_bass_kernel_spmd(nc, [{f"in_{k}": v for k, v in arrays.items()}], core_ids=[0])
    return r.results[0]["out"].reshape(1, T, D)
```
